# Optimizing a Trainium2 kernel written in Bass

```python
import jax, jax.numpy as jnp
from jax import lax
import numpy as np

D_MODEL = 1024
BATCH = 1
SEQ = 1024
DEPTH = 1

CHUNK = 64
HEAD_DIM = 64
CONV_GROUPS = 8
CONV_DIM = CONV_GROUPS * HEAD_DIM
RWKV_HEADS = 8
RWKV_DIM = RWKV_HEADS * HEAD_DIM
MIX_DIM = CONV_DIM + RWKV_DIM
CONV_K = 3
DECAY_RANK = 64
ICLR_RANK = 64
GATE_RANK = 160
D_FF = 2816
RWKV_COLS = 3 * RWKV_DIM + DECAY_RANK + ICLR_RANK + GATE_RANK
IN_COLS = 3 * CONV_DIM + RWKV_COLS
RMS_EPS = 1e-6
GN_EPS = HEAD_DIM * 1e-5


def _rms_norm(z, g):
    zf = z.astype(jnp.float32)
    zf = zf * lax.rsqrt(jnp.mean(zf * zf, axis=-1, keepdims=True) + RMS_EPS)
    return (zf * g.astype(jnp.float32)).astype(z.dtype)

def _causal_dwconv(z, w):
    c = z.shape[-1]
    return lax.conv_general_dilated(
        z, w[:, None, :].astype(z.dtype), window_strides=(1,),
        padding=[(CONV_K - 1, 0)], dimension_numbers=('NWC', 'WIO', 'NWC'),
        feature_group_count=c)

def _token_shift(z):
    return jnp.pad(z[:, :-1], ((0, 0), (1, 0), (0, 0)))

def _wkv7(r, decay, k, v, kk, a):
    b, t, h, n = r.shape
    n_chunks = t // CHUNK

    def to_chunks(z):
        return z.reshape(b, n_chunks, CHUNK, h, n).transpose(1, 2, 0, 3, 4)

    def step(S, inp):
        r_t, w_t, k_t, v_t, kk_t, a_t = inp
        sa = jnp.einsum('bhvk,bhk->bhv', S, -kk_t)
        S = (S * w_t[:, :, None, :] + sa[..., None] * (kk_t * a_t)[:, :, None, :]
             + v_t[..., None] * k_t[:, :, None, :])
        return S, jnp.einsum('bhvk,bhk->bhv', S, r_t)

    def chunk_step(S, inp):
        return lax.scan(step, S, inp)

    S0 = jnp.zeros((b, h, n, n), jnp.float32)
    xs = tuple(to_chunks(z) for z in (r, decay, k, v, kk, a))
    _, y = lax.scan(chunk_step, S0, xs)
    return y.transpose(2, 0, 1, 3, 4).reshape(b, t, h, n)

def _head_group_norm(y, wgt, bias):
    mu = jnp.mean(y, axis=-1, keepdims=True)
    var = jnp.mean(jnp.square(y - mu), axis=-1, keepdims=True)
    yn = (y - mu) * lax.rsqrt(var + GN_EPS)
    b, t, h, n = y.shape
    return yn.reshape(b, t, h * n) * wgt.astype(jnp.float32) + bias.astype(jnp.float32)

def _token_mixer(xn, w_in, conv_a_w, shift_mu, w0, w2, a0, a2, g2, k_k, k_a, r_k,
                 lnx_w, lnx_b, w_out):
    b, t, _ = xn.shape
    p = jnp.einsum('btd,de->bte', xn, w_in)
    gB, gC, hA = jnp.split(p[..., :3 * CONV_DIM], 3, axis=-1)
    y_a = gC * _causal_dwconv(gB * hA, conv_a_w)
    q = p[..., 3 * CONV_DIM:]
    q = q + (_token_shift(q) - q) * shift_mu
    splits = np.cumsum([RWKV_DIM, RWKV_DIM, RWKV_DIM, DECAY_RANK, ICLR_RANK]).tolist()
    r, k, v, wd, ad, gd = jnp.split(q, splits, axis=-1)
    wdf = wd.astype(jnp.float32)
    w_log = -jax.nn.softplus(-(w0.astype(jnp.float32)
                               + jnp.tanh(wdf) @ w2.astype(jnp.float32))) - 0.5
    decay = jnp.exp(-jnp.exp(w_log))
    a = jax.nn.sigmoid(a0 + ad @ a2)
    g = jax.nn.sigmoid(gd) @ g2
    heads = lambda z: z.astype(jnp.float32).reshape(b, t, RWKV_HEADS, HEAD_DIM)
    pheads = lambda z: z.astype(jnp.float32).reshape(RWKV_HEADS, HEAD_DIM)
    r4, k4, v4, a4, d4 = heads(r), heads(k), heads(v), heads(a), heads(decay)
    kk = k4 * pheads(k_k)
    kk = kk / jnp.maximum(jnp.linalg.norm(kk, axis=-1, keepdims=True), 1e-12)
    k4 = k4 * (1.0 + (a4 - 1.0) * pheads(k_a))
    y = _wkv7(r4, d4, k4, v4, kk, a4)
    y_b = _head_group_norm(y, lnx_w, lnx_b)
    bonus = jnp.sum(r4 * k4 * r_k.astype(jnp.float32), axis=-1, keepdims=True) * v4
    y_b = (y_b + bonus.reshape(b, t, RWKV_DIM)).astype(xn.dtype) * g
    return jnp.einsum('bte,ed->btd', jnp.concatenate([y_a, y_b], axis=-1), w_out)

def _channel_mixer(hn, w_up, ffn_conv_w, ffn_conv_b, w_down):
    f = jnp.einsum('btd,df->btf', hn, w_up)
    f = _causal_dwconv(f, ffn_conv_w) + ffn_conv_b
    gate, up = jnp.split(f, 2, axis=-1)
    return jnp.einsum('btf,fd->btd', jax.nn.gelu(gate) * up, w_down)

def first_inputs(seed: int = 0) -> dict:
    key = jax.random.key(seed)
    ks = iter(jax.random.split(key, 32))
    nrm = lambda shape, s: jax.random.normal(next(ks), shape, jnp.float32) * s
    L = DEPTH
    return {
        'x': jax.random.normal(next(ks), (BATCH, SEQ, D_MODEL), jnp.float32),
        'pre_mix_g': 1.0 + nrm((L, D_MODEL), 0.02),
        'w_in': nrm((L, D_MODEL, IN_COLS), D_MODEL ** -0.5),
        'conv_a_w': nrm((L, CONV_K, CONV_DIM), 0.5),
        'shift_mu': jax.random.uniform(next(ks), (L, RWKV_COLS), jnp.float32),
        'w0': jax.random.uniform(next(ks), (L, RWKV_DIM), jnp.float32, -6.0, 0.0),
        'w2': nrm((L, DECAY_RANK, RWKV_DIM), 0.1),
        'a0': nrm((L, RWKV_DIM), 0.1),
        'a2': nrm((L, ICLR_RANK, RWKV_DIM), ICLR_RANK ** -0.5),
        'g2': nrm((L, GATE_RANK, RWKV_DIM), GATE_RANK ** -0.5),
        'k_k': 0.85 + nrm((L, RWKV_DIM), 0.02),
        'k_a': 1.0 + nrm((L, RWKV_DIM), 0.02),
        'r_k': nrm((L, RWKV_HEADS, HEAD_DIM), 0.1),
        'lnx_w': 1.0 + nrm((L, RWKV_DIM), 0.02),
        'lnx_b': nrm((L, RWKV_DIM), 0.01),
        'w_out': nrm((L, MIX_DIM, D_MODEL), MIX_DIM ** -0.5),
        'post_mix_g': 1.0 + nrm((L, D_MODEL), 0.02),
        'pre_ffn_g': 1.0 + nrm((L, D_MODEL), 0.02),
        'w_up': nrm((L, D_MODEL, 2 * D_FF), D_MODEL ** -0.5),
        'ffn_conv_w': nrm((L, CONV_K, 2 * D_FF), 0.5),
        'ffn_conv_b': nrm((L, 2 * D_FF), 0.01),
        'w_down': nrm((L, D_FF, D_MODEL), D_FF ** -0.5),
        'post_ffn_g': 1.0 + nrm((L, D_MODEL), 0.02),
    }

def first_block(x, pre_mix_g, w_in, conv_a_w, shift_mu, w0, w2, a0, a2, g2, k_k, k_a, r_k,
              lnx_w, lnx_b, w_out, post_mix_g, pre_ffn_g, w_up, ffn_conv_w, ffn_conv_b,
              w_down, post_ffn_g):
    h = x
    for l in range(DEPTH):
        mix = _token_mixer(_rms_norm(h, pre_mix_g[l]), w_in[l], conv_a_w[l], shift_mu[l],
                           w0[l], w2[l], a0[l], a2[l], g2[l], k_k[l], k_a[l], r_k[l],
                           lnx_w[l], lnx_b[l], w_out[l])
        h = h + _rms_norm(mix, post_mix_g[l])
        ffn = _channel_mixer(_rms_norm(h, pre_ffn_g[l]), w_up[l], ffn_conv_w[l],
                             ffn_conv_b[l], w_down[l])
        h = h + _rms_norm(ffn, post_ffn_g[l])
    return h


PLE_DIM = 256
SWA_HEADS = 8
SWA_KV_HEADS = 2
SWA_GROUP = SWA_HEADS // SWA_KV_HEADS
WINDOW = 128
SWA_BLOCK = WINDOW
FOX_HEADS = 8
FOX_BLOCK = 128
D_FF_2 = 4 * D_MODEL
N_BRANCH = 2

SWA_Q = SWA_HEADS * HEAD_DIM
SWA_KV = SWA_KV_HEADS * HEAD_DIM
FOX_W = FOX_HEADS * HEAD_DIM
GATE_W = N_BRANCH * D_MODEL
SPLIT_POINTS = tuple(np.cumsum([SWA_Q, SWA_KV, SWA_KV, FOX_W, FOX_W, FOX_W, FOX_HEADS]).tolist())
D_IN = SPLIT_POINTS[-1] + GATE_W


def alibi_slopes(n_heads):
    return jnp.asarray(np.array([2.0 ** (-8.0 * (h + 1) / n_heads) for h in range(n_heads)], dtype=np.float32))

def rms_norm(x, g):
    x32 = x.astype(jnp.float32)
    y = x32 * lax.rsqrt(jnp.mean(jnp.square(x32), axis=-1, keepdims=True) + RMS_EPS)
    return (y * g.astype(jnp.float32)).astype(x.dtype)

def sliding_window_attention(q, k, v, sinks):
    B, S = q.shape[0], q.shape[1]
    nb = S // SWA_BLOCK
    SB = SWA_BLOCK
    qb = q.reshape(B, nb, SB, SWA_KV_HEADS, SWA_GROUP, HEAD_DIM)
    kb = k.reshape(B, nb, SB, SWA_KV_HEADS, HEAD_DIM)
    vb = v.reshape(B, nb, SB, SWA_KV_HEADS, HEAD_DIM)

    def band(t):
        prev = jnp.pad(t[:, :-1], ((0, 0), (1, 0), (0, 0), (0, 0), (0, 0)))
        return jnp.concatenate([prev, t], axis=2)

    k_band, v_band = band(kb), band(vb)
    s = jnp.einsum('bnqkgd,bnskd->bnkgqs', qb, k_band).astype(jnp.float32) * (HEAD_DIM ** -0.5)

    qi = jnp.arange(SB)[:, None] + SB
    si = jnp.arange(2 * SB)[None, :]
    chunk_diff = qi // CHUNK - si // CHUNK
    band_ok = (chunk_diff >= 0) & (chunk_diff <= WINDOW // CHUNK)
    real_key = (jnp.arange(nb)[:, None, None] > 0) | (si >= SB)[None]
    mask = band_ok[None] & real_key

    slopes = alibi_slopes(SWA_HEADS).reshape(SWA_KV_HEADS, SWA_GROUP)
    alibi = -slopes[:, :, None, None] * jnp.abs(qi - si).astype(jnp.float32)
    s = jnp.where(mask[None, :, None, None], s + alibi[None, None], -jnp.inf)

    sink = jnp.broadcast_to(sinks.astype(jnp.float32).reshape(SWA_KV_HEADS, SWA_GROUP)[None, None, :, :, None, None],
                            s.shape[:-1] + (1,))
    probs = jax.nn.softmax(jnp.concatenate([s, sink], axis=-1), axis=-1)[..., :-1]
    out = jnp.einsum('bnkgqs,bnskd->bnqkgd', probs.astype(v.dtype), v_band)
    return out.reshape(B, S, SWA_Q)

def forgetting_attention(q, k, v, f_logit):
    B, S = q.shape[0], q.shape[1]
    nb = S // FOX_BLOCK
    log_f = jax.nn.log_sigmoid(f_logit.astype(jnp.float32))
    c = jnp.cumsum(log_f, axis=1)
    c_k = c.transpose(0, 2, 1)
    kh = k.transpose(0, 2, 1, 3)
    vh = v.transpose(0, 2, 1, 3)
    q_blocks = q.reshape(B, nb, FOX_BLOCK, FOX_HEADS, HEAD_DIM).transpose(1, 0, 3, 2, 4)
    c_blocks = c.reshape(B, nb, FOX_BLOCK, FOX_HEADS).transpose(1, 0, 3, 2)
    k_pos = jnp.arange(S)
    scale = HEAD_DIM ** -0.5

    def one_block(args):
        qb, cq, n = args
        s = jnp.einsum('bhqd,bhsd->bhqs', qb, kh).astype(jnp.float32) * scale
        s = s + cq[..., None] - c_k[:, :, None, :]
        q_pos = n * FOX_BLOCK + jnp.arange(FOX_BLOCK)
        s = jnp.where((k_pos[None, :] <= q_pos[:, None])[None, None], s, -jnp.inf)
        probs = jax.nn.softmax(s, axis=-1)
        return jnp.einsum('bhqs,bhsd->bhqd', probs.astype(vh.dtype), vh)

    out = lax.map(one_block, (q_blocks, c_blocks, jnp.arange(nb, dtype=jnp.int32)))
    return out.transpose(1, 0, 3, 2, 4).reshape(B, S, FOX_W)

def second_inputs(seed: int = 0) -> dict:
    key = jax.random.key(seed)
    ks = jax.random.split(key, 18)

    def dense(k, fan_in, fan_out):
        return jax.random.normal(k, (DEPTH, fan_in, fan_out), jnp.float32) * fan_in ** -0.5

    def gain(k, shape):
        return 1.0 + 0.02 * jax.random.normal(k, shape, jnp.float32)

    return {
        "x": jax.random.normal(ks[0], (BATCH, SEQ, D_MODEL), jnp.float32),
        "p": jax.random.normal(ks[1], (DEPTH, BATCH, SEQ, PLE_DIM), jnp.float32),
        "g_mix": gain(ks[2], (DEPTH, D_MODEL)),
        "w_in": dense(ks[3], D_MODEL, D_IN),
        "b_forget": 3.0 + 0.5 * jax.random.normal(ks[4], (DEPTH, FOX_HEADS), jnp.float32),
        "swa_sinks": 0.5 * jax.random.normal(ks[5], (DEPTH, SWA_HEADS), jnp.float32),
        "w_br_swa": dense(ks[6], SWA_Q, D_MODEL),
        "w_br_fox": dense(ks[7], FOX_W, D_MODEL),
        "w_mix_out": dense(ks[8], D_MODEL, D_MODEL),
        "g_mlp": gain(ks[9], (DEPTH, D_MODEL)),
        "w_ff1": dense(ks[10], D_MODEL, D_FF_2),
        "w_ff2": dense(ks[11], D_FF_2, D_MODEL),
        "g_ple": gain(ks[12], (DEPTH, D_MODEL)),
        "w_ple_gate": dense(ks[13], D_MODEL, D_MODEL),
        "w_ple_proj": dense(ks[14], PLE_DIM, D_MODEL),
        "g_final": gain(ks[15], (D_MODEL,)),
    }

def second_block(x, p, g_mix, w_in, b_forget, swa_sinks, w_br_swa, w_br_fox, w_mix_out,
              g_mlp, w_ff1, w_ff2, g_ple, w_ple_gate, w_ple_proj, g_final):
    B, S = x.shape[0], x.shape[1]
    h = x
    for i in range(DEPTH):
        u = rms_norm(h, g_mix[i])
        z = u @ w_in[i]
        q_a, k_a, v_a, q_b, k_b, v_b, f_b, gate_logits = jnp.split(z, SPLIT_POINTS, axis=-1)
        y_a = sliding_window_attention(
            q_a.reshape(B, S, SWA_HEADS, HEAD_DIM),
            k_a.reshape(B, S, SWA_KV_HEADS, HEAD_DIM),
            v_a.reshape(B, S, SWA_KV_HEADS, HEAD_DIM),
            swa_sinks[i]) @ w_br_swa[i]
        y_b = forgetting_attention(
            q_b.reshape(B, S, FOX_HEADS, HEAD_DIM),
            k_b.reshape(B, S, FOX_HEADS, HEAD_DIM),
            v_b.reshape(B, S, FOX_HEADS, HEAD_DIM),
            f_b + b_forget[i]) @ w_br_fox[i]
        gates = jax.nn.sigmoid(gate_logits).reshape(B, S, N_BRANCH, D_MODEL)
        mixed = gates[:, :, 0] * y_a + gates[:, :, 1] * y_b
        h = h + mixed @ w_mix_out[i]
        u = rms_norm(h, g_mlp[i])
        h = h + jnp.square(jax.nn.relu(u @ w_ff1[i])) @ w_ff2[i]
        ple_gate = jax.nn.sigmoid(rms_norm(h, g_ple[i]) @ w_ple_gate[i])
        h = h + ple_gate * (p[i] @ w_ple_proj[i])
    return rms_norm(h, g_final)


def setup_inputs(seed=0):
    out = dict(first_inputs(seed))
    for name, value in second_inputs(seed + 1).items():
        if name != "x":
            out[name + "_2"] = value
    return out


def reference(
    x, pre_mix_g, w_in, conv_a_w, shift_mu, w0, w2, a0, a2, g2, k_k, k_a, r_k, lnx_w, lnx_b,
    w_out, post_mix_g, pre_ffn_g, w_up, ffn_conv_w, ffn_conv_b, w_down, post_ffn_g, p_2,
    g_mix_2, w_in_2, b_forget_2, swa_sinks_2, w_br_swa_2, w_br_fox_2, w_mix_out_2, g_mlp_2,
    w_ff1_2, w_ff2_2, g_ple_2, w_ple_gate_2, w_ple_proj_2, g_final_2,
):
    x = first_block(
        x, pre_mix_g, w_in, conv_a_w, shift_mu, w0, w2, a0, a2, g2, k_k, k_a, r_k, lnx_w, lnx_b,
        w_out, post_mix_g, pre_ffn_g, w_up, ffn_conv_w, ffn_conv_b, w_down, post_ffn_g,
    )
    return second_block(
        x, p_2, g_mix_2, w_in_2, b_forget_2, swa_sinks_2, w_br_swa_2, w_br_fox_2, w_mix_out_2,
        g_mlp_2, w_ff1_2, w_ff2_2, g_ple_2, w_ple_gate_2, w_ple_proj_2, g_final_2,
    )


_drawn_inputs = setup_inputs


def setup_inputs(seed=0):
    import zlib

    import numpy as np

    out = dict(_drawn_inputs(seed))
    spreads = {}
    factors = {'w2': 3.13,
     'a0': 3.302,
     'k_k': 5.714,
     'k_a': 5.447,
     'lnx_w': 5.952,
     'lnx_b': 8.0,
     'post_mix_g': 3.338,
     'pre_ffn_g': 3.315,
     'ffn_conv_b': 5.706,
     'post_ffn_g': 4.714,
     'g_mix_2': 8.0,
     'swa_sinks_2': 8.0,
     'g_mlp_2': 4.219,
     'g_ple_2': 8.0,
     'g_final_2': 2.878}
    for name, (base, spread) in spreads.items():
        noise = np.random.default_rng([zlib.crc32(name.encode()), seed]).standard_normal(out[name].shape)
        drawn = base * np.exp(spread * noise) if base else spread * noise
        out[name] = __import__('jax').numpy.asarray(drawn.astype(out[name].dtype))
    for name, factor in factors.items():
        out[name] = (out[name] * factor).astype(out[name].dtype)
    return out
```

```python
from contextlib import ExitStack

import concourse.bass as bass
import numpy as np
from concourse import mybir

F32 = mybir.dt.float32
F32R = mybir.dt.float32r
ALU = mybir.AluOpType
ACT = mybir.ActivationFunctionType
AX = mybir.AxisListType

P = 128
T = 1024
HT = T // 2
D = 1024
KT = D // P
HD = 64
CONV = 512
RWKV = 512
DECAY_R, ICLR_R, GATE_R = 64, 64, 160
FF1 = 2816
NF1 = FF1 // P
FF2 = 4096
NF2 = FF2 // P
CH = 64
NCH = T // CH
NP = RWKV // P
QT = T // P
RMS_EPS = 1e-6
GN_EPS = HD * 1e-5
DECAY_SCALE = -float(np.exp(-0.5))
NEG = -1e30
NH = 8

UNITS_IN1 = 27
UNITS_OUT1 = KT
UNITS_FFN1 = 3 * NF1
UNITS_IN2 = 19
UNITS_MIX = 3 * KT
UNITS_MIXOUT = KT
UNITS_FFN2 = 2 * NF2
UNITS_PLE = KT + 2
U_IN1 = 0
U_OUT1 = U_IN1 + UNITS_IN1
U_FFN1 = U_OUT1 + UNITS_OUT1
U_IN2 = U_FFN1 + UNITS_FFN1
U_MIX = U_IN2 + UNITS_IN2
U_MIXOUT = U_MIX + UNITS_MIX
U_FFN2 = U_MIXOUT + UNITS_MIXOUT
U_PLE = U_FFN2 + UNITS_FFN2
UNITS = U_PLE + UNITS_PLE
assert UNITS % 2 == 0

PAR = {}
_at = 0
for _name, _n in [("pre_mix_g", 8), ("mu", 15), ("conv_a", 12), ("w0", 4), ("a0", 4), ("k_k", 4), ("k_a", 4),
                  ("r_k", 4), ("lnx_w", 4), ("lnx_b", 4), ("post_mix_g", 8), ("pre_ffn_g", 8),
                  ("ffn_conv_w", 3 * 2 * NF1), ("ffn_conv_b", 2 * NF1), ("post_ffn_g", 8), ("g_mix", 8),
                  ("g_mlp", 8), ("g_ple", 8), ("g_final", 8), ("b_forget", 1), ("sinks", 8), ("rms_eps", 1),
                  ("gn_eps", 1)]:
    PAR[_name] = _at
    _at += _n
N_PAR = _at
CONSTS = ["ident", "ones", "head_sum", "head_mean", "up16", "low16", "low_off", "up", "up_diag", "causal"]
N_CONST = len(CONSTS) * P


class Steps:

    def __init__(self, sem, names, streams=1, offset=0):
        self.sem, self.names, self.streams, self.offset = sem, names, streams, offset
        self.emitted = 0

    def begin(self):
        return self.sem, 1

    def inc(self, name, stream=0):
        k = self.emitted % (len(self.names) * self.streams)
        assert (self.names[k // self.streams], k % self.streams) == (name, stream), (name, stream, self.names[k // self.streams])
        self.emitted += 1
        return self.sem, 1

    def at(self, rnd, name, stream=0):
        per = len(self.names) * self.streams
        return self.sem, self.offset + rnd * per + self.names.index(name) * self.streams + stream + 1


def build_program(nc, x_in, p_in, weights, params, consts, dists, w2_in, a2_in, g2_in, out):
    ctx = ExitStack()
    with ctx:
        base = 16512

        def at(name, shape, kib, dt=F32):
            n = int(np.prod(shape[1:])) * 4
            off = base + int(round(kib * 1024))
            assert off % 32 == 0 and off + n <= 229368, (name, off, n)
            return nc.alloc_sbuf_tensor_at(name, shape, dt, offset=off)

        def sem(name):
            return ctx.enter_context(nc.semaphore(name))

        w_raw = [at(f"w_raw{s}", [P, 8, P], 4 * s) for s in range(2)]
        w_hi = [at(f"w_hi{s}", [P, 8, P], 8 + 4 * s, F32R) for s in range(2)]
        w_lo = [at(f"w_lo{s}", [P, 8, P], 16 + 4 * s, F32R) for s in range(2)]
        par = at("par", [P, N_PAR], 24)
        cst = at("cst", [P, N_CONST], 25.5)
        small = at("small", [P, 64], 30.5)
        dist = at("dist", [P, 2, 2 * P], 30.75)
        rs = at("rs", [P, T], 32.75)
        sums = at("sums", [P, T], 36.75)
        sq = at("sq", [P, T], 40.75)
        B0 = 44.75
        A1, A2, A3, A4 = B0, B0 + 32, B0 + 64, B0 + 96
        END = B0 + 128

        def ptile(n):
            return cst[:, CONSTS.index(n) * P:(CONSTS.index(n) + 1) * P]

        ident = ptile("ident")

        def pcol(name, k=0):
            return par[:, bass.ds(PAR[name] + k, 1)]

        def tiles8(name, kib, dt=F32, n=8):
            return at(name, [P, n, T], kib, dt)

        u1_hi, u1_lo = tiles8("u1_hi", A1, F32R), tiles8("u1_lo", A2, F32R)
        x0 = tiles8("x0", A3)
        rkv = tiles8("rkv", A3, n=12)
        ta = at("ta", [P, T], A4 + 16)
        sg = at("sg", [P, 2, T], A4 + 20)
        ya = at("ya", [P, NP, T], A4 + 28)
        w2 = at("w2", [P, RWKV], A4 + 44)
        a2 = at("a2", [P, RWKV], A4 + 46)
        g2 = at("g2", [P, 2, RWKV], A4 + 48)
        t1 = at("t1", [P, T + 2], A4 + 52)
        t2 = at("t2", [P, T], A4 + 56.25)
        t3 = at("t3", [P, T], A4 + 60.25)
        kap = at("kap", [P, NP, T], A1)
        bet = at("bet", [P, NP, T], A1 + 16)
        bon = at("bon", [P, NP, T], A2)
        q1, q2, q3, q4 = (at(f"q{j + 1}", [P, T], A2 + 16 + 4 * j) for j in range(4))
        r_, k_, v_ = (rkv[:, 4 * j:4 * j + 4, :] for j in range(3))
        g_end = at("g_end", [P, NP, NCH], 30.5)

        slots = [36.75, 38.75, 40.75, 42.75] + [A2 + 16 + 2 * j for j in range(8)] + [A4 + 52 + 2 * j for j in range(7)]
        slots += [A4 + 16, A4 + 18, A4 + 44, A4 + 46]
        slots.reverse()

        def mat(name):
            return at(name, [P, NP, P], slots.pop())

        kap_d, bet_d, eta_d, rho_d, v_d = (mat(n) for n in ("kap_d", "bet_d", "eta_d", "rho_d", "v_d"))
        wd, nd, n_off, h_t, p_t, q_t = (mat(n) for n in ("wd", "nd", "n_off", "h_t", "p_t", "q_t"))
        bet_t, eta_t, v_t = (mat(n) for n in ("bet_t", "eta_t", "v_t"))
        w2m, n2m, w4m, n4m, n8m = (mat(n) for n in ("w2m", "n2m", "w4m", "n4m", "n8m"))
        pa, g_m, s_m, u_m = (mat(n) for n in ("pa", "g_m", "s_m", "u_m"))
        z0, y_m, z1, z2 = w2m, n2m, w4m, n4m

        m1_hi = tiles8("m1_hi", A3, F32R)
        m1_lo = [at(f"m1_lo{k}", [P, T], (A1 + 16 + 4 * k) if k < 4 else (A4 + 4 * (k - 4)), F32R) for k in range(8)]
        o1 = tiles8("o1", A2)
        h = tiles8("h", END)
        u2_hi, u2_lo = tiles8("u2_hi", A3, F32R), tiles8("u2_lo", A1, F32R)
        f_hi = at("f_hi", [P, 2, T], A4, F32R)
        f_lo = at("f_lo", [P, 2, T], A4 + 8, F32R)
        fpg = at("fpg", [P, T + 2], A4 + 16)
        fpu = at("fpu", [P, T + 2], A4 + 20.03125)
        cg = at("cg", [P, T], A4 + 24.0625)
        cu = sq
        u3_hi, u3_lo = tiles8("u3_hi", A3, F32R), tiles8("u3_lo", A1, F32R)
        qa = at("qa", [P, 4, T], A2)
        qb = at("qb", [P, 4, T], A2 + 16)
        v_cm = at("v_cm", [P, 5, T], A2)
        k65 = at("k65", [65, NH, T], A4)
        vb = at("vb", [P, QT, CONV], A4 + 32)
        ka = at("ka", [P, T + P], A4 + 48)
        va = at("va", [P, QT + 1, P], A4 + 52.5)
        W0 = A4 + 57
        negc = at("negc", [8, T], W0)
        fr = [at(f"fr{j}", [8, T], 36.75 + 4 * j) for j in range(2)]
        sc = [at(f"sc{g}", [P, 4, 2 * P], 36.75 + 4 * g) for g in range(2)]
        pt_a = at("pt_a", [P, 8, P], W0)
        qs = [at(f"qs{g}", [P, 4, P], W0 + 4 + 2 * g) for g in range(2)]
        ysw = [at(f"ysw{g}", [P, 4, HD], W0 + 8 + g) for g in range(2)]
        pr = [at(f"pr{s}", [P, T], 36.75 + 4 * s) for s in range(2)]
        pt = [at(f"pt{s}", [P, QT, P], W0 + 4 * s) for s in range(2)]
        yf = at("yf", [P, P], W0 + 8)
        qf = [at(f"qf{s}", [65, P], W0 + 8.5 + s / 2) for s in range(2)]
        mx, nm, ls, ri, es = (at(n, [P, 8], 30.5 + 0.03125 * j) for j, n in enumerate(["mx", "nm", "ls", "ri", "es"]))
        nsink = at("nsink", [P, 8], 30.5 + 0.03125 * 5)
        y_hi, y_lo = tiles8("y_hi", A4, F32R), tiles8("y_lo", END, F32R)
        mixed = tiles8("mixed", A2)
        ga = at("ga", [P, T], 36.75)
        gb = at("gb", [P, T], 40.75)
        m2_hi, m2_lo = tiles8("m2_hi", A3, F32R), tiles8("m2_lo", A1, F32R)
        u4_hi, u4_lo = tiles8("u4_hi", A2, F32R), tiles8("u4_lo", A4, F32R)
        e_hi = [at(f"e_hi{s}", [P, 2, T], (A1, A3)[s], F32R) for s in range(2)]
        e_lo = [at(f"e_lo{s}", [P, 2, T], (A1, A3)[s] + 8, F32R) for s in range(2)]
        fa = [at(f"fa{j}", [P, T], A1 + 16 + 4 * j) for j in range(2)]
        fs = [at(f"fs{j}", [P, T], A1 + 24 + 4 * j) for j in range(2)]
        u5_hi, u5_lo = tiles8("u5_hi", A2, F32R), tiles8("u5_lo", A4, F32R)
        pe_raw = at("pe_raw", [P, 2, T], A3 + 16)
        pe_hi = at("pe_hi", [P, 2, T], A3 + 24, F32R)
        pe_lo = at("pe_lo", [P, 2, T], A3 + 16, F32R)
        proj = tiles8("proj", A1)
        gt = [at(f"gt{j}", [P, T], A3 + 24 + 4 * j) for j in range(2)]

        h_spill = nc.dram_tensor("h_spill", (KT, P, T), F32, kind="Internal").ap()

        ps = [ctx.enter_context(nc.psum_tensor(f"ps{i}", [P, T], F32)) for i in range(4)]

        cst_in = sem("cst_in")
        x_ld = [sem(f"x_ld{m}") for m in range(KT)]
        w_landed = [sem(f"w_landed{s}") for s in range(2)]
        w_ready = sem("w_ready")
        w_used = sem("w_used")
        ss_done, var_done, rs_done = sem("ss_done"), sem("var_done"), sem("rs_done")
        sq_done, sq_added = sem("sq_done"), sem("sq_added")
        setup_done = sem("setup_done")

        def steps(name, names, streams=1, offset=0):
            return Steps(sem(name), names, streams, offset)

        a_x = steps("act_x", ["hi"])
        d_x = steps("dve_x", ["lo"])
        in1_freed = sem("in1_freed")
        d_sh = steps("dve_shift", ["diff", "mix"], offset=1)
        d_cv = steps("dve_conv", ["prod", "tap2", "tap1", "tap0", "out"], offset=1)
        a_mis = steps("act_misc", ["tanh", "sig0", "sig1"])
        d_pre = steps("dve_prep", ["kkr", "clamp", "kk", "lw", "scan", "cprev", "kap", "bet", "ika", "k4", "rk",
                                   "bon", "rho", "gend", "betg", "eta"])
        a_pre = steps("act_prep", ["ksq", "kln", "kinv", "sigz", "siga", "eprev", "eg", "einv"])
        p_pre = steps("pe_prep", ["za", "kss", "bon"])
        R_ST = 2
        l_st = steps("pool_stage", [f"{m}{hh}" for m in ("bet", "eta", "v", "kap", "rho") for hh in range(2)])
        p_r = steps("pe_rwkv", ["w", "n", "h", "pq", "tr", "sq2", "sq4", "sq8", "p4", "g", "c1", "c2", "c3", "c4", "c5",
                                "c6", "y"], R_ST)
        d_r = steps("dve_rwkv", ["wd", "p1", "nd", "noff", "h", "p", "q", "p2", "p3", "p4", "z0", "y", "z1", "z2", "u",
                                 "sadd", "s"], R_ST, offset=1)
        a_r = steps("act_rwkv", ["bt", "et", "vt", "w2", "n2", "w4", "n4", "n8", "g", "y0", "y1"], R_ST, offset=1)
        p_gn = steps("pe_gn", ["mean", "var", "gate"])
        d_gn = steps("dve_gn", ["cen", "nrm", "aff", "bon", "gate", "lo"])
        a_gn = steps("act_gn", ["sq", "ln", "rstd", "hi"])
        d_ya = steps("dve_ya", ["lo"])
        a_ya = steps("act_ya", ["hi"])
        a_o1 = steps("act_o1", ["ev"])
        d_h1 = steps("dve_h1", ["scale", "res"])
        d_h1l = steps("dve_h1l", ["lo"])
        a_h1 = steps("act_h1", ["hi"])
        d_f = steps("dve_f", ["evg", "cg1", "cg2", "cg3", "evu"] + [f"add{m}" for m in range(KT)]
                    + ["cu1", "cu2", "cu3", "prod", "lo"])
        a_f = steps("act_f", ["gelu", "hi"])
        dn1 = sem("ffn1_tile_done")
        d_f_last = steps("dve_f_last", ["add"])
        d_h2 = steps("dve_h2", ["scale", "res"])
        d_h2l = steps("dve_h2l", ["lo"])
        a_h2 = steps("act_h2", ["hi"])
        spilled = sem("spilled")
        in2_freed = sem("in2_freed")
        d_fg = steps("dve_forget", ["bias", "abs", "min", "log", "scan", "neg"])
        a_fg = steps("act_forget", ["exp", "ln"])
        negc_in = sem("negc_in")
        p_v = steps("pe_v", ["t"])
        a_v = steps("act_v", ["t"])
        d_si = steps("dve_swa_init", ["z"])
        SW = 2
        d_s = steps("dve_swa", ["qe", "qo", "b0", "b1", "b2", "b3", "max", "neg", "sd", "sum", "inv", "y"], SW)
        a_s = steps("act_swa", ["es", "e0", "e1", "e2", "e3", "pt", "yt"], SW)
        p_s = steps("pe_swa", ["s", "t", "pv", "yt"], SW)
        d_fs = steps("dve_fox_scores", ["q", "mask", "max", "neg"], 2)
        a_fs = steps("act_fox_scores", ["exp"], 2)
        p_fs = steps("pe_fox_scores", ["s"], 2)
        d_fo = steps("dve_fox_out", ["inv", "y"], 2, offset=1)
        a_fo = steps("act_fox_out", ["pt"], 2)
        p_fo = steps("pe_fox_out", ["t", "pv"], 2)
        a_fy = steps("act_fox_y", ["y"])
        p_fy = steps("pe_fox_y", ["y"])
        d_y = steps("dve_ysplit", ["lo"])
        a_y = steps("act_ysplit", ["hi"])
        d_mx = steps("dve_mix", ["ga", "gb", "a", "b", "mix"])
        a_mx = steps("act_mix", ["siga", "sigb"])
        d_m2 = steps("dve_m2", ["lo"])
        a_m2 = steps("act_m2", ["hi"])
        d_h3 = steps("dve_h3", ["res"])
        d_h3l = steps("dve_h3l", ["lo"])
        a_h3 = steps("act_h3", ["hi"])
        d_e = steps("dve_e", ["ev0", "lo0", "ev1", "lo1"])
        a_e = steps("act_e", ["sq0", "hi0", "sq1", "hi1"])
        dn2 = sem("ffn2_tile_done")
        d_ea = steps("dve_e_add", ["add"])
        d_h4 = steps("dve_h4", ["lo"])
        a_h4 = steps("act_h4", ["hi"])
        p_ld = sem("p_ld")
        d_p = steps("dve_p", ["lo"])
        a_p = steps("act_p", ["hi"])
        dn3 = sem("proj_tile_done")
        a_pj = steps("act_proj", ["ev"])
        d_g = steps("dve_g", ["ev", "prod", "res"])
        a_g = steps("act_g", ["sig"])
        d_o = steps("dve_o", ["out"])
        stored = sem("stored")
        l_hi = steps("pool_hi", ["hi"])

        HALVES = [slice(0, HT), slice(HT, T)]

        block = ctx.enter_context(nc.Block())

        @block.sync
        def _(sp):
            sp.dma_start(par[:], params).then_inc(cst_in, 16)
            for m in range(KT):
                sp.dma_start(x0[:, m, :], x_in[m]).then_inc(x_ld[m], 16)
            for dst, src in ((cst[:], consts), (dist[:], dists), (w2[:], w2_in), (a2[:], a2_in), (g2[:], g2_in)):
                sp.dma_start(dst, src).then_inc(cst_in, 16)

            def load(n, s):
                sp.dma_start(w_raw[s][:].rearrange("p k m -> p (k m)"), weights[n]).then_inc(w_landed[s], 16)

            for s in range(2):
                load(s, s)
            with sp.Fori(1, UNITS // 2) as i:
                for s in range(2):
                    sp.wait_ge(w_ready, 2 * i + s - 1)
                    load(2 * i + s, s)

        @block.gpsimd
        def _(pool):
            def copy(dst, src, rows=slice(0, P)):
                n, k, c = src.shape
                ones = ptile("ones")[rows, 0:c].unsqueeze(1).broadcast_to([n, k, c])
                return nc.gpsimd.tensor_tensor(dst, src, ones, ALU.mult)

            def split(n, s, it, first=False):
                pool.wait_ge(w_landed[s], 16 * it + 16)
                if not first:
                    pool.wait_ge(w_used, n - 1)
                copy(w_hi[s][:], w_raw[s][:]).then_inc(*l_hi.inc("hi"))
                pool.wait_ge(l_hi.sem, n + 1)
                nc.gpsimd.tensor_tensor(w_lo[s][:], w_raw[s][:], w_hi[s][:].bitcast(F32), ALU.subtract).then_inc(w_ready, 1)

            pool.wait_ge(cst_in, 16 * 6)
            for s in range(2):
                split(s, s, 0, first=True)
            with pool.Fori(1, (U_OUT1 + 1) // 2) as i:
                for s in range(2):
                    split(2 * i + s, s, i)

            mats = (("bet", bet_d, bet, "tr"), ("eta", eta_d, k_, "tr"), ("v", v_d, v_, "tr"), ("kap", kap_d, kap, "c1"),
                    ("rho", rho_d, r_, "y"))

            def stage_chunk(c, first=False):
                for name, dst, src, freed_by in mats:
                    if not first:
                        pool.wait_ge(*p_r.at(c - 1, freed_by, 1))
                    for hh in range(2):
                        rows = slice(64 * hh, 64 * hh + 64)
                        copy(dst[rows, :, 64 * hh:64 * hh + 64], src[rows, :, bass.ds(c * CH, CH)], rows)\
                            .then_inc(*l_st.inc(f"{name}{hh}"))
                        pool.wait_ge(*l_st.at(c, f"{name}{hh}"))

            pool.wait_ge(w_ready, 2 * ((U_OUT1 + 1) // 2))
            pool.wait_ge(*d_pre.at(NP - 1, "eta"))
            pool.wait_ge(d_r.sem, 1)
            stage_chunk(0, first=True)
            with pool.Fori(1, NCH) as c:
                stage_chunk(c)

            with pool.Fori((U_OUT1 + 1) // 2, UNITS // 2) as i:
                for s in range(2):
                    split(2 * i + s, s, i)

        @block.tensor
        def _(pe):
            mm = nc.tensor.matmul

            def unit(n, s, parts):
                pe.wait_ge(w_ready, n + 1)
                for k, (acc, xh, xl, start, stop, waits) in enumerate(parts):
                    for w in waits:
                        pe.wait_ge(*w)
                    for j, (w, x) in enumerate(((w_hi, xh), (w_hi, xl), (w_lo, xh))):
                        for c in HALVES:
                            ins = mm(acc[:, c], w[s][:, k, :], x[:, c], start=start and j == 0, stop=stop and j == 2)
                    yield k, ins

            def tile(n, s, acc, xh, xl, ready=None):
                parts = [(acc, xh(k), xl(k), k == 0, k == KT - 1, [ready(k)] if ready else []) for k in range(KT)]
                for _, ins in unit(n, s, parts):
                    pass
                ins.then_inc(w_used, 1)

            def of(t):
                return lambda k: t[:, k, :]

            def sum_squares(q):
                pe.wait_ge(sq_added, KT * (q + 1))
                for c in HALVES:
                    ins = mm(ps[3][:, c], ptile("ones"), sums[:, c], start=True, stop=True)
                ins.then_inc(ss_done, 1)

            def fp32(acc, lhsT, rhs, start=True, stop=True):
                for c in HALVES:
                    ins = mm(acc[:, c], lhsT, rhs[:, c], start=start, stop=stop)
                return ins

            pe.wait_ge(cst_in, 16 * 6)
            tile(0, 0, ps[0], of(u1_hi), of(u1_lo), lambda k: d_x.at(k, "lo"))
            sum_squares(0)
            with pe.Fori(0, UNITS_IN1 // 2) as i:
                for s in range(2):
                    n = 2 * i + s + 1
                    pe.wait_ge(in1_freed, 2 * i + s + 1)
                    tile(n, (s + 1) % 2, ps[(s + 1) % 2], of(u1_hi), of(u1_lo))

            pe.wait_ge(in1_freed, UNITS_IN1 + 1)
            pe.wait_ge(*a_mis.at(0, "sig1"))
            for i in range(NP):
                c = slice(i * P, (i + 1) * P)
                if i:
                    pe.wait_ge(*a_pre.at(i - 1, "siga"))
                fp32(ps[0], w2[:, c], ta)
                fp32(ps[1], a2[:, c], ta).then_inc(*p_pre.inc("za"))
                pe.wait_ge(*a_pre.at(i, "ksq"))
                fp32(ps[2], ptile("head_sum"), t3).then_inc(*p_pre.inc("kss"))
                pe.wait_ge(*d_pre.at(i, "rk"))
                fp32(ps[3], ptile("head_sum"), q4).then_inc(*p_pre.inc("bon"))

            def bank(s, b, half=0):
                o = 512 * (b % 2) + 256 * half
                return ps[2 * s + b // 2][:, o:o + 256].rearrange("p (j c) -> p j c", j=2)

            def products(s, dst, *terms):
                for j in range(2):
                    for t, (a, b) in enumerate(terms):
                        ins = mm(dst[:, j, :], a[:, 2 * s + j, :], b[:, 2 * s + j, :], start=t == 0, stop=t == len(terms) - 1)
                return ins

            def turned(s, dst, src):
                for j in range(2):
                    ins = nc.tensor.transpose(dst[:, j, :], src[:, 2 * s + j, :], ident)
                return ins

            pe.wait_ge(*d_pre.at(NP - 1, "eta"))
            pe.wait_ge(d_r.sem, 1)
            pe.wait_ge(a_r.sem, 1)
            with pe.Fori(0, NCH) as c:
                pe.wait_ge(*l_st.at(c, "kap1"))
                for s in range(2):
                    products(s, bank(s, 0), (bet_d, kap_d)).then_inc(*p_r.inc("w", s))
                pe.wait_ge(*d_r.at(c - 1, "s", 1))
                for s in range(2):
                    products(s, bank(s, 1), (kap_d, bet_d)).then_inc(*p_r.inc("n", s))
                pe.wait_ge(*a_r.at(c - 1, "y1", 1))
                for s in range(2):
                    products(s, bank(s, 2), (eta_d, kap_d)).then_inc(*p_r.inc("h", s))
                pe.wait_ge(*l_st.at(c, "rho1"))
                for s in range(2):
                    products(s, bank(s, 3), (bet_d, rho_d))
                    products(s, bank(s, 3, 1), (eta_d, rho_d)).then_inc(*p_r.inc("pq", s))
                for s in range(2):
                    pe.wait_ge(*d_r.at(c, "wd", s))
                    turned(s, bank(s, 0), bet_d)
                    turned(s, bank(s, 0, 1), eta_d)
                    pe.wait_ge(*d_r.at(c, "noff", s))
                    turned(s, bank(s, 1), v_d).then_inc(*p_r.inc("tr", s))
                for s in range(2):
                    pe.wait_ge(*d_r.at(c, "h", s))
                    products(s, bank(s, 2), (nd, wd))
                    products(s, bank(s, 2, 1), (wd, nd)).then_inc(*p_r.inc("sq2", s))
                for s in range(2):
                    pe.wait_ge(*a_r.at(c, "n2", s))
                    pe.wait_ge(*d_r.at(c, "q", s))
                    products(s, bank(s, 3), (n2m, pa))
                    products(s, bank(s, 0), (n2m, w2m))
                    products(s, bank(s, 0, 1), (w2m, n2m)).then_inc(*p_r.inc("sq4", s))
                for s in range(2):
                    pe.wait_ge(*a_r.at(c, "n4", s))
                    pe.wait_ge(*d_r.at(c, "p2", s))
                    products(s, bank(s, 1, 1), (n4m, pa))
                    products(s, bank(s, 2), (w4m, n4m)).then_inc(*p_r.inc("sq8", s))
                for s in range(2):
                    pe.wait_ge(*a_r.at(c, "n8", s))
                    pe.wait_ge(*d_r.at(c, "p3", s))
                    products(s, bank(s, 3, 1), (n8m, pa)).then_inc(*p_r.inc("p4", s))
                for s in range(2):
                    pe.wait_ge(*d_r.at(c, "p4", s))
                    products(s, bank(s, 2, 1), (n_off, pa)).then_inc(*p_r.inc("g", s))
                for s in range(2):
                    products(s, bank(s, 0), (kap_d, s_m), (h_t, v_t)).then_inc(*p_r.inc("c1", s))
                for s in range(2):
                    pe.wait_ge(*d_r.at(c, "z0", s))
                    products(s, bank(s, 1), (pa, z0)).then_inc(*p_r.inc("c2", s))
                for s in range(2):
                    pe.wait_ge(*a_r.at(c, "g", s))
                    pe.wait_ge(*d_r.at(c, "y", s))
                    products(s, bank(s, 2), (g_m, y_m)).then_inc(*p_r.inc("c3", s))
                for s in range(2):
                    pe.wait_ge(*d_r.at(c, "z1", s))
                    products(s, bank(s, 3), (g_m, z1)).then_inc(*p_r.inc("c4", s))
                for s in range(2):
                    pe.wait_ge(*d_r.at(c, "z2", s))
                    products(s, bank(s, 0, 1), (g_m, z2)).then_inc(*p_r.inc("c5", s))
                for s in range(2):
                    pe.wait_ge(*d_r.at(c, "u", s))
                    products(s, bank(s, 1, 1), (bet_t, u_m), (eta_t, v_t)).then_inc(*p_r.inc("c6", s))
                for s in range(2):
                    products(s, bank(s, 2, 1), (s_m, rho_d), (u_m, p_t), (v_t, q_t)).then_inc(*p_r.inc("y", s))

            pe.wait_ge(*a_r.at(NCH - 1, "y1", 1))
            pe.wait_ge(*d_r.at(NCH - 1, "s", 1))
            for i in range(NP):
                c = slice(i * P, (i + 1) * P)
                if i:
                    pe.wait_ge(*d_gn.at(i - 1, "gate"))
                fp32(ps[0], ptile("head_mean"), kap[:, i, :]).then_inc(*p_gn.inc("mean"))
                pe.wait_ge(*a_gn.at(i, "sq"))
                fp32(ps[1], ptile("head_mean"), q2).then_inc(*p_gn.inc("var"))
                fp32(ps[2], g2[:, 0, c], sg[:, 0, :], stop=False)
                fp32(ps[2], g2[:, 1, c], sg[:, 1, :], start=False).then_inc(*p_gn.inc("gate"))

            def out1(i, first=False):
                for s in range(2):
                    if not first:
                        pe.wait_ge(*a_o1.at(2 * i + s - 2, "ev"))
                    tile(U_OUT1 + 2 * i + s, (U_OUT1 + s) % 2, ps[s], of(m1_hi), lambda k: m1_lo[k][:],
                         lambda k: d_ya.at(k, "lo") if k < NP else d_gn.at(k - NP, "lo"))

            pe.wait_ge(*a_gn.at(NP - 1, "ln"))
            out1(0, first=True)
            with pe.Fori(1, KT // 2) as i:
                out1(i)
            sum_squares(1)

            def up1(p, n, s, first=False):
                for j, ev in enumerate(("evg", "evu")):
                    if not first:
                        pe.wait_ge(*d_f.at(p - 1, ev))
                    tile(n + j, (s + j) % 2, ps[j], of(u2_hi), of(u2_lo), (lambda k: d_h1l.at(k, "lo")) if first else None)
                    if first and j == 0:
                        sum_squares(2)

            def down1(p, n, s, b):
                parts = [(ps[2 + m % 2], f_hi[:, b, :], f_lo[:, b, :], True, True,
                          [d_f.at(p, "lo")] * (m == 0) + [d_f.at(p, f"add{m + 6}") if m < 2 else d_f.at(p + 1, f"add{m - 2}")])
                         for m in range(KT)]
                for m, ins in unit(n, s, parts):
                    if m < KT - 1:
                        ins.then_inc(dn1, 1)
                ins.then_inc(w_used, 1)

            up1(0, U_FFN1, U_FFN1 % 2, first=True)
            n0 = U_FFN1 + 2
            with pe.Fori(0, (NF1 - 2) // 2) as i:
                for t in range(2):
                    p = 2 * i + t + 1
                    up1(p, n0 + 6 * i + 3 * t, (n0 + 3 * t) % 2)
                    down1(p - 1, n0 + 6 * i + 3 * t + 2, (n0 + 3 * t) % 2, t)
            n1 = n0 + 3 * (NF1 - 2)
            up1(NF1 - 1, n1, n1 % 2)
            down1(NF1 - 2, n1 + 2, n1 % 2, (NF1 - 2) % 2)
            parts = [(ps[2 + m % 2], f_hi[:, 1, :], f_lo[:, 1, :], True, True,
                      [d_f.at(NF1 - 1, "lo")] * (m == 0)
                      + [d_f.at(NF1 - 1, f"add{m + 6}") if m < 2 else (d_f_last.sem, m - 1)]) for m in range(KT)]
            for m, ins in unit(n1 + 3, (n1 + 3) % 2, parts):
                if m < KT - 1:
                    ins.then_inc(dn1, 1)
            ins.then_inc(w_used, 1)
            pe.wait_ge(*d_f_last.at(KT - 1, "add"))
            sum_squares(3)

            def in2(j, n, s, first=False):
                tile(n, s, ps[(n - U_IN2) % 2] if isinstance(n, int) else ps[(s + U_IN2) % 2], of(u3_hi), of(u3_lo),
                     (lambda k: d_h2l.at(k, "lo")) if first else None)

            in2(0, U_IN2, U_IN2 % 2, first=True)
            sum_squares(4)
            for j in range(1, 6):
                if j > 1:
                    pe.wait_ge(in2_freed, j - 1)
                in2(j, U_IN2 + j, (U_IN2 + j) % 2)
            pe.wait_ge(var_done, 5)
            for vt in range(5):
                pe.wait_ge(in2_freed, vt + 2)
                if vt > 1:
                    pe.wait_ge(*a_v.at(vt - 2, "t"))
                for k in range(QT):
                    ins = nc.tensor.transpose(ps[2 + vt % 2][:, k * P:(k + 1) * P], v_cm[:, vt, k * P:(k + 1) * P], ident)
                ins.then_inc(*p_v.inc("t"))
            pe.wait_ge(in2_freed, 5)
            in2(6, U_IN2 + 6, (U_IN2 + 6) % 2)
            with pe.Fori(0, 6) as i:
                for s in range(2):
                    pe.wait_ge(in2_freed, 2 * i + s + 6)
                    in2(7 + s, 2 * i + (U_IN2 + 7 + s), (U_IN2 + 7 + s) % 2)

            pe.wait_ge(in2_freed, UNITS_IN2)
            pe.wait_ge(*a_v.at(4, "t"))

            def swa(n, first=False):
                for g in range(SW):
                    pe.wait_ge(*d_s.at(n, "qo", g))
                    if not first:
                        pe.wait_ge(*a_s.at(n - 1, "yt", g))
                    for j in range(4):
                        ins = mm(ps[g][:, j * 256:(j + 1) * 256], qs[g][:, j, :], ka[:, bass.ds(n * P, 2 * P)],
                                 start=True, stop=True)
                    ins.then_inc(*p_s.inc("s", g))
                for g in range(SW):
                    pe.wait_ge(*a_s.at(n, "e3", g))
                    for j in range(4):
                        for k in range(2):
                            o = (2 * j + k) * P
                            ins = nc.tensor.transpose(ps[2 + g][:, o:o + P], sc[g][:, j, k * P:(k + 1) * P], ident)
                    ins.then_inc(*p_s.inc("t", g))
                for g in range(SW):
                    pe.wait_ge(*a_s.at(n, "pt", g))
                    for j in range(4):
                        for k in range(2):
                            ins = mm(ps[g][:, j * P:(j + 1) * P], pt_a[:, 2 * j + k, :],
                                     va[:, bass.ds(n + k, 1), :].rearrange("p a c -> p (a c)"), start=k == 0, stop=k == 1)
                    ins.then_inc(*p_s.inc("pv", g))
                for g in range(SW):
                    pe.wait_ge(*d_s.at(n, "y", g))
                    for j in range(2):
                        ins = nc.tensor.transpose(ps[g][:, 512 + j * P:512 + (j + 1) * P],
                                                  ysw[g][:, 2 * j:2 * j + 2, :].rearrange("p a c -> p (a c)"), ident)
                    ins.then_inc(*p_s.inc("yt", g))

            swa(0, first=True)
            with pe.Fori(1, QT) as n:
                swa(n)

            pe.wait_ge(*a_s.at(QT - 1, "yt", 1))
            pe.wait_ge(negc_in, 16)

            def scores(n, p, s):
                r, cols = p + n * (NH // 2), (n + 1) * P
                pe.wait_ge(*d_fs.at(r, "q", s))
                for c in range(0, cols, HT):
                    w = min(HT, cols - c)
                    ins = mm(ps[s][:, c:c + w], qf[s][:],
                             k65[:, bass.ds(2 * p + s, 1), c:c + w].rearrange("p a c -> p (a c)"), start=True, stop=True)
                ins.then_inc(*p_fs.inc("s", s))

            def fox(n, p, following):
                r = p + n * (NH // 2)
                for s in range(2):
                    pe.wait_ge(*a_fs.at(r, "exp", s))
                    if following:
                        scores(*following, s)
                    if s:
                        pe.wait_ge(*a_fo.at(r, "pt", 0))
                    for k in range(n + 1):
                        ins = nc.tensor.transpose(ps[2][:, k * P:(k + 1) * P], pr[s][:, k * P:(k + 1) * P], ident)
                    ins.then_inc(*p_fo.inc("t", s))
                for s in range(2):
                    pe.wait_ge(*a_fo.at(r, "pt", s))
                    for k in range(n + 1):
                        ins = mm(ps[3][:, s * HT:s * HT + P], pt[s][:, k, :], vb[:, k, bass.ds(p * P, P)],
                                 start=k == 0, stop=k == n)
                    ins.then_inc(*p_fo.inc("pv", s))
                pe.wait_ge(*d_fo.at(r, "y", 1))
                nc.tensor.transpose(ps[3][:, HT + P:HT + 2 * P], yf[:], ident).then_inc(*p_fy.inc("y"))

            for s in range(2):
                scores(0, 0, s)
            for n in range(QT):
                with pe.Fori(0, NH // 2 - 1) as p:
                    fox(n, p, (n, p + 1))
                fox(n, NH // 2 - 1, (n + 1, 0) if n < QT - 1 else None)

            def mix(i, first=False):
                for t in range(2):
                    m, n, s = 2 * i + t, U_MIX + 6 * i + 3 * t, (U_MIX + 3 * t) % 2
                    fresh = first and t == 0
                    if not fresh:
                        pe.wait_ge(*d_mx.at(m - 1, "ga"))
                    tile(n, s, ps[0], of(u3_hi), of(u3_lo))
                    if not fresh:
                        pe.wait_ge(*d_mx.at(m - 1, "gb"))
                    tile(n + 1, (s + 1) % 2, ps[1], of(u3_hi), of(u3_lo))
                    if not fresh:
                        pe.wait_ge(*d_mx.at(m - 1, "b"))
                    parts = [(ps[2 + k // 4], y_hi[:, k, :], y_lo[:, k, :], k % 4 == 0, k % 4 == 3, [d_y.at(k, "lo")])
                             for k in range(KT)]
                    for _, ins in unit(n + 2, s, parts):
                        pass
                    ins.then_inc(w_used, 1)

            pe.wait_ge(*a_fy.at(QT * NH // 2 - 1, "y"))
            mix(0, first=True)
            with pe.Fori(1, KT // 2) as i:
                mix(i)

            def out2(i, first=False):
                for s in range(2):
                    if not first:
                        pe.wait_ge(*d_h3.at(2 * i + s - 2, "res"))
                    tile(U_MIXOUT + 2 * i + s, (U_MIXOUT + s) % 2, ps[s], of(m2_hi), of(m2_lo), lambda k: d_m2.at(k, "lo"))

            out2(0, first=True)
            with pe.Fori(1, KT // 2) as i:
                out2(i)

            def up2(p, n, s, first=False):
                for j in range(2):
                    if first:
                        pe.wait_ge(*d_h3.at(KT - 2 + j, "res"))
                    else:
                        pe.wait_ge(*d_e.at(p - 1, f"ev{j}"))
                    tile(n + j, (s + j) % 2, ps[j], of(u4_hi), of(u4_lo), (lambda k: d_h3l.at(k, "lo")) if first else None)
                    if first and j == 0:
                        sum_squares(5)

            def down2(p, n, s, b, first=False):
                for j in range(2):
                    parts = []
                    for m in range(4 * j, 4 * j + 4):
                        for k in range(2):
                            waits = [d_e.at(p, "lo1")] * (m == 0 and k == 0)
                            if k == 0:
                                if m >= 2:
                                    waits += [(d_ea.sem, KT * p + m - 1)]
                                elif not first:
                                    waits += [(d_ea.sem, KT * p + m - 1)]
                            parts.append((ps[2 + m % 2], e_hi[b][:, k, :], e_lo[b][:, k, :], k == 0, k == 1, waits))
                    for q, ins in unit(n + j, (s + j) % 2, parts):
                        if q % 2 and q < KT - 1:
                            ins.then_inc(dn2, 1)
                    ins.then_inc(w_used, 1)

            R2 = NF2 // 2
            up2(0, U_FFN2, U_FFN2 % 2, first=True)
            n0 = U_FFN2 + 2
            pe.wait_ge(var_done, 6)
            up2(1, n0, n0 % 2)
            down2(0, n0 + 2, n0 % 2, 0, first=True)
            with pe.Fori(0, (R2 - 2) // 2) as i:
                for t in range(2):
                    p = 2 * i + t + 2
                    up2(p, n0 + 4 + 8 * i + 4 * t, n0 % 2)
                    down2(p - 1, n0 + 6 + 8 * i + 4 * t, n0 % 2, (t + 1) % 2)
            down2(R2 - 1, n0 + 4 * (R2 - 1), n0 % 2, 1)

            for j in range(2):
                parts = []
                for m in range(4 * j, 4 * j + 4):
                    for k in range(2):
                        waits = [d_p.at(1, "lo")] * (m == 0 and k == 0)
                        if k == 0:
                            waits += [(a_pj.sem, m - 1)] if m >= 2 else [d_ea.at(NF2 // 2 * KT - 2 + m, "add")]
                        parts.append((ps[2 + m % 2], pe_hi[:, k, :], pe_lo[:, k, :], k == 0, k == 1, waits))
                for q, ins in unit(U_PLE + j, (U_PLE + j) % 2, parts):
                    if q % 2 and q < KT - 1:
                        ins.then_inc(dn3, 1)
                ins.then_inc(w_used, 1)

            def gate(i, first=False):
                for s in range(2):
                    pe.wait_ge(*(d_e.at(R2 - 1, f"ev{s}") if first else d_g.at(2 * i + s - 2, "ev")))
                    tile(U_PLE + 2 + 2 * i + s, s, ps[s], of(u5_hi), of(u5_lo), lambda k: d_h4.at(k, "lo"))
                    if first and s == 0:
                        pe.wait_ge(*a_pj.at(KT - 1, "ev"))
                        sum_squares(6)

            gate(0, first=True)
            with pe.Fori(1, KT // 2) as i:
                gate(i)
            sum_squares(7)

        @block.vector
        def _(dve):
            V = nc.vector

            def add_square(q, m):
                dve.wait_ge(sq_done, KT * q + m + 1)
                if isinstance(m, int) and m == 0:
                    V.tensor_copy(sums[:], sq[:]).then_inc(sq_added, 1)
                else:
                    dve.wait_ge(sq_added, KT * q + m)
                    V.tensor_tensor(sums[:], sums[:], sq[:], ALU.add).then_inc(sq_added, 1)

            def factor(q):
                dve.wait_ge(rs_done, q + 1)

            def lo_of(dst, src, hi, gain=None):
                if gain is None:
                    return V.tensor_tensor(dst, src, hi.bitcast(F32), ALU.subtract)
                return V.scalar_tensor_tensor(out=dst, in0=src, scalar=gain, in1=hi.bitcast(F32), op0=ALU.mult, op1=ALU.subtract)

            dve.wait_ge(cst_in, 16 * 6)
            V.memset(t1[:, 0:2], 0.0).then_inc(in1_freed, 1)
            for m in range(KT):
                add_square(0, m)
                dve.wait_ge(*a_x.at(m, "hi"))
                lo_of(u1_lo[:, m, :], x0[:, m, :], u1_hi[:, m, :], pcol("pre_mix_g", m)).then_inc(*d_x.inc("lo"))
            factor(0)

            V.memset(sums[:], 1.0).then_inc(*d_sh.begin())
            dve.wait_ge(d_sh.sem, 1)
            V.memset(sums[:].rearrange("p (c t) -> p c t", t=CH)[:, :, 0:1], 0.0).then_inc(*d_cv.begin())

            def shifted(t, src, mu, dst):
                dve.wait_ge(*d_sh.at(t - 1, "mix"))
                dve.wait_ge(w_used, t + 1)
                V.tensor_tensor(t1[:, 2:], src[:], rs[:], ALU.mult).then_inc(in1_freed, 1)
                dve.wait_ge(in1_freed, t + 2)
                V.tensor_tensor(t2[:], t1[:, 1:T + 1], t1[:, 2:], ALU.subtract).then_inc(*d_sh.inc("diff"))
                dve.wait_ge(*d_sh.at(t, "diff"))
                V.scalar_tensor_tensor(out=dst, in0=t2[:], scalar=mu, in1=t1[:, 2:], op0=ALU.mult, op1=ALU.add)\
                    .then_inc(*d_sh.inc("mix"))

            dve.wait_ge(in1_freed, 1)
            for t, dst in enumerate((ta[:], sg[:, 0, :], sg[:, 1, :])):
                shifted(t, ps[t % 2], pcol("mu", 12 + t), dst)
            with dve.Fori(0, 6) as i:
                for s in range(2):
                    t = 2 * i + s
                    shifted(t + 3, ps[(s + 1) % 2], pcol("mu", t), rkv[:, bass.ds(t, 1), :].rearrange("p a c -> p (a c)"))
            dve.wait_ge(*d_sh.at(14, "mix"))
            with dve.Fori(0, 2) as i:
                for jj in range(2):
                    c, t, par_ = 2 * i + jj, 6 * i + 3 * jj + 15, (15 + 3 * jj) % 2
                    dve.wait_ge(*d_cv.at(c - 1, "out"))
                    dve.wait_ge(w_used, t + 1)
                    V.tensor_tensor(t2[:], ps[par_][:], rs[:], ALU.mult).then_inc(in1_freed, 1)
                    dve.wait_ge(w_used, t + 2)
                    V.tensor_tensor(t3[:], ps[(par_ + 1) % 2][:], rs[:], ALU.mult).then_inc(in1_freed, 1)
                    dve.wait_ge(in1_freed, t + 3)
                    V.tensor_tensor(t1[:, 2:], t2[:], t3[:], ALU.mult).then_inc(*d_cv.inc("prod"))
                    dve.wait_ge(*d_cv.at(c, "prod"))
                    V.tensor_scalar(t2[:], t1[:, 2:], pcol("conv_a", 8 + c), None, ALU.mult).then_inc(*d_cv.inc("tap2"))
                    dve.wait_ge(*d_cv.at(c, "tap2"))
                    V.scalar_tensor_tensor(out=t2[:], in0=t1[:, 1:T + 1], scalar=pcol("conv_a", 4 + c), in1=t2[:],
                                           op0=ALU.mult, op1=ALU.add).then_inc(*d_cv.inc("tap1"))
                    dve.wait_ge(*d_cv.at(c, "tap1"))
                    V.scalar_tensor_tensor(out=t2[:], in0=t1[:, 0:T], scalar=pcol("conv_a", c), in1=t2[:],
                                           op0=ALU.mult, op1=ALU.add).then_inc(*d_cv.inc("tap0"))
                    dve.wait_ge(w_used, t + 3)
                    V.tensor_tensor(t3[:], ps[par_][:], rs[:], ALU.mult).then_inc(in1_freed, 1)
                    dve.wait_ge(in1_freed, t + 4)
                    dve.wait_ge(*d_cv.at(c, "tap0"))
                    V.tensor_tensor(ya[:, bass.ds(c, 1), :].rearrange("p a c -> p (a c)"), t3[:], t2[:], ALU.mult)\
                        .then_inc(*d_cv.inc("out"))

            dve.wait_ge(*d_cv.at(3, "out"))
            for i in range(NP):
                def do(ins, name):
                    ins.then_inc(*d_pre.inc(name))
                    dve.wait_ge(*d_pre.at(i, name))

                ri_, ki, vi = r_[:, i, :], k_[:, i, :], v_[:, i, :]
                do(V.tensor_scalar(t2[:], ki, pcol("k_k", i), None, ALU.mult), "kkr")
                dve.wait_ge(*p_pre.at(i, "kss"))
                do(V.tensor_scalar(t3[:], ps[2][:], 1e-24, None, ALU.max), "clamp")
                dve.wait_ge(*a_pre.at(i, "kinv"))
                do(V.tensor_tensor(t2[:], t2[:], t3[:], ALU.mult), "kk")
                dve.wait_ge(*a_pre.at(i, "siga"))
                do(V.tensor_scalar(q2[:], q2[:], DECAY_SCALE, None, ALU.mult), "lw")
                do(V.tensor_tensor_scan(q3[:], sums[:], q2[:], 0.0, ALU.mult, ALU.add), "scan")
                do(V.tensor_tensor(q4[:], q3[:], q2[:], ALU.subtract), "cprev")
                dve.wait_ge(*a_pre.at(i, "eprev"))
                do(V.tensor_tensor(kap[:, i, :], t2[:], q4[:], ALU.mult), "kap")
                do(V.tensor_tensor(bet[:, i, :], t2[:], q1[:], ALU.mult), "bet")
                do(V.tensor_scalar(q1[:], q1[:], pcol("k_a", i), pcol("k_a", i), ALU.mult, ALU.subtract), "ika")
                do(V.scalar_tensor_tensor(out=ki, in0=q1[:], scalar=1.0, in1=ki, op0=ALU.add, op1=ALU.mult), "k4")
                do(V.scalar_tensor_tensor(out=q4[:], in0=ri_, scalar=pcol("r_k", i), in1=ki, op0=ALU.mult, op1=ALU.mult), "rk")
                dve.wait_ge(*p_pre.at(i, "bon"))
                do(V.tensor_tensor(bon[:, i, :], ps[3][:], vi, ALU.mult), "bon")
                dve.wait_ge(*a_pre.at(i, "eg"))
                do(V.tensor_tensor(ri_, ri_, q1[:], ALU.mult), "rho")
                do(V.tensor_copy(g_end[:, i, :], q1[:].rearrange("p (c t) -> p c t", t=CH)[:, :, CH - 1]), "gend")
                dve.wait_ge(*a_pre.at(i, "einv"))
                do(V.tensor_tensor(bet[:, i, :], bet[:, i, :], q2[:], ALU.mult), "betg")
                do(V.tensor_tensor(ki, ki, q2[:], ALU.mult), "eta")
            dve.wait_ge(*p_pre.at(NP - 1, "bon"))
            for t in (kap_d, bet_d, eta_d, rho_d, v_d):
                ins = V.memset(t[:], 0.0)
            ins.then_inc(*d_r.begin())

            def bank(s, b, half=0):
                o = 512 * (b % 2) + 256 * half
                return ps[2 * s + b // 2][:, o:o + 256].rearrange("p (j c) -> p j c", j=2)

            def both(t):
                return t.unsqueeze(1).broadcast_to([P, 2, P])

            with dve.Fori(0, NCH) as c:
                dve.wait_ge(*d_r.at(c - 1, "s", 1))

                def pair(t, s):
                    return t[:, 2 * s:2 * s + 2, :]

                def masked(name, src_step, dst, b, half, mask):
                    for s in range(2):
                        dve.wait_ge(*p_r.at(c, src_step, s))
                        V.tensor_tensor(pair(dst, s), bank(s, b, half), both(ptile(mask)), ALU.mult).then_inc(*d_r.inc(name, s))

                masked("wd", "w", wd, 0, 0, "up16")
                for s in range(2):
                    dve.wait_ge(*d_r.at(c, "wd", s))
                    V.tensor_tensor(pair(pa, s), both(ident), pair(wd, s), ALU.subtract).then_inc(*d_r.inc("p1", s))
                masked("nd", "n", nd, 1, 0, "low16")
                masked("noff", "n", n_off, 1, 0, "low_off")
                masked("h", "h", h_t, 2, 0, "up")
                masked("p", "pq", p_t, 3, 0, "up_diag")
                masked("q", "pq", q_t, 3, 1, "up_diag")
                for name, step, b, half in (("p2", "sq4", 3, 0), ("p3", "sq8", 1, 1), ("p4", "p4", 3, 1)):
                    for s in range(2):
                        dve.wait_ge(*p_r.at(c, step, s))
                        V.tensor_tensor(pair(pa, s), bank(s, b, half), pair(pa, s), ALU.add).then_inc(*d_r.inc(name, s))
                for name, step, b, dst in (("z0", "c1", 0, z0), ("y", "c2", 1, y_m)):
                    for s in range(2):
                        dve.wait_ge(*p_r.at(c, step, s))
                        V.tensor_copy(pair(dst, s), bank(s, b)).then_inc(*d_r.inc(name, s))
                for name, step, b, dst in (("z1", "c3", 2, z1), ("z2", "c4", 3, z2)):
                    for s in range(2):
                        dve.wait_ge(*p_r.at(c, step, s))
                        V.tensor_tensor(pair(dst, s), pair(y_m, s), bank(s, b), ALU.subtract).then_inc(*d_r.inc(name, s))
                for s in range(2):
                    dve.wait_ge(*p_r.at(c, "c5", s))
                    V.tensor_tensor(pair(u_m, s), bank(s, 0, 1), pair(y_m, s), ALU.subtract).then_inc(*d_r.inc("u", s))
                for s in range(2):
                    dve.wait_ge(*p_r.at(c, "y", s))
                    V.tensor_tensor(pair(s_m, s), bank(s, 1, 1), pair(s_m, s), ALU.add).then_inc(*d_r.inc("sadd", s))
                for s in range(2):
                    dve.wait_ge(*d_r.at(c, "sadd", s))
                    V.tensor_tensor(pair(s_m, s), pair(s_m, s),
                                    g_end[:, 2 * s:2 * s + 2, bass.ds(c, 1)].broadcast_to([P, 2, P]), ALU.mult)\
                        .then_inc(*d_r.inc("s", s))

            for k in range(NP):
                dve.wait_ge(*a_ya.at(k, "hi"))
                lo_of(m1_lo[k][:], ya[:, k, :], m1_hi[:, k, :]).then_inc(*d_ya.inc("lo"))
            for i in range(NP):
                def do(ins, name):
                    ins.then_inc(*d_gn.inc(name))
                    dve.wait_ge(*d_gn.at(i, name))

                dve.wait_ge(*p_gn.at(i, "mean"))
                do(V.tensor_tensor(q1[:], kap[:, i, :], ps[0][:], ALU.subtract), "cen")
                dve.wait_ge(*a_gn.at(i, "rstd"))
                do(V.tensor_tensor(q1[:], q1[:], q3[:], ALU.mult), "nrm")
                do(V.tensor_scalar(q1[:], q1[:], pcol("lnx_w", i), pcol("lnx_b", i), ALU.mult, ALU.add), "aff")
                do(V.tensor_tensor(q1[:], q1[:], bon[:, i, :], ALU.add), "bon")
                dve.wait_ge(*p_gn.at(i, "gate"))
                do(V.tensor_tensor(q1[:], q1[:], ps[2][:], ALU.mult), "gate")
                dve.wait_ge(*a_gn.at(i, "hi"))
                do(lo_of(m1_lo[NP + i][:], q1[:], m1_hi[:, NP + i, :]), "lo")

            for m in range(KT):
                add_square(1, m)
            factor(1)

            def residual(q, o, gain, gain_next, st, st_lo, a_st, hi, lo, before=None):
                for m in range(KT + 1):
                    if m < KT:
                        V.scalar_tensor_tensor(out=o[:, m, :], in0=o[:, m, :], scalar=pcol(gain, m), in1=rs[:],
                                               op0=ALU.mult, op1=ALU.mult).then_inc(*st.inc("scale"))
                        if before:
                            dve.wait_ge(*before(m))
                        dve.wait_ge(*st.at(m, "scale"))
                        V.tensor_tensor(h[:, m, :], h[:, m, :], o[:, m, :], ALU.add).then_inc(*st.inc("res"))
                    if m:
                        add_square(q, m - 1)
                        dve.wait_ge(*a_st.at(m - 1, "hi"))
                        lo_of(lo[:, m - 1, :], h[:, m - 1, :], hi[:, m - 1, :], pcol(gain_next, m - 1)).then_inc(*st_lo.inc("lo"))

            dve.wait_ge(w_used, U_FFN1)
            residual(2, o1, "post_mix_g", "pre_ffn_g", d_h1, d_h1l, a_h1, u2_hi, u2_lo, lambda m: (x_ld[m], 32))
            factor(2)

            for t in (fpg, fpu):
                ins = V.memset(t[:, 0:2], 0.0)
            ins.then_inc(setup_done, 1)
            dve.wait_ge(setup_done, 1)

            def round1(p, n, t, first=False):
                def conv(dst, src, j, names):
                    fc = PAR["ffn_conv_w"]
                    tile_ = p + NF1 * j
                    V.tensor_scalar(dst[:], src[:, 2:], par[:, bass.ds(tile_ + fc + 4 * NF1, 1)],
                                    par[:, bass.ds(tile_ + PAR["ffn_conv_b"], 1)], ALU.mult, ALU.add).then_inc(*d_f.inc(names[0]))
                    for q in (1, 0):
                        dve.wait_ge(*d_f.at(p, names[1 - q]))
                        V.scalar_tensor_tensor(out=dst[:], in0=src[:, q:T + q], scalar=par[:, bass.ds(tile_ + fc + 2 * NF1 * q, 1)],
                                               in1=dst[:], op0=ALU.mult, op1=ALU.add).then_inc(*d_f.inc(names[2 - q]))

                dve.wait_ge(w_used, n + 1)
                if not first:
                    dve.wait_ge(*d_f.at(p - 1, "lo"))
                V.tensor_tensor(fpg[:, 2:], ps[0][:], rs[:], ALU.mult).then_inc(*d_f.inc("evg"))
                dve.wait_ge(*d_f.at(p, "evg"))
                conv(cg, fpg, 0, ("cg1", "cg2", "cg3"))
                dve.wait_ge(w_used, n + 2)
                V.tensor_tensor(fpu[:, 2:], ps[1][:], rs[:], ALU.mult).then_inc(*d_f.inc("evu"))
                for m in range(KT):
                    if first:
                        V.memset(o1[:, m, :], 0.0).then_inc(*d_f.inc(f"add{m}"))
                        continue
                    if m < KT - 1:
                        dve.wait_ge(dn1, 7 * (p - 1) + m + 1)
                    else:
                        dve.wait_ge(w_used, n + 3)
                    V.tensor_tensor(o1[:, m, :], o1[:, m, :], ps[2 + m % 2][:], ALU.add).then_inc(*d_f.inc(f"add{m}"))
                dve.wait_ge(*d_f.at(p, "evu"))
                conv(cu, fpu, 1, ("cu1", "cu2", "cu3"))
                dve.wait_ge(*d_f.at(p, "cu3"))
                dve.wait_ge(*a_f.at(p, "gelu"))
                V.tensor_tensor(cu[:], cu[:], cg[:], ALU.mult).then_inc(*d_f.inc("prod"))
                dve.wait_ge(*a_f.at(p, "hi"))
                lo_of(f_lo[:, t, :], cu[:], f_hi[:, t, :]).then_inc(*d_f.inc("lo"))

            round1(0, U_FFN1, 0, first=True)
            with dve.Fori(0, (NF1 - 2) // 2) as i:
                for t in range(2):
                    round1(2 * i + t + 1, U_FFN1 + 2 + 6 * i + 3 * t, (t + 1) % 2)
            round1(NF1 - 1, U_FFN1 + 2 + 3 * (NF1 - 2), 1)
            dve.wait_ge(*d_f.at(NF1 - 1, "lo"))
            for m in range(KT):
                dve.wait_ge(*((dn1, 7 * (NF1 - 1) + m + 1) if m < KT - 1 else (w_used, U_IN2)))
                V.tensor_tensor(o1[:, m, :], o1[:, m, :], ps[2 + m % 2][:], ALU.add).then_inc(*d_f_last.inc("add"))
                if m:
                    add_square(3, m - 1)
            add_square(3, KT - 1)
            factor(3)
            residual(4, o1, "post_ffn_g", "g_mix", d_h2, d_h2l, a_h2, u3_hi, u3_lo)
            factor(4)

            def ev2(j, dst, part=slice(0, P), src=None):
                dve.wait_ge(w_used, U_IN2 + j + 1)
                return V.tensor_tensor(dst, ps[j % 2][part, :], rs[part, :], ALU.mult)

            ev2(0, fr[0][:], slice(0, 8)).then_inc(in2_freed, 1)
            for vt in range(5):
                ev2(1 + vt, v_cm[:, vt, :]).then_inc(in2_freed, 1)
            def do(ins, name):
                ins.then_inc(*d_fg.inc(name))
                dve.wait_ge(*d_fg.at(0, name))

            dve.wait_ge(in2_freed, 1)
            do(V.tensor_scalar(fr[0][:], fr[0][:], par[0:8, PAR["b_forget"]:PAR["b_forget"] + 1], None, ALU.add), "bias")
            do(V.scalar_tensor_tensor(out=fr[1][:], in0=fr[0][:], scalar=-1.0, in1=fr[0][:], op0=ALU.mult, op1=ALU.max), "abs")
            do(V.tensor_scalar(fr[0][:], fr[0][:], 0.0, None, ALU.min), "min")
            dve.wait_ge(*a_fg.at(0, "ln"))
            do(V.tensor_tensor(fr[0][:], fr[0][:], fr[1][:], ALU.subtract), "log")
            dve.wait_ge(spilled, 16 * KT)
            do(V.tensor_tensor_scan(negc[:], ptile("ones")[0:8, 0:1].broadcast_to([8, T]), fr[0][:], 0.0, ALU.mult, ALU.add),
               "scan")
            do(V.tensor_scalar(negc[:], negc[:], -1.0, None, ALU.mult), "neg")
            ev2(6, ka[:, P:]).then_inc(in2_freed, 1)
            for j in range(4):
                ev2(7 + j, k65[0:64, 2 * j, :], slice(0, 64))
                ev2(7 + j, k65[0:64, 2 * j + 1, :], slice(64, 128)).then_inc(in2_freed, 1)
            dve.wait_ge(*a_v.at(4, "t"))
            for j in range(4):
                ev2(11 + j, qa[:, j, :]).then_inc(in2_freed, 1)
            for j in range(4):
                ev2(15 + j, qb[:, j, :]).then_inc(in2_freed, 1)

            dve.wait_ge(negc_in, 16)
            V.memset(ka[:, 0:P], 0.0)
            V.memset(va[:, 0, :], 0.0)
            V.tensor_scalar(nsink[:], par[:, PAR["sinks"]:PAR["sinks"] + 8], -1.0, None, ALU.mult)
            for g in range(2):
                ins = V.memset(qs[g][64 * (1 - g):64 * (1 - g) + 64, :, :], 0.0)
            ins.then_inc(*d_si.inc("z"))
            dve.wait_ge(*d_si.at(0, "z"))
            dve.wait_ge(in2_freed, UNITS_IN2)

            def swa(n, variant):
                for half, name in ((0, "qe"), (1, "qo")):
                    for g in range(SW):
                        V.tensor_scalar(qs[g][64 * g:64 * g + 64, half::2, :],
                                        qa[64 * half:64 * half + 64, 2 * g:2 * g + 2, bass.ds(n * P, P)],
                                        HD ** -0.5, None, ALU.mult).then_inc(*d_s.inc(name, g))
                for j in range(4):
                    for g in range(SW):
                        if j == 0:
                            dve.wait_ge(*p_s.at(n, "s", g))
                        V.scalar_tensor_tensor(out=sc[g][:, j, :], in0=dist[:, variant, :], scalar=-(2.0 ** -(4 * g + j + 1)),
                                               in1=ps[g][:, j * 256:(j + 1) * 256], op0=ALU.mult, op1=ALU.add)\
                            .then_inc(*d_s.inc(f"b{j}", g))
                for g in range(SW):
                    dve.wait_ge(*d_s.at(n, "b3", g))
                    V.tensor_reduce(mx[:, 4 * g:4 * g + 4], sc[g][:], AX.X, ALU.max).then_inc(*d_s.inc("max", g))
                for g in range(SW):
                    c = slice(4 * g, 4 * g + 4)
                    dve.wait_ge(*d_s.at(n, "max", g))
                    V.scalar_tensor_tensor(out=nm[:, c], in0=mx[:, c], scalar=-1.0, in1=nsink[:, c], op0=ALU.mult, op1=ALU.min)\
                        .then_inc(*d_s.inc("neg", g))
                for g in range(SW):
                    c = slice(4 * g, 4 * g + 4)
                    dve.wait_ge(*d_s.at(n, "neg", g))
                    V.tensor_tensor(es[:, c], nm[:, c], nsink[:, c], ALU.subtract).then_inc(*d_s.inc("sd", g))
                for g in range(SW):
                    c = slice(4 * g, 4 * g + 4)
                    dve.wait_ge(*a_s.at(n, "e3", g))
                    V.tensor_tensor(ls[:, c], ls[:, c], es[:, c], ALU.add).then_inc(*d_s.inc("sum", g))
                for g in range(SW):
                    c = slice(4 * g, 4 * g + 4)
                    dve.wait_ge(*d_s.at(n, "sum", g))
                    V.reciprocal(ri[:, c], ls[:, c]).then_inc(*d_s.inc("inv", g))
                for g in range(SW):
                    dve.wait_ge(*p_s.at(n, "pv", g))
                    dve.wait_ge(*d_s.at(n, "inv", g))
                    V.tensor_tensor(ysw[g][:], ps[g][:, 0:512].rearrange("p (j c) -> p j c", j=4)[:, :, 64 * g:64 * g + 64],
                                    ri[:, 4 * g:4 * g + 4].unsqueeze(2).broadcast_to([P, 4, HD]), ALU.mult)\
                        .then_inc(*d_s.inc("y", g))

            swa(0, 1)
            with dve.Fori(1, QT) as n:
                swa(n, 0)

            dve.wait_ge(*p_s.at(QT - 1, "yt", 1))
            V.memset(qf[0][64:65, :], 1.0).then_inc(*d_fo.begin())
            V.memset(qf[1][64:65, :], 1.0).then_inc(*d_si.inc("z"))
            dve.wait_ge(*d_si.at(1, "z"))

            def queries(n, p):
                for s in range(2):
                    V.tensor_scalar(qf[s][0:64, :], qb[64 * s:64 * s + 64, bass.ds(p, 1), n * P:(n + 1) * P].rearrange("p a c -> p (a c)"),
                                    HD ** -0.5, None, ALU.mult).then_inc(*d_fs.inc("q", s))

            def maxima(n, p):
                r, cols = p + n * (NH // 2), (n + 1) * P
                for s in range(2):
                    dve.wait_ge(*p_fs.at(r, "s", s))
                    V.tensor_tensor(ps[s][:, n * P:cols], ps[s][:, n * P:cols], ptile("causal"), ALU.add).then_inc(*d_fs.inc("mask", s))
                for s in range(2):
                    dve.wait_ge(*d_fs.at(r, "mask", s))
                    V.tensor_reduce(mx[:, s:s + 1], ps[s][:, 0:cols], AX.X, ALU.max).then_inc(*d_fs.inc("max", s))
                for s in range(2):
                    dve.wait_ge(*d_fs.at(r, "max", s))
                    V.tensor_scalar(nm[:, s:s + 1], mx[:, s:s + 1], -1.0, None, ALU.mult).then_inc(*d_fs.inc("neg", s))

            def fox(n, p, following):
                r = p + n * (NH // 2)
                dve.wait_ge(*d_fo.at(r - 1, "y", 1))
                if following:
                    queries(*following)
                for s in range(2):
                    dve.wait_ge(*a_fs.at(r, "exp", s))
                    V.reciprocal(ri[:, s:s + 1], ls[:, s:s + 1]).then_inc(*d_fo.inc("inv", s))
                if following:
                    maxima(*following)
                for s in range(2):
                    dve.wait_ge(*p_fo.at(r, "pv", s))
                    dve.wait_ge(*d_fo.at(r, "inv", s))
                    V.tensor_scalar(yf[:, 64 * s:64 * s + 64], ps[3][:, s * (HT + 64):s * (HT + 64) + 64], ri[:, s:s + 1],
                                    None, ALU.mult).then_inc(*d_fo.inc("y", s))

            queries(0, 0)
            maxima(0, 0)
            for n in range(QT):
                with dve.Fori(0, NH // 2 - 1) as p:
                    fox(n, p, (n, p + 1))
                fox(n, NH // 2 - 1, (n + 1, 0) if n < QT - 1 else None)

            for k in range(KT):
                dve.wait_ge(*a_y.at(k, "hi"))
                src = qa[:, k, :] if k < 4 else qb[:, k - 4, :]
                lo_of(y_lo[:, k, :], src, y_hi[:, k, :]).then_inc(*d_y.inc("lo"))
            dve.wait_ge(*a_y.at(KT - 1, "hi"))

            def mix(m, first=False):
                n = 3 * m + U_MIX
                if not first:
                    dve.wait_ge(*d_mx.at(m - 1, "mix"))
                dve.wait_ge(w_used, n + 1)
                V.tensor_tensor(ga[:], ps[0][:], rs[:], ALU.mult).then_inc(*d_mx.inc("ga"))
                dve.wait_ge(w_used, n + 2)
                V.tensor_tensor(gb[:], ps[1][:], rs[:], ALU.mult).then_inc(*d_mx.inc("gb"))
                dve.wait_ge(w_used, n + 3)
                dve.wait_ge(*a_mx.at(m, "siga"))
                V.tensor_tensor(ga[:], ga[:], ps[2][:], ALU.mult).then_inc(*d_mx.inc("a"))
                dve.wait_ge(*a_mx.at(m, "sigb"))
                V.tensor_tensor(gb[:], gb[:], ps[3][:], ALU.mult).then_inc(*d_mx.inc("b"))
                dve.wait_ge(*d_mx.at(m, "b"))
                V.tensor_tensor(mixed[:, bass.ds(m, 1), :].rearrange("p a c -> p (a c)"), ga[:], gb[:], ALU.add)\
                    .then_inc(*d_mx.inc("mix"))

            mix(0, first=True)
            with dve.Fori(1, KT) as m:
                mix(m)
            dve.wait_ge(w_used, U_MIXOUT)
            for k in range(KT):
                dve.wait_ge(*a_m2.at(k, "hi"))
                lo_of(m2_lo[:, k, :], mixed[:, k, :], m2_hi[:, k, :]).then_inc(*d_m2.inc("lo"))

            for m in range(KT + 1):
                if m < KT:
                    dve.wait_ge(w_used, U_MIXOUT + m + 1)
                    dve.wait_ge(x_ld[m], 48)
                    V.tensor_tensor(h[:, m, :], ps[m % 2][:], h[:, m, :], ALU.add).then_inc(*d_h3.inc("res"))
                if m:
                    add_square(5, m - 1)
                    dve.wait_ge(*a_h3.at(m - 1, "hi"))
                    lo_of(u4_lo[:, m - 1, :], h[:, m - 1, :], u4_hi[:, m - 1, :], pcol("g_mlp", m - 1)).then_inc(*d_h3l.inc("lo"))
            factor(5)

            def hidden(p, n, t):
                for j in range(2):
                    dve.wait_ge(w_used, n + j + 1)
                    V.scalar_tensor_tensor(out=fa[j][:], in0=ps[j][:], scalar=0.0, in1=rs[:], op0=ALU.max, op1=ALU.mult)\
                        .then_inc(*d_e.inc(f"ev{j}"))
                    dve.wait_ge(*a_e.at(p, f"hi{j}"))
                    lo_of(e_lo[t][:, j, :], fs[j][:], e_hi[t][:, j, :]).then_inc(*d_e.inc(f"lo{j}"))

            def adds(p, n, tail=None):
                for m in range(KT):
                    dve.wait_ge(*((w_used, n + m // 4 + 1) if m % 4 == 3 else (dn2, 6 * p + 3 * (m // 4) + m % 4 + 1)))
                    V.tensor_tensor(h[:, m, :], h[:, m, :], ps[2 + m % 2][:], ALU.add).then_inc(*d_ea.inc("add"))
                    if tail:
                        tail(m)

            n0 = U_FFN2 + 2
            hidden(0, U_FFN2, 0)
            hidden(1, n0, 1)
            adds(0, n0 + 2)
            with dve.Fori(0, (NF2 // 2 - 2) // 2) as i:
                for t in range(2):
                    p = 2 * i + t + 2
                    hidden(p, n0 + 4 + 8 * i + 4 * t, t)
                    adds(p - 1, n0 + 6 + 8 * i + 4 * t)
            R2 = NF2 // 2

            def split4(m):
                add_square(6, m)
                dve.wait_ge(*a_h4.at(m, "hi"))
                lo_of(u5_lo[:, m, :], h[:, m, :], u5_hi[:, m, :], pcol("g_ple", m)).then_inc(*d_h4.inc("lo"))

            for k in range(2):
                dve.wait_ge(*a_p.at(k, "hi"))
                lo_of(pe_lo[:, k, :], pe_raw[:, k, :], pe_hi[:, k, :]).then_inc(*d_p.inc("lo"))
            adds(R2 - 1, n0 + 4 * (R2 - 1), tail=lambda m: split4(m - 1) if m else None)
            split4(KT - 1)
            factor(6)

            def embed(i, first=False):
                for s in range(2):
                    m = 2 * i + s
                    hm = h[:, bass.ds(m, 1), :].rearrange("p a c -> p (a c)")
                    dve.wait_ge(w_used, U_PLE + 3 + m)
                    if not first:
                        dve.wait_ge(*d_g.at(m - 2, "res"))
                    V.tensor_tensor(gt[s][:], ps[s][:], rs[:], ALU.mult).then_inc(*d_g.inc("ev"))
                    dve.wait_ge(*a_g.at(m, "sig"))
                    dve.wait_ge(*a_pj.at(KT - 1, "ev"))
                    V.tensor_tensor(gt[s][:], gt[s][:], proj[:, bass.ds(m, 1), :].rearrange("p a c -> p (a c)"), ALU.mult)\
                        .then_inc(*d_g.inc("prod"))
                    dve.wait_ge(*d_g.at(m, "prod"))
                    V.tensor_tensor(hm, hm, gt[s][:], ALU.add).then_inc(*d_g.inc("res"))
                    if not (first and s == 0):
                        add_square(7, m - 1)

            embed(0, first=True)
            with dve.Fori(1, KT // 2) as i:
                embed(i)
            add_square(7, KT - 1)
            factor(7)
            for m in range(KT):
                V.scalar_tensor_tensor(out=h[:, m, :], in0=h[:, m, :], scalar=pcol("g_final", m), in1=rs[:],
                                       op0=ALU.mult, op1=ALU.mult).then_inc(*d_o.inc("out"))

        @block.scalar
        def _(act):
            A = nc.scalar.activation

            def square(q, m, src):
                if q or m:
                    act.wait_ge(sq_added, KT * q + m)
                A(sq[:], src, ACT.Square).then_inc(sq_done, 1)

            def root(q):
                act.wait_ge(ss_done, q + 1)
                A(rs[:], ps[3][:], ACT.Ln, bias=pcol("rms_eps"), scale=1.0 / D).then_inc(var_done, 1)
                act.wait_ge(var_done, q + 1)
                A(rs[:], rs[:], ACT.Exp, scale=-0.5).then_inc(rs_done, 1)

            act.wait_ge(cst_in, 16)
            for m in range(KT):
                act.wait_ge(x_ld[m], 16)
                square(0, m, x0[:, m, :])
                A(u1_hi[:, m, :], x0[:, m, :], ACT.Copy, scale=pcol("pre_mix_g", m)).then_inc(*a_x.inc("hi"))
            root(0)
            act.wait_ge(*d_sh.at(0, "mix"))
            A(ta[0:64, :], ta[0:64, :], ACT.Tanh).then_inc(*a_mis.inc("tanh"))
            for j in range(2):
                act.wait_ge(*d_sh.at(1 + j, "mix"))
                A(sg[:, j, :], sg[:, j, :], ACT.Sigmoid).then_inc(*a_mis.inc(f"sig{j}"))

            for i in range(NP):
                act.wait_ge(*d_pre.at(i, "kkr"))
                A(t3[:], t2[:], ACT.Square).then_inc(*a_pre.inc("ksq"))
                act.wait_ge(*d_pre.at(i, "clamp"))
                A(t3[:], t3[:], ACT.Ln).then_inc(*a_pre.inc("kln"))
                act.wait_ge(*a_pre.at(i, "kln"))
                A(t3[:], t3[:], ACT.Exp, scale=-0.5).then_inc(*a_pre.inc("kinv"))
                act.wait_ge(*p_pre.at(i, "za"))
                A(q2[:], ps[0][:], ACT.Sigmoid, bias=pcol("w0", i)).then_inc(*a_pre.inc("sigz"))
                A(q1[:], ps[1][:], ACT.Sigmoid, bias=pcol("a0", i)).then_inc(*a_pre.inc("siga"))
                act.wait_ge(*d_pre.at(i, "cprev"))
                A(q4[:], q4[:], ACT.Exp).then_inc(*a_pre.inc("eprev"))
                act.wait_ge(*d_pre.at(i, "ika"))
                act.wait_ge(*d_pre.at(i, "k4"))
                A(q1[:], q3[:], ACT.Exp).then_inc(*a_pre.inc("eg"))
                A(q2[:], q3[:], ACT.Exp, scale=-1.0).then_inc(*a_pre.inc("einv"))

            def bank(s, b, half=0):
                o = 512 * (b % 2) + 256 * half
                return ps[2 * s + b // 2][:, o:o + 256].rearrange("p (j c) -> p j c", j=2)

            act.wait_ge(*d_pre.at(NP - 1, "eta"))
            A(s_m[:], ident.unsqueeze(1).broadcast_to([P, NP, P]), ACT.Copy, scale=0.0).then_inc(*a_r.begin())
            with act.Fori(0, NCH) as c:
                for name, step, b, half, dst in (("bt", "tr", 0, 0, bet_t), ("et", "tr", 0, 1, eta_t), ("vt", "tr", 1, 0, v_t),
                                                 ("w2", "sq2", 2, 0, w2m), ("n2", "sq2", 2, 1, n2m), ("w4", "sq4", 0, 0, w4m),
                                                 ("n4", "sq4", 0, 1, n4m), ("n8", "sq8", 2, 0, n8m), ("g", "g", 2, 1, g_m)):
                    for s in range(2):
                        act.wait_ge(*p_r.at(c, step, s))
                        A(dst[:, 2 * s:2 * s + 2, :], bank(s, b, half), ACT.Copy).then_inc(*a_r.inc(name, s))
                for hh in range(2):
                    rows = slice(64 * hh, 64 * hh + 64)
                    for s in range(2):
                        act.wait_ge(*p_r.at(c, "y", s))
                        A(kap[rows, 2 * s:2 * s + 2, bass.ds(c * CH, CH)], bank(s, 2, 1)[rows, :, 64 * hh:64 * hh + 64], ACT.Copy)\
                            .then_inc(*a_r.inc(f"y{hh}", s))

            for k in range(NP):
                A(m1_hi[:, k, :], ya[:, k, :], ACT.Copy).then_inc(*a_ya.inc("hi"))
            for i in range(NP):
                act.wait_ge(*d_gn.at(i, "cen"))
                A(q2[:], q1[:], ACT.Square).then_inc(*a_gn.inc("sq"))
                act.wait_ge(*p_gn.at(i, "var"))
                A(q3[:], ps[1][:], ACT.Ln, bias=pcol("gn_eps")).then_inc(*a_gn.inc("ln"))
                act.wait_ge(*a_gn.at(i, "ln"))
                A(q3[:], q3[:], ACT.Exp, scale=-0.5).then_inc(*a_gn.inc("rstd"))
                act.wait_ge(*d_gn.at(i, "gate"))
                A(m1_hi[:, NP + i, :], q1[:], ACT.Copy).then_inc(*a_gn.inc("hi"))
            act.wait_ge(*d_gn.at(NP - 1, "lo"))
            for m in range(KT):
                act.dma_start(h[:, m, :], x_in[m]).then_inc(x_ld[m], 16)
            for m in range(KT):
                act.wait_ge(w_used, U_OUT1 + m + 1)
                square(1, m, ps[m % 2][:])
                A(o1[:, m, :], ps[m % 2][:], ACT.Copy).then_inc(*a_o1.inc("ev"))
            root(1)
            for m in range(KT):
                act.wait_ge(*d_h1.at(m, "res"))
                square(2, m, h[:, m, :])
                A(u2_hi[:, m, :], h[:, m, :], ACT.Copy, scale=pcol("pre_ffn_g", m)).then_inc(*a_h1.inc("hi"))
            root(2)

            def round1(p, t):
                act.wait_ge(*d_f.at(p, "cg3"))
                A(cg[:], cg[:], ACT.Gelu_apprx_tanh).then_inc(*a_f.inc("gelu"))
                act.wait_ge(*d_f.at(p, "prod"))
                A(f_hi[:, t, :], cu[:], ACT.Copy).then_inc(*a_f.inc("hi"))

            with act.Fori(0, NF1 // 2) as i:
                for t in range(2):
                    round1(2 * i + t, t)
            for m in range(KT):
                act.wait_ge(*d_f_last.at(m, "add"))
                square(3, m, o1[:, m, :])
            root(3)
            for m in range(KT):
                act.wait_ge(*d_h2.at(m, "res"))
                square(4, m, h[:, m, :])
                A(u3_hi[:, m, :], h[:, m, :], ACT.Copy, scale=pcol("g_mix", m)).then_inc(*a_h2.inc("hi"))
                act.dma_start(h_spill[m], h[:, m, :]).then_inc(spilled, 16)
            root(4)

            act.wait_ge(*d_fg.at(0, "abs"))
            A(fr[1][:], fr[1][:], ACT.Exp, scale=-1.0).then_inc(*a_fg.inc("exp"))
            act.wait_ge(*a_fg.at(0, "exp"))
            A(fr[1][:], fr[1][:], ACT.Ln, bias=1.0).then_inc(*a_fg.inc("ln"))
            act.wait_ge(spilled, 16 * KT)
            for vt in range(5):
                act.wait_ge(*p_v.at(vt, "t"))
                src = ps[2 + vt % 2][:].rearrange("p (k c) -> p k c", c=P)
                dst = va[:, 1:, :] if vt == 0 else vb[:, :, (vt - 1) * P:vt * P]
                A(dst, src, ACT.Copy).then_inc(*a_v.inc("t"))
            act.wait_ge(*d_fg.at(0, "neg"))
            act.dma_start(k65[64:65, :, :], negc[:]).then_inc(negc_in, 16)

            def swa(n):
                for g in range(SW):
                    act.wait_ge(*d_s.at(n, "sd", g))
                    A(es[:, 4 * g:4 * g + 4], es[:, 4 * g:4 * g + 4], ACT.Exp).then_inc(*a_s.inc("es", g))
                for j in range(4):
                    for g in range(SW):
                        c = slice(4 * g + j, 4 * g + j + 1)
                        A(sc[g][:, j, :], sc[g][:, j, :], ACT.Exp, bias=nm[:, c], accum_out=ls[:, c]).then_inc(*a_s.inc(f"e{j}", g))
                for g in range(SW):
                    act.wait_ge(*p_s.at(n, "t", g))
                    if g:
                        act.wait_ge(*p_s.at(n, "pv", 0))
                    A(pt_a[:].rearrange("p k c -> p (k c)"), ps[2 + g][:], ACT.Copy).then_inc(*a_s.inc("pt", g))
                for g in range(SW):
                    act.wait_ge(*p_s.at(n, "yt", g))
                    A(qa[:, 2 * g:2 * g + 2, bass.ds(n * P, P)], ps[g][:, 512:768].rearrange("p (j c) -> p j c", j=2), ACT.Copy)\
                        .then_inc(*a_s.inc("yt", g))

            with act.Fori(0, QT) as n:
                swa(n)

            def exponentials(n, p):
                r, cols = p + n * (NH // 2), (n + 1) * P
                for s in range(2):
                    act.wait_ge(*d_fs.at(r, "neg", s))
                    A(pr[s][:, 0:cols], ps[s][:, 0:cols], ACT.Exp, bias=nm[:, s:s + 1], accum_out=ls[:, s:s + 1])\
                        .then_inc(*a_fs.inc("exp", s))

            def fox(n, p, following):
                r, cols = p + n * (NH // 2), (n + 1) * P
                for s in range(2):
                    act.wait_ge(*p_fo.at(r, "t", s))
                    A(pt[s][:, 0:n + 1, :].rearrange("p k c -> p (k c)"), ps[2][:, 0:cols], ACT.Copy).then_inc(*a_fo.inc("pt", s))
                if following:
                    exponentials(*following)
                act.wait_ge(*p_fy.at(r, "y"))
                A(qb[:, bass.ds(p, 1), n * P:cols].rearrange("p a c -> p (a c)"), ps[3][:, HT + P:HT + 2 * P], ACT.Copy)\
                    .then_inc(*a_fy.inc("y"))

            exponentials(0, 0)
            for n in range(QT):
                with act.Fori(0, NH // 2 - 1) as p:
                    fox(n, p, (n, p + 1))
                fox(n, NH // 2 - 1, (n + 1, 0) if n < QT - 1 else None)

            act.wait_ge(*a_fy.at(QT * NH // 2 - 1, "y"))
            for k in range(KT):
                src = qa[:, k, :] if k < 4 else qb[:, k - 4, :]
                A(y_hi[:, k, :], src, ACT.Copy).then_inc(*a_y.inc("hi"))
            with act.Fori(0, KT) as m:
                act.wait_ge(*d_mx.at(m, "ga"))
                A(ga[:], ga[:], ACT.Sigmoid).then_inc(*a_mx.inc("siga"))
                act.wait_ge(*d_mx.at(m, "gb"))
                A(gb[:], gb[:], ACT.Sigmoid).then_inc(*a_mx.inc("sigb"))
            act.wait_ge(w_used, U_MIXOUT)
            for m in range(KT):
                act.dma_start(h[:, m, :], h_spill[m]).then_inc(x_ld[m], 16)
            for k in range(KT):
                act.wait_ge(*d_mx.at(k, "mix"))
                A(m2_hi[:, k, :], mixed[:, k, :], ACT.Copy).then_inc(*a_m2.inc("hi"))
            for m in range(KT):
                act.wait_ge(*d_h3.at(m, "res"))
                square(5, m, h[:, m, :])
                A(u4_hi[:, m, :], h[:, m, :], ACT.Copy, scale=pcol("g_mlp", m)).then_inc(*a_h3.inc("hi"))
            root(5)

            act.wait_ge(w_used, U_FFN2)
            for k in range(2):
                act.dma_start(pe_raw[:, k, :], p_in[k]).then_inc(p_ld, 16)
            act.wait_ge(p_ld, 32)
            for k in range(2):
                A(pe_hi[:, k, :], pe_raw[:, k, :], ACT.Copy).then_inc(*a_p.inc("hi"))
            with act.Fori(0, NF2 // 4) as i:
                for t in range(2):
                    p = 2 * i + t
                    for j in range(2):
                        act.wait_ge(*d_e.at(p, f"ev{j}"))
                        A(fs[j][:], fa[j][:], ACT.Square).then_inc(*a_e.inc(f"sq{j}"))
                        act.wait_ge(*a_e.at(p, f"sq{j}"))
                        A(e_hi[t][:, j, :], fs[j][:], ACT.Copy).then_inc(*a_e.inc(f"hi{j}"))
            for m in range(KT):
                act.wait_ge(*d_ea.at((NF2 // 2 - 1) * KT + m, "add"))
                square(6, m, h[:, m, :])
                A(u5_hi[:, m, :], h[:, m, :], ACT.Copy, scale=pcol("g_ple", m)).then_inc(*a_h4.inc("hi"))
            for m in range(KT):
                act.wait_ge(*((w_used, U_PLE + m // 4 + 1) if m % 4 == 3 else (dn3, 3 * (m // 4) + m % 4 + 1)))
                A(proj[:, m, :], ps[2 + m % 2][:], ACT.Copy).then_inc(*a_pj.inc("ev"))
            root(6)
            def embed(i, first=False):
                for s in range(2):
                    m = 2 * i + s
                    act.wait_ge(*d_g.at(m, "ev"))
                    A(gt[s][:], gt[s][:], ACT.Sigmoid).then_inc(*a_g.inc("sig"))
                    if not (first and s == 0):
                        act.wait_ge(*d_g.at(m - 1, "res"))
                        square(7, m - 1, h[:, bass.ds(m - 1, 1), :].rearrange("p a c -> p (a c)"))

            embed(0, first=True)
            with act.Fori(1, KT // 2) as i:
                embed(i)
            act.wait_ge(*d_g.at(KT - 1, "res"))
            square(7, KT - 1, h[:, KT - 1, :])
            root(7)
            for m in range(KT):
                act.wait_ge(*d_o.at(m, "out"))
                act.dma_start(out[m], h[:, m, :]).then_inc(stored, 16)
            act.wait_ge(stored, 16 * KT)


def pack_columns(w, cols):
    k = w.shape[0] // P
    out = np.zeros((P, k, P), np.float32)
    out[:, :, :len(cols)] = w[:, cols].reshape(k, P, len(cols)).transpose(1, 0, 2)
    return out


def weight_units(a):
    units = []

    def tile(w, start, n=P):
        units.append(pack_columns(w, np.arange(start, start + n)))

    w_in, w_out, w_up, w_down = a["w_in"][0], a["w_out"][0], a["w_up"][0], a["w_down"][0]
    q0 = 3 * CONV
    low = q0 + 3 * RWKV
    tile(w_in, low)
    tile(w_in, low + P)
    tile(w_in, low + 2 * P, GATE_R - P)
    for j in range(3 * RWKV // P):
        tile(w_in, q0 + j * P)
    for j in range(CONV // P):
        for part in (0, 2, 1):
            tile(w_in, part * CONV + j * P)
    for m in range(KT):
        tile(w_out, m * P)

    def rows(blocks):
        units.append(np.stack(blocks, 1))

    def block(w, k, m):
        return w[k * P:(k + 1) * P, m * P:(m + 1) * P]

    for p in range(NF1):
        tile(w_up, p * P)
        tile(w_up, FF1 + p * P)
        if p:
            rows([block(w_down, p - 1, m) for m in range(KT)])
    rows([block(w_down, NF1 - 1, m) for m in range(KT)])
    w2 = a["w_in_2"][0]
    off = dict(qa=0, ka=512, va=640, qb=768, kb=1280, vb=1792, f=2304, g=2312)
    tile(w2, off["f"], NH)
    tile(w2, off["va"])
    for j in range(4):
        tile(w2, off["vb"] + j * P)
    tile(w2, off["ka"])
    for name in ("kb", "qa", "qb"):
        for j in range(4):
            tile(w2, off[name] + j * P)
    for m in range(KT):
        tile(w2, off["g"] + m * P)
        tile(w2, off["g"] + D + m * P)
        rows([block(a["w_br_swa_2"][0], k, m) for k in range(4)] + [block(a["w_br_fox_2"][0], k, m) for k in range(4)])
    for m in range(KT):
        tile(a["w_mix_out_2"][0], m * P)
    ff1, ff2 = a["w_ff1_2"][0], a["w_ff2_2"][0]

    def down(p):
        for j in range(2):
            rows([block(ff2, 2 * p + k, m) for m in range(4 * j, 4 * j + 4) for k in range(2)])

    for p in range(NF2 // 2):
        tile(ff1, 2 * p * P)
        tile(ff1, (2 * p + 1) * P)
        if p:
            down(p - 1)
    down(NF2 // 2 - 1)
    for j in range(2):
        rows([block(a["w_ple_proj_2"][0], k, m) for m in range(4 * j, 4 * j + 4) for k in range(2)])
    for m in range(KT):
        tile(a["w_ple_gate_2"][0], m * P)
    assert len(units) == UNITS
    return np.ascontiguousarray(np.stack(units).reshape(UNITS, P, KT * P))


def parameters(a):
    par = np.zeros((P, N_PAR), np.float32)

    def put(name, v):
        n = -(-v.size // P)
        flat = np.zeros(n * P, np.float32)
        flat[:v.size] = v.reshape(-1)
        par[:, PAR[name]:PAR[name] + n] = flat.reshape(n, P).T

    for name in ("pre_mix_g", "w0", "a0", "k_k", "k_a", "r_k", "lnx_w", "lnx_b", "post_mix_g", "pre_ffn_g", "post_ffn_g",
                 "ffn_conv_b"):
        put(name, a[name][0])
    for name in ("g_mix", "g_mlp", "g_ple"):
        put(name, a[name + "_2"][0])
    put("g_final", a["g_final_2"])
    put("mu", a["shift_mu"][0])
    put("conv_a", a["conv_a_w"][0])
    put("ffn_conv_w", a["ffn_conv_w"][0])
    par[:NH, PAR["b_forget"]] = a["b_forget_2"][0]
    par[:, PAR["rms_eps"]] = RMS_EPS
    par[:, PAR["gn_eps"]] = GN_EPS
    par[:, PAR["sinks"]:PAR["sinks"] + NH] = a["swa_sinks_2"][0][None, :]
    return par


def constant_tables():
    i = np.arange(P)
    row, col = i[:, None], i[None, :]
    head, blk = row // CH == col // CH, row // 16 == col // 16
    m = {
        "ident": row == col,
        "ones": row >= 0 * col,
        "head_sum": head,
        "head_mean": head / HD,
        "up16": (row < col) & blk,
        "low16": (row > col) & blk,
        "low_off": (row > col) & head & ~blk,
        "up": (row < col) & head,
        "up_diag": (row <= col) & head,
        "causal": np.where(col <= row, 0.0, NEG),
    }
    consts = np.concatenate([np.broadcast_to(m[n], (P, P)).astype(np.float32) for n in CONSTS], 1)
    qi, si = row + P, np.arange(2 * P)[None, :]
    chunks = qi // CH - si // CH
    ok = (chunks >= 0) & (chunks <= 2)
    d = np.abs(qi - si).astype(np.float32)
    dists = np.stack([np.where(ok, d, -NEG), np.where(ok & (si >= P), d, -NEG)], 1).astype(np.float32)
    return np.ascontiguousarray(consts), np.ascontiguousarray(dists)


def kernel(**inputs):
    import concourse.bacc as _bacc
    from concourse import mybir as _mybir
    from concourse.bass_utils import run_bass_kernel_spmd as _run

    a = {k: np.asarray(v) for k, v in inputs.items()}
    consts, dists = constant_tables()
    w2 = np.zeros((P, RWKV), np.float32)
    w2[:DECAY_R] = a["w2"][0]
    a2 = np.zeros((P, RWKV), np.float32)
    a2[DECAY_R:] = a["a2"][0]
    g2 = np.zeros((P, 2, RWKV), np.float32)
    g2[:, 0] = a["g2"][0][:P]
    g2[:GATE_R - P, 1] = a["g2"][0][P:]
    arrays = {
        "xT": np.ascontiguousarray(a["x"][0].T).reshape(KT, P, T),
        "pT": np.ascontiguousarray(a["p_2"][0, 0].T).reshape(2, P, T),
        "weights": weight_units(a),
        "params": parameters(a),
        "consts": consts,
        "dists": dists,
        "w2p": w2,
        "a2p": a2,
        "g2p": g2,
    }
    nc = _bacc.Bacc("TRN2", target_bir_lowering=False, num_devices=1)
    args = [nc.dram_tensor(n, v.shape, _mybir.dt.float32, kind="ExternalInput").ap() for n, v in arrays.items()]
    out = nc.dram_tensor("outT", (KT, P, T), _mybir.dt.float32, kind="ExternalOutput").ap()
    build_program(nc, *args, out)
    r = _run(nc, [arrays], core_ids=[0])
    y = np.asarray(r.results[0]["outT"]).reshape(D, T)
    return np.ascontiguousarray(y.T)[None]
```

```python
from contextlib import ExitStack

import concourse.bass as bass
import numpy as np
from concourse import mybir

F32 = mybir.dt.float32
F32R = mybir.dt.float32r
ALU = mybir.AluOpType
ACT = mybir.ActivationFunctionType
AX = mybir.AxisListType

P = 128
T = 1024
HT = T // 2
D = 1024
KT = D // P
HD = 64
CONV = 512
RWKV = 512
DECAY_R, ICLR_R, GATE_R = 64, 64, 160
FF1 = 2816
NF1 = FF1 // P
FF2 = 4096
NF2 = FF2 // P
CH = 64
NCH = T // CH
NP = RWKV // P
QT = T // P
RMS_EPS = 1e-6
GN_EPS = HD * 1e-5
DECAY_SCALE = -float(np.exp(-0.5))
NEG = -1e30
NH = 8
DIRECT = (2, 4)

UNITS_IN1 = 27
UNITS_OUT1 = KT
UNITS_FFN1 = 3 * NF1
UNITS_IN2 = 19
UNITS_MIX = 3 * KT
UNITS_MIXOUT = KT
UNITS_FFN2 = 2 * NF2
UNITS_PLE = KT + 2
U_IN1 = 0
U_OUT1 = U_IN1 + UNITS_IN1
U_FFN1 = U_OUT1 + UNITS_OUT1
U_IN2 = U_FFN1 + UNITS_FFN1
U_MIX = U_IN2 + UNITS_IN2
U_MIXOUT = U_MIX + UNITS_MIX
U_FFN2 = U_MIXOUT + UNITS_MIXOUT
U_PLE = U_FFN2 + UNITS_FFN2
UNITS = U_PLE + UNITS_PLE
assert UNITS % 2 == 0

PAR = {}
_at = 0
for _name, _n in [("pre_mix_g", 8), ("mu", 15), ("conv_a", 12), ("w0", 4), ("a0", 4), ("k_k", 4), ("k_a", 4),
                  ("r_k", 4), ("lnx_w", 4), ("lnx_b", 4), ("post_mix_g", 8), ("pre_ffn_g", 8),
                  ("ffn_conv_w", 3 * 2 * NF1), ("ffn_conv_b", 2 * NF1), ("post_ffn_g", 8), ("g_mix", 8),
                  ("g_mlp", 8), ("g_ple", 8), ("g_final", 8), ("b_forget", 1), ("sinks", 8), ("rms_eps", 1),
                  ("gn_eps", 1)]:
    PAR[_name] = _at
    _at += _n
N_PAR = _at
CONSTS = ["ident", "ones", "head_sum", "head_mean", "up16", "low16", "low_off", "up", "up_diag", "causal"]
N_CONST = len(CONSTS) * P


class Steps:

    def __init__(self, sem, names, streams=1, offset=0):
        self.sem, self.names, self.streams, self.offset = sem, names, streams, offset
        self.emitted = 0

    def begin(self):
        return self.sem, 1

    def inc(self, name, stream=0):
        k = self.emitted % (len(self.names) * self.streams)
        assert (self.names[k // self.streams], k % self.streams) == (name, stream), (name, stream, self.names[k // self.streams])
        self.emitted += 1
        return self.sem, 1

    def at(self, rnd, name, stream=0):
        per = len(self.names) * self.streams
        return self.sem, self.offset + rnd * per + self.names.index(name) * self.streams + stream + 1


def build_program(nc, x_in, p_in, weights, params, consts, dists, w2_in, a2_in, g2_in, out):
    ctx = ExitStack()
    with ctx:
        base = 16512

        def at(name, shape, kib, dt=F32):
            n = int(np.prod(shape[1:])) * 4
            off = base + int(round(kib * 1024))
            assert off % 32 == 0 and off + n <= 229368, (name, off, n)
            return nc.alloc_sbuf_tensor_at(name, shape, dt, offset=off)

        def sem(name):
            return ctx.enter_context(nc.semaphore(name))

        w_raw = [at(f"w_raw{s}", [P, 8, P], 4 * s) for s in range(2)]
        w_hi = [at(f"w_hi{s}", [P, 8, P], 8 + 4 * s, F32R) for s in range(2)]
        w_lo = [at(f"w_lo{s}", [P, 8, P], 16 + 4 * s, F32R) for s in range(2)]
        par = at("par", [P, N_PAR], 24)
        cst = at("cst", [P, N_CONST], 25.5)
        small = at("small", [P, 64], 30.5)
        dist = at("dist", [P, 2, 2 * P], 30.75)
        rs = at("rs", [P, T], 32.75)
        sums = at("sums", [P, T], 36.75)
        sq = at("sq", [P, T], 40.75)
        B0 = 44.75
        A1, A2, A3, A4 = B0, B0 + 32, B0 + 64, B0 + 96
        END = B0 + 128

        def ptile(n):
            return cst[:, CONSTS.index(n) * P:(CONSTS.index(n) + 1) * P]

        ident = ptile("ident")

        def pcol(name, k=0):
            return par[:, bass.ds(PAR[name] + k, 1)]

        def tiles8(name, kib, dt=F32, n=8):
            return at(name, [P, n, T], kib, dt)

        u1_hi, u1_lo = tiles8("u1_hi", A1, F32R), tiles8("u1_lo", A2, F32R)
        x0 = tiles8("x0", A3)
        rkv = tiles8("rkv", A3, n=12)
        ta = at("ta", [P, T], A4 + 16)
        sg = at("sg", [P, 2, T], A4 + 20)
        ya = at("ya", [P, NP, T], A4 + 28)
        w2 = at("w2", [P, RWKV], A4 + 44)
        a2 = at("a2", [P, RWKV], A4 + 46)
        g2 = at("g2", [P, 2, RWKV], A4 + 48)
        t1 = at("t1", [P, T + 2], A4 + 52)
        t2 = at("t2", [P, T], A4 + 56.25)
        t3 = at("t3", [P, T], A4 + 60.25)
        kap = at("kap", [P, NP, T], A1)
        bet = at("bet", [P, NP, T], A1 + 16)
        bon = at("bon", [P, NP, T], A2)
        q1, q2, q3, q4 = (at(f"q{j + 1}", [P, T], A2 + 16 + 4 * j) for j in range(4))
        r_, k_, v_ = (rkv[:, 4 * j:4 * j + 4, :] for j in range(3))
        g_end = at("g_end", [P, NP, NCH], 30.5)

        slots = [36.75, 38.75, 40.75, 42.75] + [A2 + 16 + 2 * j for j in range(8)] + [A4 + 52 + 2 * j for j in range(7)]
        slots += [A4 + 16, A4 + 18, A4 + 44, A4 + 46]
        slots.reverse()

        def mat(name):
            return at(name, [P, NP, P], slots.pop())

        kap_d, bet_d, eta_d, rho_d, v_d = (mat(n) for n in ("kap_d", "bet_d", "eta_d", "rho_d", "v_d"))
        wd, nd, n_off, h_t, p_t, q_t = (mat(n) for n in ("wd", "nd", "n_off", "h_t", "p_t", "q_t"))
        bet_t, eta_t, v_t = (mat(n) for n in ("bet_t", "eta_t", "v_t"))
        w2m, n2m, w4m, n4m, n8m = (mat(n) for n in ("w2m", "n2m", "w4m", "n4m", "n8m"))
        pa, g_m, s_m, u_m = (mat(n) for n in ("pa", "g_m", "s_m", "u_m"))
        z0, y_m, z1, z2 = w2m, n2m, w4m, n4m

        gn_set = [(q1, q2, q3), (t2, t3, q4)]
        m1_hi = tiles8("m1_hi", A3, F32R)
        m1_lo = [at(f"m1_lo{k}", [P, T], (A1 + 16 + 4 * k) if k < 4 else (A4 + 4 * (k - 4)), F32R) for k in range(8)]
        o1 = tiles8("o1", A2)
        h = tiles8("h", END)
        u2_hi, u2_lo = tiles8("u2_hi", A3, F32R), tiles8("u2_lo", A1, F32R)
        f_hi = at("f_hi", [P, 2, T], A4, F32R)
        f_lo = at("f_lo", [P, 2, T], A4 + 8, F32R)
        fpg = at("fpg", [P, T + 2], A4 + 16)
        fpu = at("fpu", [P, T + 2], A4 + 20.03125)
        cg = at("cg", [P, T], A4 + 24.0625)
        cu = sq
        u3_hi, u3_lo = tiles8("u3_hi", A3, F32R), tiles8("u3_lo", A1, F32R)
        qa = at("qa", [P, 4, T], A2)
        qb = at("qb", [P, 4, T], A2 + 16)
        v_cm = at("v_cm", [P, 5, T], A2)
        k65 = at("k65", [65, NH, T], A4)
        vb = at("vb", [P, QT, CONV], A4 + 32)
        ka = at("ka", [P, T + P], A4 + 48)
        va = at("va", [P, QT + 1, P], A4 + 52.5)
        W0 = A4 + 57
        negc = at("negc", [8, T], W0)
        fr = [at(f"fr{j}", [8, T], 36.75 + 4 * j) for j in range(2)]
        sc = [at(f"sc{g}", [P, 4, 2 * P], 36.75 + 4 * g) for g in range(2)]
        pt_a = at("pt_a", [P, 8, P], W0)
        qs = [at(f"qs{g}", [P, 4, P], W0 + 4 + 2 * g) for g in range(2)]
        ysw = [at(f"ysw{g}", [P, 4, HD], W0 + 8 + g) for g in range(2)]
        pr = [at(f"pr{s}", [P, T], 36.75 + 4 * s) for s in range(2)]
        pt = [at(f"pt{s}", [P, QT, P], W0 + 4 * s) for s in range(2)]
        yf = at("yf", [P, P], W0 + 8)
        qf = [at(f"qf{s}", [65, P], W0 + 8.5 + s / 2) for s in range(2)]
        mx, nm, ls, ri, es = (at(n, [P, 8], 30.5 + 0.03125 * j) for j, n in enumerate(["mx", "nm", "ls", "ri", "es"]))
        nsink = at("nsink", [P, 8], 30.5 + 0.03125 * 5)
        y_hi, y_lo = tiles8("y_hi", A4, F32R), tiles8("y_lo", END, F32R)
        mixed = tiles8("mixed", A2)
        ga = at("ga", [P, T], 36.75)
        gb = at("gb", [P, T], 40.75)
        m2_hi, m2_lo = tiles8("m2_hi", A3, F32R), tiles8("m2_lo", A1, F32R)
        u4_hi, u4_lo = tiles8("u4_hi", A2, F32R), tiles8("u4_lo", A4, F32R)
        e_hi = [at(f"e_hi{s}", [P, 2, T], (A1, A3)[s], F32R) for s in range(2)]
        e_lo = [at(f"e_lo{s}", [P, 2, T], (A1, A3)[s] + 8, F32R) for s in range(2)]
        fa = [at(f"fa{j}", [P, T], A1 + 16 + 4 * j) for j in range(2)]
        fs = [at(f"fs{j}", [P, T], A1 + 24 + 4 * j) for j in range(2)]
        u5_hi, u5_lo = tiles8("u5_hi", A2, F32R), tiles8("u5_lo", A4, F32R)
        pe_raw = at("pe_raw", [P, 2, T], A3 + 16)
        pe_hi = at("pe_hi", [P, 2, T], A3 + 24, F32R)
        pe_lo = at("pe_lo", [P, 2, T], A3 + 16, F32R)
        proj = tiles8("proj", A1)
        gt = [at(f"gt{j}", [P, T], A3 + 24 + 4 * j) for j in range(2)]

        h_spill = nc.dram_tensor("h_spill", (KT, P, T), F32, kind="Internal").ap()

        ps = [ctx.enter_context(nc.psum_tensor(f"ps{i}", [P, T], F32)) for i in range(4)]

        par_in, consts_in, tables_in = sem("par_in"), sem("consts_in"), sem("tables_in")
        x_ld = [sem(f"x_ld{m}") for m in range(KT)]
        w_landed = [sem(f"w_landed{s}") for s in range(2)]
        w_ready = sem("w_ready")
        w_used = sem("w_used")
        ss_done, var_done, rs_done = sem("ss_done"), sem("var_done"), sem("rs_done")
        sq_done, sq_added = sem("sq_done"), sem("sq_added")
        setup_done = sem("setup_done")

        def steps(name, names, streams=1, offset=0):
            return Steps(sem(name), names, streams, offset)

        a_x = steps("act_x", ["hi"])
        d_x = steps("dve_x", ["lo"])
        in1_freed = sem("in1_freed")
        d_sh = steps("dve_shift", ["diff", "mix"], offset=1)
        d_cv = steps("dve_conv", ["prod", "tap2", "tap1", "tap0", "out"], offset=1)
        a_mis = steps("act_misc", ["tanh", "sig0", "sig1"])
        d_kk = steps("dve_prep_key", ["kkr"])
        a_kk = steps("act_prep_key", ["ksq"])
        d_pre = steps("dve_prep", ["lw", "scan", "cprev", "clamp", "kk", "kap", "bet", "ika", "k4", "rk", "rho", "gend", "betg",
                                   "eta", "bon"])
        a_pre = steps("act_prep", ["sigz", "siga", "eprev", "kln", "kinv", "eg", "einv"])
        p_za, p_ks, p_bn = (steps(n, ["done"]) for n in ("pe_prep_low_rank", "pe_prep_norm", "pe_prep_bonus"))
        R_ST = 2
        l_st = steps("pool_stage", [f"{m}{hh}" for m in ("bet", "eta", "v", "kap", "rho") for hh in range(2)])
        p_r = steps("pe_rwkv", ["w", "n", "h", "pq", "tr", "sq2", "sq4", "sq8", "c1", "p4", "g", "c2", "c3", "c4", "c5",
                                "c6", "y"], R_ST)
        d_r = steps("dve_rwkv", ["wd", "nd", "noff", "h", "p1", "p", "q", "p2", "p3", "z0", "p4", "y", "z1", "z2", "u",
                                 "sadd", "s"], R_ST, offset=1)
        a_r = steps("act_rwkv", ["bt", "et", "w2", "n2", "vt", "w4", "n4", "n8", "g", "y0", "y1"], R_ST, offset=1)
        p_gn = steps("pe_gn", ["mean", "var", "gate"])
        d_gs = steps("dve_gn_centred", ["cen"])
        d_gn = steps("dve_gn_out", ["nrm", "aff", "bon", "gate", "lo"])
        a_gs = steps("act_gn_stats", ["sq", "ln", "rstd"])
        a_gn = steps("act_gn_out", ["hi"])
        d_ya = steps("dve_ya", ["lo"])
        a_ya = steps("act_ya", ["hi"])
        a_o1 = steps("act_o1", ["ev"])
        d_h1 = steps("dve_h1", ["scale", "res"])
        d_h1l = steps("dve_h1l", ["lo"])
        a_h1 = steps("act_h1", ["hi"])
        d_f = steps("dve_f", ["evg", "cg1", "cg2", "cg3", "evu"] + [f"add{m}" for m in range(KT)]
                    + ["cu1", "cu2", "cu3", "prod", "lo"])
        a_f = steps("act_f", ["gelu", "hi"])
        dn1 = sem("ffn1_tile_done")
        d_f_last = steps("dve_f_last", ["add"])
        d_h2 = steps("dve_h2", ["scale", "res"])
        d_h2l = steps("dve_h2l", ["lo"])
        a_h2 = steps("act_h2", ["hi"])
        spilled = sem("spilled")
        in2_freed = sem("in2_freed")
        d_fg = steps("dve_forget", ["bias", "abs", "min", "log", "scan", "neg"])
        a_fg = steps("act_forget", ["exp", "ln"])
        negc_in = sem("negc_in")
        p_v = steps("pe_v", ["t"])
        a_v = steps("act_v", ["t"])
        d_si = steps("dve_swa_init", ["z"])
        SW = 2
        d_ss = steps("dve_swa_scores", ["qe", "qo", "b0", "b1", "b2", "b3", "max", "neg", "sd"], SW)
        a_ss = steps("act_swa_scores", ["es", "e0", "e1", "e2", "e3"], SW)
        p_ss = steps("pe_swa_scores", ["s"], SW)
        d_so = steps("dve_swa_out", ["sum", "inv", "y"], SW, offset=1)
        a_so = steps("act_swa_out", ["pt", "yt"], SW)
        p_so = steps("pe_swa_out", ["t", "pv", "yt"], SW)
        d_fs = steps("dve_fox_scores", ["q", "mask", "max", "neg"], 2)
        a_fs = steps("act_fox_scores", ["exp"], 2)
        p_fs = steps("pe_fox_scores", ["s"], 2)
        d_fo = steps("dve_fox_out", ["inv", "y"], 2, offset=1)
        a_fo = steps("act_fox_out", ["pt"], 2)
        p_fo = steps("pe_fox_out", ["t", "pv"], 2)
        a_fy = steps("act_fox_y", ["y"])
        p_fy = steps("pe_fox_y", ["y"])
        d_y = steps("dve_ysplit", ["lo"])
        a_y = steps("act_ysplit", ["hi"])
        d_mx = steps("dve_mix", ["ga", "gb", "a", "b", "mix"])
        a_mx = steps("act_mix", ["siga", "sigb"])
        d_m2 = steps("dve_m2", ["lo"])
        a_m2 = steps("act_m2", ["hi"])
        d_h3 = steps("dve_h3", ["res"])
        d_h3l = steps("dve_h3l", ["lo"])
        a_h3 = steps("act_h3", ["hi"])
        d_e = steps("dve_e", ["ev0", "lo0", "ev1", "lo1"])
        a_e = steps("act_e", ["sq0", "hi0", "sq1", "hi1"])
        dn2 = sem("ffn2_tile_done")
        d_ea = steps("dve_e_add", ["add"])
        d_h4 = steps("dve_h4", ["lo"])
        a_h4 = steps("act_h4", ["hi"])
        p_ld = sem("p_ld")
        d_p = steps("dve_p", ["lo"])
        a_p = steps("act_p", ["hi"])
        dn3 = sem("proj_tile_done")
        a_pj = steps("act_proj", ["ev"])
        d_g = steps("dve_g", ["ev", "prod", "res"])
        a_g = steps("act_g", ["sig"])
        d_o = steps("dve_o", ["out"])
        stored = sem("stored")
        l_hi = steps("pool_hi", ["hi"])

        HALVES = [slice(0, HT), slice(HT, T)]

        block = ctx.enter_context(nc.Block())

        @block.sync
        def _(sp):
            def load(n, s):
                sp.dma_start(w_raw[s][:].rearrange("p k m -> p (k m)"), weights[n]).then_inc(w_landed[s], 16)

            sp.dma_start(par[:], params).then_inc(par_in, 16)
            sp.dma_start(cst[:], consts).then_inc(consts_in, 16)
            for m in range(KT):
                sp.dma_start(x0[:, m, :], x_in[m]).then_inc(x_ld[m], 16)
                if m == 0:
                    load(0, 0)
            load(1, 1)
            for dst, src in ((dist[:], dists), (w2[:], w2_in), (a2[:], a2_in), (g2[:], g2_in)):
                sp.dma_start(dst, src).then_inc(tables_in, 16)
            with sp.Fori(1, UNITS // 2) as i:
                for s in range(2):
                    sp.wait_ge(w_ready, 2 * i + s - 1)
                    load(2 * i + s, s)

        @block.gpsimd
        def _(pool):
            def copy(dst, src, rows=slice(0, P)):
                n, k, c = src.shape
                ones = ptile("ones")[rows, 0:c].unsqueeze(1).broadcast_to([n, k, c])
                return nc.gpsimd.tensor_tensor(dst, src, ones, ALU.mult)

            def split(n, s, it, first=False):
                pool.wait_ge(w_landed[s], 16 * it + 16)
                if not first:
                    pool.wait_ge(w_used, n - 1)
                copy(w_hi[s][:], w_raw[s][:]).then_inc(*l_hi.inc("hi"))
                pool.wait_ge(l_hi.sem, n + 1)
                nc.gpsimd.tensor_tensor(w_lo[s][:], w_raw[s][:], w_hi[s][:].bitcast(F32), ALU.subtract).then_inc(w_ready, 1)

            pool.wait_ge(consts_in, 16)
            for s in range(2):
                split(s, s, 0, first=True)
            with pool.Fori(1, (U_OUT1 + 1) // 2) as i:
                for s in range(2):
                    split(2 * i + s, s, i)

            mats = (("bet", bet_d, bet, "tr"), ("eta", eta_d, k_, "tr"), ("v", v_d, v_, "tr"), ("kap", kap_d, kap, "c1"),
                    ("rho", rho_d, r_, "y"))

            def stage_chunk(c, first=False):
                for name, dst, src, freed_by in mats:
                    if not first:
                        pool.wait_ge(*p_r.at(c - 1, freed_by, 1))
                    for hh in range(2):
                        rows = slice(64 * hh, 64 * hh + 64)
                        copy(dst[rows, :, 64 * hh:64 * hh + 64], src[rows, :, bass.ds(c * CH, CH)], rows)\
                            .then_inc(*l_st.inc(f"{name}{hh}"))
                        pool.wait_ge(*l_st.at(c, f"{name}{hh}"))

            pool.wait_ge(w_ready, 2 * ((U_OUT1 + 1) // 2))
            pool.wait_ge(*d_pre.at(NP - 1, "bon"))
            pool.wait_ge(d_r.sem, 1)
            stage_chunk(0, first=True)
            with pool.Fori(1, NCH) as c:
                stage_chunk(c)

            with pool.Fori((U_OUT1 + 1) // 2, UNITS // 2) as i:
                for s in range(2):
                    split(2 * i + s, s, i)

        @block.tensor
        def _(pe):
            mm = nc.tensor.matmul

            def unit(n, s, parts):
                pe.wait_ge(w_ready, n + 1)
                for k, (acc, xh, xl, start, stop, waits) in enumerate(parts):
                    for w in waits:
                        pe.wait_ge(*w)
                    for j, (w, x) in enumerate(((w_hi, xh), (w_hi, xl), (w_lo, xh))):
                        for c in HALVES:
                            ins = mm(acc[:, c], w[s][:, k, :], x[:, c], start=start and j == 0, stop=stop and j == 2)
                    yield k, ins

            def tile(n, s, acc, xh, xl, ready=None):
                parts = [(acc, xh(k), xl(k), k == 0, k == KT - 1, [ready(k)] if ready else []) for k in range(KT)]
                for _, ins in unit(n, s, parts):
                    pass
                ins.then_inc(w_used, 1)

            def of(t):
                return lambda k: t[:, k, :]

            def tile_and_squares(q, n, s, acc, xh, xl, ready):
                for k, ins in unit(n, s, [(acc, xh(k), xl(k), k == 0, k == KT - 1, [ready(k)]) for k in range(KT)]):
                    if k == KT - 1:
                        ins.then_inc(w_used, 1)
                    pe.wait_ge(sq_done, KT * q + k + 1)
                    fp32(ps[3], ptile("ones"), (sq, sums)[k % 2], start=k == 0, stop=k == KT - 1).then_inc(sq_added, 1)

            def sum_squares(q):
                pe.wait_ge(sq_added, KT * (q + 1))
                for c in HALVES:
                    ins = mm(ps[3][:, c], ptile("ones"), sums[:, c], start=True, stop=True)
                ins.then_inc(ss_done, 1)

            def fp32(acc, lhsT, rhs, start=True, stop=True):
                for c in HALVES:
                    ins = mm(acc[:, c], lhsT, rhs[:, c], start=start, stop=stop)
                return ins

            pe.wait_ge(consts_in, 16)
            tile(0, 0, ps[0], of(u1_hi), of(u1_lo), lambda k: d_x.at(k, "lo"))
            sum_squares(0)
            with pe.Fori(0, UNITS_IN1 // 2) as i:
                for s in range(2):
                    n = 2 * i + s + 1
                    pe.wait_ge(in1_freed, 2 * i + s + 1)
                    tile(n, (s + 1) % 2, ps[(s + 1) % 2], of(u1_hi), of(u1_lo))

            pe.wait_ge(in1_freed, UNITS_IN1 + 1)
            pe.wait_ge(*a_mis.at(0, "sig1"))
            def low_rank(i):
                c = slice(i * P, (i + 1) * P)
                fp32(ps[0], w2[:, c], ta)
                fp32(ps[1], a2[:, c], ta).then_inc(*p_za.inc("done"))

            def norms(i):
                pe.wait_ge(*a_kk.at(i, "ksq"))
                fp32(ps[2], ptile("head_sum"), t3).then_inc(*p_ks.inc("done"))

            pe.wait_ge(tables_in, 16 * 4)
            low_rank(0)
            norms(0)
            for i in range(NP):
                if i + 1 < NP:
                    pe.wait_ge(*a_pre.at(i, "siga"))
                    low_rank(i + 1)
                pe.wait_ge(*d_pre.at(i, "rk"))
                fp32(ps[3], ptile("head_sum"), q4).then_inc(*p_bn.inc("done"))
                if i + 1 < NP:
                    norms(i + 1)

            def bank(s, b, half=0):
                o = 512 * (b % 2) + 256 * half
                return ps[2 * s + b // 2][:, o:o + 256].rearrange("p (j c) -> p j c", j=2)

            def products(s, dst, *terms, start=True, stop=True):
                for j in range(2):
                    for t, (a, b) in enumerate(terms):
                        ins = mm(dst[:, j, :], a[:, 2 * s + j, :], b[:, 2 * s + j, :], start=start and t == 0 and (stop or j == 0),
                                 stop=stop and t == len(terms) - 1 and (start or j == 1))
                return ins

            def turned(s, dst, src):
                for j in range(2):
                    ins = nc.tensor.transpose(dst[:, j, :], src[:, 2 * s + j, :], ident)
                return ins

            pe.wait_ge(*d_pre.at(NP - 1, "bon"))
            pe.wait_ge(d_r.sem, 1)
            pe.wait_ge(a_r.sem, 1)
            with pe.Fori(0, NCH) as c:
                pe.wait_ge(*l_st.at(c, "kap1"))
                for s in range(2):
                    products(s, bank(s, 0), (bet_d, kap_d)).then_inc(*p_r.inc("w", s))
                pe.wait_ge(*d_r.at(c - 1, "s", 1))
                for s in range(2):
                    products(s, bank(s, 1), (kap_d, bet_d)).then_inc(*p_r.inc("n", s))
                pe.wait_ge(*a_r.at(c - 1, "y1", 1))
                for s in range(2):
                    products(s, bank(s, 2), (eta_d, kap_d)).then_inc(*p_r.inc("h", s))
                pe.wait_ge(*l_st.at(c, "rho1"))
                for s in range(2):
                    products(s, bank(s, 3), (bet_d, rho_d))
                    products(s, bank(s, 3, 1), (eta_d, rho_d)).then_inc(*p_r.inc("pq", s))
                for s in range(2):
                    pe.wait_ge(*d_r.at(c, "wd", s))
                    turned(s, bank(s, 0), bet_d)
                    turned(s, bank(s, 0, 1), eta_d)
                    pe.wait_ge(*d_r.at(c, "noff", s))
                    turned(s, bank(s, 1), v_d).then_inc(*p_r.inc("tr", s))
                for s in range(2):
                    pe.wait_ge(*d_r.at(c, "h", s))
                    products(s, bank(s, 2), (nd, wd))
                    products(s, bank(s, 2, 1), (wd, nd)).then_inc(*p_r.inc("sq2", s))
                for s in range(2):
                    pe.wait_ge(*a_r.at(c, "n2", s))
                    pe.wait_ge(*d_r.at(c, "q", s))
                    products(s, bank(s, 3), (n2m, pa))
                    products(s, bank(s, 0), (n2m, w2m))
                    products(s, bank(s, 0, 1), (w2m, n2m)).then_inc(*p_r.inc("sq4", s))
                for s in range(2):
                    pe.wait_ge(*a_r.at(c, "n4", s))
                    pe.wait_ge(*d_r.at(c, "p2", s))
                    products(s, bank(s, 1, 1), (n4m, pa))
                    products(s, bank(s, 2), (w4m, n4m)).then_inc(*p_r.inc("sq8", s))
                for s in range(2):
                    products(s, bank(s, 0), (kap_d, s_m), (h_t, v_t)).then_inc(*p_r.inc("c1", s))
                for s in range(2):
                    pe.wait_ge(*a_r.at(c, "n8", s))
                    pe.wait_ge(*d_r.at(c, "p3", s))
                    products(s, bank(s, 3, 1), (n8m, pa)).then_inc(*p_r.inc("p4", s))
                for s in range(2):
                    pe.wait_ge(*d_r.at(c, "p4", s))
                    products(s, bank(s, 2, 1), (n_off, pa)).then_inc(*p_r.inc("g", s))
                for s in range(2):
                    pe.wait_ge(*d_r.at(c, "z0", s))
                    products(s, bank(s, 1), (pa, z0)).then_inc(*p_r.inc("c2", s))
                for s in range(2):
                    pe.wait_ge(*a_r.at(c, "g", s))
                    pe.wait_ge(*d_r.at(c, "y", s))
                    products(s, bank(s, 2), (g_m, y_m)).then_inc(*p_r.inc("c3", s))
                for s in range(2):
                    products(s, bank(s, 1, 1), (eta_t, v_t), stop=False)
                for s in range(2):
                    pe.wait_ge(*d_r.at(c, "z1", s))
                    products(s, bank(s, 3), (g_m, z1)).then_inc(*p_r.inc("c4", s))
                for s in range(2):
                    products(s, bank(s, 2, 1), (s_m, rho_d), (v_t, q_t), stop=False)
                for s in range(2):
                    pe.wait_ge(*d_r.at(c, "z2", s))
                    products(s, bank(s, 0, 1), (g_m, z2)).then_inc(*p_r.inc("c5", s))
                for s in range(2):
                    pe.wait_ge(*d_r.at(c, "u", s))
                    products(s, bank(s, 1, 1), (bet_t, u_m), start=False).then_inc(*p_r.inc("c6", s))
                for s in range(2):
                    products(s, bank(s, 2, 1), (u_m, p_t), start=False).then_inc(*p_r.inc("y", s))

            pe.wait_ge(*a_r.at(NCH - 1, "y1", 1))
            pe.wait_ge(*d_r.at(NCH - 1, "s", 1))
            for i in range(NP):
                c = slice(i * P, (i + 1) * P)
                if i:
                    pe.wait_ge(*d_gs.at(i - 1, "cen"))
                fp32(ps[0], ptile("head_mean"), kap[:, i, :]).then_inc(*p_gn.inc("mean"))
                pe.wait_ge(*a_gs.at(i, "sq"))
                fp32(ps[1], ptile("head_mean"), gn_set[i % 2][1]).then_inc(*p_gn.inc("var"))
                if i:
                    pe.wait_ge(*d_gn.at(i - 1, "gate"))
                fp32(ps[2], g2[:, 0, c], sg[:, 0, :], stop=False)
                fp32(ps[2], g2[:, 1, c], sg[:, 1, :], start=False).then_inc(*p_gn.inc("gate"))

            def out1(i, first=False):
                for s in range(2):
                    if not first:
                        pe.wait_ge(*a_o1.at(2 * i + s - 2, "ev"))
                    tile(U_OUT1 + 2 * i + s, (U_OUT1 + s) % 2, ps[s], of(m1_hi), lambda k: m1_lo[k][:],
                         lambda k: d_ya.at(k, "lo") if k < NP else d_gn.at(k - NP, "lo"))

            pe.wait_ge(*a_gs.at(NP - 1, "ln"))
            out1(0, first=True)
            with pe.Fori(1, KT // 2) as i:
                out1(i)
            sum_squares(1)

            def up1(p, n, s, first=False):
                for j, ev in enumerate(("evg", "evu")):
                    if not first:
                        pe.wait_ge(*d_f.at(p - 1, ev))
                    if first and j == 0:
                        tile_and_squares(2, n, s, ps[0], of(u2_hi), of(u2_lo), lambda k: d_h1l.at(k, "lo"))
                    else:
                        tile(n + j, (s + j) % 2, ps[j], of(u2_hi), of(u2_lo))

            def down1(p, n, s, b):
                parts = [(ps[2 + m % 2], f_hi[:, b, :], f_lo[:, b, :], True, True,
                          [d_f.at(p, "lo")] * (m == 0) + [d_f.at(p, f"add{m + 6}") if m < 2 else d_f.at(p + 1, f"add{m - 2}")])
                         for m in range(KT)]
                for m, ins in unit(n, s, parts):
                    if m < KT - 1:
                        ins.then_inc(dn1, 1)
                ins.then_inc(w_used, 1)

            up1(0, U_FFN1, U_FFN1 % 2, first=True)
            n0 = U_FFN1 + 2
            with pe.Fori(0, (NF1 - 2) // 2) as i:
                for t in range(2):
                    p = 2 * i + t + 1
                    up1(p, n0 + 6 * i + 3 * t, (n0 + 3 * t) % 2)
                    down1(p - 1, n0 + 6 * i + 3 * t + 2, (n0 + 3 * t) % 2, t)
            n1 = n0 + 3 * (NF1 - 2)
            up1(NF1 - 1, n1, n1 % 2)
            down1(NF1 - 2, n1 + 2, n1 % 2, (NF1 - 2) % 2)
            parts = [(ps[2 + m % 2], f_hi[:, 1, :], f_lo[:, 1, :], True, True,
                      [d_f.at(NF1 - 1, "lo")] * (m == 0)
                      + [d_f.at(NF1 - 1, f"add{m + 6}") if m < 2 else (d_f_last.sem, m - 1)]) for m in range(KT)]
            for m, ins in unit(n1 + 3, (n1 + 3) % 2, parts):
                if m < KT - 1:
                    ins.then_inc(dn1, 1)
            ins.then_inc(w_used, 1)
            pe.wait_ge(*d_f_last.at(KT - 1, "add"))
            sum_squares(3)

            def in2(n, s):
                tile(n, s, ps[(s + U_IN2) % 2], of(u3_hi), of(u3_lo))

            tile_and_squares(4, U_IN2, U_IN2 % 2, ps[0], of(u3_hi), of(u3_lo), lambda k: d_h2l.at(k, "lo"))
            for j in range(1, 6):
                if j > 1:
                    pe.wait_ge(in2_freed, j - 1)
                in2(U_IN2 + j, (U_IN2 + j) % 2)
            pe.wait_ge(var_done, 5)
            for vt in range(5):
                pe.wait_ge(in2_freed, vt + 2)
                if vt > 1:
                    pe.wait_ge(*a_v.at(vt - 2, "t"))
                for k in range(QT):
                    ins = nc.tensor.transpose(ps[2 + vt % 2][:, k * P:(k + 1) * P], v_cm[:, vt, k * P:(k + 1) * P], ident)
                ins.then_inc(*p_v.inc("t"))
            pe.wait_ge(in2_freed, 5)
            in2(U_IN2 + 6, (U_IN2 + 6) % 2)
            with pe.Fori(0, 6) as i:
                for s in range(2):
                    pe.wait_ge(in2_freed, 2 * i + s + 6)
                    in2(2 * i + (U_IN2 + 7 + s), (U_IN2 + 7 + s) % 2)

            pe.wait_ge(in2_freed, UNITS_IN2)
            pe.wait_ge(*a_v.at(4, "t"))

            def swa_scores(n, g):
                pe.wait_ge(*d_ss.at(n, "qo", g))
                for j in range(4):
                    ins = mm(ps[g][:, j * 256:(j + 1) * 256], qs[g][:, j, :], ka[:, bass.ds(n * P, 2 * P)],
                             start=True, stop=True)
                ins.then_inc(*p_ss.inc("s", g))

            def swa(n, following):
                for g in range(SW):
                    pe.wait_ge(*a_ss.at(n, "e3", g))
                    if following is not None:
                        swa_scores(following, g)
                    if g:
                        pe.wait_ge(*a_so.at(n, "pt", 0))
                    for j in range(4):
                        for k in range(2):
                            o = (2 * j + k) * P
                            ins = nc.tensor.transpose(ps[2][:, o:o + P], sc[g][:, j, k * P:(k + 1) * P], ident)
                    ins.then_inc(*p_so.inc("t", g))
                for g in range(SW):
                    pe.wait_ge(*a_so.at(n, "pt", g))
                    for j in range(4):
                        for k in range(2):
                            ins = mm(ps[3][:, g * HT + j * P:g * HT + (j + 1) * P], pt_a[:, 2 * j + k, :],
                                     va[:, bass.ds(n + k, 1), :].rearrange("p a c -> p (a c)"), start=k == 0, stop=k == 1)
                    ins.then_inc(*p_so.inc("pv", g))
                for g in range(SW):
                    pe.wait_ge(*d_so.at(n, "y", g))
                    for j in range(2):
                        ins = nc.tensor.transpose(ps[3][:, g * HT + j * P:g * HT + (j + 1) * P],
                                                  ysw[g][:, 2 * j:2 * j + 2, :].rearrange("p a c -> p (a c)"), ident)
                    ins.then_inc(*p_so.inc("yt", g))

            for g in range(SW):
                swa_scores(0, g)
            with pe.Fori(0, QT - 1) as n:
                swa(n, n + 1)
            swa(QT - 1, None)

            pe.wait_ge(*a_so.at(QT - 1, "yt", 1))
            pe.wait_ge(negc_in, 16)

            def scores(n, p, s):
                r, cols = p + n * (NH // 2), (n + 1) * P
                pe.wait_ge(*d_fs.at(r, "q", s))
                for c in range(0, cols, HT):
                    w = min(HT, cols - c)
                    ins = mm(ps[s][:, c:c + w], qf[s][:],
                             k65[:, bass.ds(2 * p + s, 1), c:c + w].rearrange("p a c -> p (a c)"), start=True, stop=True)
                ins.then_inc(*p_fs.inc("s", s))

            def fox(n, p, following):
                r = p + n * (NH // 2)
                for s in range(2):
                    pe.wait_ge(*a_fs.at(r, "exp", s))
                    if following:
                        scores(*following, s)
                    if s:
                        pe.wait_ge(*a_fo.at(r, "pt", 0))
                    for k in range(n + 1):
                        ins = nc.tensor.transpose(ps[2][:, k * P:(k + 1) * P], pr[s][:, k * P:(k + 1) * P], ident)
                    ins.then_inc(*p_fo.inc("t", s))
                for s in range(2):
                    pe.wait_ge(*a_fo.at(r, "pt", s))
                    for k in range(n + 1):
                        ins = mm(ps[3][:, s * HT:s * HT + P], pt[s][:, k, :], vb[:, k, bass.ds(p * P, P)],
                                 start=k == 0, stop=k == n)
                    ins.then_inc(*p_fo.inc("pv", s))
                pe.wait_ge(*d_fo.at(r, "y", 1))
                nc.tensor.transpose(ps[3][:, HT + P:HT + 2 * P], yf[:], ident).then_inc(*p_fy.inc("y"))

            for s in range(2):
                scores(0, 0, s)
            for n in range(QT):
                with pe.Fori(0, NH // 2 - 1) as p:
                    fox(n, p, (n, p + 1))
                fox(n, NH // 2 - 1, (n + 1, 0) if n < QT - 1 else None)

            def mix(i, first=False):
                for t in range(2):
                    m, n, s = 2 * i + t, U_MIX + 6 * i + 3 * t, (U_MIX + 3 * t) % 2
                    fresh = first and t == 0
                    if not fresh:
                        pe.wait_ge(*d_mx.at(m - 1, "ga"))
                    tile(n, s, ps[0], of(u3_hi), of(u3_lo))
                    if not fresh:
                        pe.wait_ge(*d_mx.at(m - 1, "gb"))
                    tile(n + 1, (s + 1) % 2, ps[1], of(u3_hi), of(u3_lo))
                    if not fresh:
                        pe.wait_ge(*d_mx.at(m - 1, "b"))
                    parts = [(ps[2 + k // 4], y_hi[:, k, :], y_lo[:, k, :], k % 4 == 0, k % 4 == 3, [d_y.at(k, "lo")])
                             for k in range(KT)]
                    for _, ins in unit(n + 2, s, parts):
                        pass
                    ins.then_inc(w_used, 1)

            pe.wait_ge(*a_fy.at(QT * NH // 2 - 1, "y"))
            mix(0, first=True)
            with pe.Fori(1, KT // 2) as i:
                mix(i)

            def out2(i, first=False):
                for s in range(2):
                    if not first:
                        pe.wait_ge(*d_h3.at(2 * i + s - 2, "res"))
                    tile(U_MIXOUT + 2 * i + s, (U_MIXOUT + s) % 2, ps[s], of(m2_hi), of(m2_lo), lambda k: d_m2.at(k, "lo"))

            out2(0, first=True)
            with pe.Fori(1, KT // 2) as i:
                out2(i)

            def up2(p, n, s, first=False):
                for j in range(2):
                    if first:
                        pe.wait_ge(*d_h3.at(KT - 2 + j, "res"))
                    else:
                        pe.wait_ge(*d_e.at(p - 1, f"ev{j}"))
                    tile(n + j, (s + j) % 2, ps[j], of(u4_hi), of(u4_lo), (lambda k: d_h3l.at(k, "lo")) if first else None)
                    if first and j == 0:
                        sum_squares(5)

            def down2(p, n, s, b, first=False):
                for j in range(2):
                    parts = []
                    for m in range(4 * j, 4 * j + 4):
                        for k in range(2):
                            waits = [d_e.at(p, "lo1")] * (m == 0 and k == 0)
                            if k == 0:
                                if m >= 2:
                                    waits += [(d_ea.sem, KT * p + m - 1)]
                                elif not first:
                                    waits += [(d_ea.sem, KT * p + m - 1)]
                            parts.append((ps[2 + m % 2], e_hi[b][:, k, :], e_lo[b][:, k, :], k == 0, k == 1, waits))
                    for q, ins in unit(n + j, (s + j) % 2, parts):
                        if q % 2 and q < KT - 1:
                            ins.then_inc(dn2, 1)
                    ins.then_inc(w_used, 1)

            R2 = NF2 // 2
            up2(0, U_FFN2, U_FFN2 % 2, first=True)
            n0 = U_FFN2 + 2
            pe.wait_ge(var_done, 6)
            up2(1, n0, n0 % 2)
            down2(0, n0 + 2, n0 % 2, 0, first=True)
            with pe.Fori(0, (R2 - 2) // 2) as i:
                for t in range(2):
                    p = 2 * i + t + 2
                    up2(p, n0 + 4 + 8 * i + 4 * t, n0 % 2)
                    down2(p - 1, n0 + 6 + 8 * i + 4 * t, n0 % 2, (t + 1) % 2)
            down2(R2 - 1, n0 + 4 * (R2 - 1), n0 % 2, 1)

            for j in range(2):
                parts = []
                for m in range(4 * j, 4 * j + 4):
                    for k in range(2):
                        waits = [d_p.at(1, "lo")] * (m == 0 and k == 0)
                        if k == 0:
                            waits += [(a_pj.sem, m - 1)] if m >= 2 else [d_ea.at(NF2 // 2 * KT - 2 + m, "add")]
                        parts.append((ps[2 + m % 2], pe_hi[:, k, :], pe_lo[:, k, :], k == 0, k == 1, waits))
                for q, ins in unit(U_PLE + j, (U_PLE + j) % 2, parts):
                    if q % 2 and q < KT - 1:
                        ins.then_inc(dn3, 1)
                ins.then_inc(w_used, 1)

            def gate(i, first=False):
                for s in range(2):
                    pe.wait_ge(*(d_e.at(R2 - 1, f"ev{s}") if first else d_g.at(2 * i + s - 2, "ev")))
                    tile(U_PLE + 2 + 2 * i + s, s, ps[s], of(u5_hi), of(u5_lo), lambda k: d_h4.at(k, "lo"))
                    if first and s == 0:
                        pe.wait_ge(*a_pj.at(KT - 1, "ev"))
                        sum_squares(6)

            gate(0, first=True)
            with pe.Fori(1, KT // 2) as i:
                gate(i)
            sum_squares(7)

        @block.vector
        def _(dve):
            V = nc.vector

            def add_square(q, m):
                dve.wait_ge(sq_done, KT * q + m + 1)
                if isinstance(m, int) and m == 0:
                    V.tensor_copy(sums[:], sq[:]).then_inc(sq_added, 1)
                else:
                    dve.wait_ge(sq_added, KT * q + m)
                    V.tensor_tensor(sums[:], sums[:], sq[:], ALU.add).then_inc(sq_added, 1)

            def factor(q):
                dve.wait_ge(rs_done, q + 1)

            def lo_of(dst, src, hi, gain=None):
                if gain is None:
                    return V.tensor_tensor(dst, src, hi.bitcast(F32), ALU.subtract)
                return V.scalar_tensor_tensor(out=dst, in0=src, scalar=gain, in1=hi.bitcast(F32), op0=ALU.mult, op1=ALU.subtract)

            dve.wait_ge(par_in, 16)
            V.memset(t1[:, 0:2], 0.0).then_inc(in1_freed, 1)
            for m in range(KT):
                add_square(0, m)
                dve.wait_ge(*a_x.at(m, "hi"))
                lo_of(u1_lo[:, m, :], x0[:, m, :], u1_hi[:, m, :], pcol("pre_mix_g", m)).then_inc(*d_x.inc("lo"))
            factor(0)

            dve.wait_ge(consts_in, 16)
            dve.wait_ge(tables_in, 16 * 4)
            V.memset(sums[:], 1.0).then_inc(*d_sh.begin())
            dve.wait_ge(d_sh.sem, 1)
            V.memset(sums[:].rearrange("p (c t) -> p c t", t=CH)[:, :, 0:1], 0.0).then_inc(*d_cv.begin())

            def shifted(t, src, mu, dst):
                dve.wait_ge(*d_sh.at(t - 1, "mix"))
                dve.wait_ge(w_used, t + 1)
                V.tensor_tensor(t1[:, 2:], src[:], rs[:], ALU.mult).then_inc(in1_freed, 1)
                dve.wait_ge(in1_freed, t + 2)
                V.tensor_tensor(t2[:], t1[:, 1:T + 1], t1[:, 2:], ALU.subtract).then_inc(*d_sh.inc("diff"))
                dve.wait_ge(*d_sh.at(t, "diff"))
                V.scalar_tensor_tensor(out=dst, in0=t2[:], scalar=mu, in1=t1[:, 2:], op0=ALU.mult, op1=ALU.add)\
                    .then_inc(*d_sh.inc("mix"))

            dve.wait_ge(in1_freed, 1)
            for t, dst in enumerate((ta[:], sg[:, 0, :], sg[:, 1, :])):
                shifted(t, ps[t % 2], pcol("mu", 12 + t), dst)
            with dve.Fori(0, 6) as i:
                for s in range(2):
                    t = 2 * i + s
                    shifted(t + 3, ps[(s + 1) % 2], pcol("mu", t), rkv[:, bass.ds(t, 1), :].rearrange("p a c -> p (a c)"))
            dve.wait_ge(*d_sh.at(14, "mix"))
            with dve.Fori(0, 2) as i:
                for jj in range(2):
                    c, t, par_ = 2 * i + jj, 6 * i + 3 * jj + 15, (15 + 3 * jj) % 2
                    dve.wait_ge(*d_cv.at(c - 1, "out"))
                    dve.wait_ge(w_used, t + 1)
                    V.tensor_tensor(t2[:], ps[par_][:], rs[:], ALU.mult).then_inc(in1_freed, 1)
                    dve.wait_ge(w_used, t + 2)
                    V.tensor_tensor(t3[:], ps[(par_ + 1) % 2][:], rs[:], ALU.mult).then_inc(in1_freed, 1)
                    dve.wait_ge(in1_freed, t + 3)
                    V.tensor_tensor(t1[:, 2:], t2[:], t3[:], ALU.mult).then_inc(*d_cv.inc("prod"))
                    dve.wait_ge(*d_cv.at(c, "prod"))
                    V.tensor_scalar(t2[:], t1[:, 2:], pcol("conv_a", 8 + c), None, ALU.mult).then_inc(*d_cv.inc("tap2"))
                    dve.wait_ge(*d_cv.at(c, "tap2"))
                    V.scalar_tensor_tensor(out=t2[:], in0=t1[:, 1:T + 1], scalar=pcol("conv_a", 4 + c), in1=t2[:],
                                           op0=ALU.mult, op1=ALU.add).then_inc(*d_cv.inc("tap1"))
                    dve.wait_ge(*d_cv.at(c, "tap1"))
                    V.scalar_tensor_tensor(out=t2[:], in0=t1[:, 0:T], scalar=pcol("conv_a", c), in1=t2[:],
                                           op0=ALU.mult, op1=ALU.add).then_inc(*d_cv.inc("tap0"))
                    dve.wait_ge(w_used, t + 3)
                    V.tensor_tensor(t3[:], ps[par_][:], rs[:], ALU.mult).then_inc(in1_freed, 1)
                    dve.wait_ge(in1_freed, t + 4)
                    dve.wait_ge(*d_cv.at(c, "tap0"))
                    V.tensor_tensor(ya[:, bass.ds(c, 1), :].rearrange("p a c -> p (a c)"), t3[:], t2[:], ALU.mult)\
                        .then_inc(*d_cv.inc("out"))

            dve.wait_ge(*d_cv.at(3, "out"))

            def key(i):
                V.tensor_scalar(t2[:], k_[:, i, :], pcol("k_k", i), None, ALU.mult).then_inc(*d_kk.inc("kkr"))

            key(0)
            for i in range(NP):
                def do(ins, name):
                    ins.then_inc(*d_pre.inc(name))
                    dve.wait_ge(*d_pre.at(i, name))

                ri_, ki, vi = r_[:, i, :], k_[:, i, :], v_[:, i, :]
                dve.wait_ge(*a_pre.at(i, "siga"))
                do(V.tensor_scalar(q2[:], q2[:], DECAY_SCALE, None, ALU.mult), "lw")
                do(V.tensor_tensor_scan(q3[:], sums[:], q2[:], 0.0, ALU.mult, ALU.add), "scan")
                do(V.tensor_tensor(q4[:], q3[:], q2[:], ALU.subtract), "cprev")
                dve.wait_ge(*p_ks.at(i, "done"))
                do(V.tensor_scalar(t3[:], ps[2][:], 1e-24, None, ALU.max), "clamp")
                dve.wait_ge(*a_pre.at(i, "kinv"))
                do(V.tensor_tensor(t2[:], t2[:], t3[:], ALU.mult), "kk")
                do(V.tensor_tensor(kap[:, i, :], t2[:], q4[:], ALU.mult), "kap")
                do(V.tensor_tensor(bet[:, i, :], t2[:], q1[:], ALU.mult), "bet")
                do(V.tensor_scalar(q1[:], q1[:], pcol("k_a", i), pcol("k_a", i), ALU.mult, ALU.subtract), "ika")
                do(V.scalar_tensor_tensor(out=ki, in0=q1[:], scalar=1.0, in1=ki, op0=ALU.add, op1=ALU.mult), "k4")
                do(V.scalar_tensor_tensor(out=q4[:], in0=ri_, scalar=pcol("r_k", i), in1=ki, op0=ALU.mult, op1=ALU.mult), "rk")
                if i + 1 < NP:
                    key(i + 1)
                dve.wait_ge(*a_pre.at(i, "eg"))
                do(V.tensor_tensor(ri_, ri_, q1[:], ALU.mult), "rho")
                do(V.tensor_copy(g_end[:, i, :], q1[:].rearrange("p (c t) -> p c t", t=CH)[:, :, CH - 1]), "gend")
                dve.wait_ge(*a_pre.at(i, "einv"))
                do(V.tensor_tensor(bet[:, i, :], bet[:, i, :], q2[:], ALU.mult), "betg")
                do(V.tensor_tensor(ki, ki, q2[:], ALU.mult), "eta")
                dve.wait_ge(*p_bn.at(i, "done"))
                do(V.tensor_tensor(bon[:, i, :], ps[3][:], vi, ALU.mult), "bon")
            for t in (kap_d, bet_d, eta_d, rho_d, v_d):
                ins = V.memset(t[:], 0.0)
            ins.then_inc(*d_r.begin())

            def bank(s, b, half=0):
                o = 512 * (b % 2) + 256 * half
                return ps[2 * s + b // 2][:, o:o + 256].rearrange("p (j c) -> p j c", j=2)

            def both(t):
                return t.unsqueeze(1).broadcast_to([P, 2, P])

            with dve.Fori(0, NCH) as c:
                dve.wait_ge(*d_r.at(c - 1, "s", 1))

                def pair(t, s):
                    return t[:, 2 * s:2 * s + 2, :]

                def masked(name, src_step, dst, b, half, mask):
                    for s in range(2):
                        dve.wait_ge(*p_r.at(c, src_step, s))
                        V.tensor_tensor(pair(dst, s), bank(s, b, half), both(ptile(mask)), ALU.mult).then_inc(*d_r.inc(name, s))

                masked("wd", "w", wd, 0, 0, "up16")
                masked("nd", "n", nd, 1, 0, "low16")
                masked("noff", "n", n_off, 1, 0, "low_off")
                masked("h", "h", h_t, 2, 0, "up")
                for s in range(2):
                    dve.wait_ge(*d_r.at(c, "wd", s))
                    V.tensor_tensor(pair(pa, s), both(ident), pair(wd, s), ALU.subtract).then_inc(*d_r.inc("p1", s))
                masked("p", "pq", p_t, 3, 0, "up_diag")
                masked("q", "pq", q_t, 3, 1, "up_diag")

                def refine(name, step, b, half):
                    for s in range(2):
                        dve.wait_ge(*p_r.at(c, step, s))
                        V.tensor_tensor(pair(pa, s), bank(s, b, half), pair(pa, s), ALU.add).then_inc(*d_r.inc(name, s))

                def copied(name, step, b, dst):
                    for s in range(2):
                        dve.wait_ge(*p_r.at(c, step, s))
                        V.tensor_copy(pair(dst, s), bank(s, b)).then_inc(*d_r.inc(name, s))

                refine("p2", "sq4", 3, 0)
                refine("p3", "sq8", 1, 1)
                copied("z0", "c1", 0, z0)
                refine("p4", "p4", 3, 1)
                copied("y", "c2", 1, y_m)
                for name, step, b, dst in (("z1", "c3", 2, z1), ("z2", "c4", 3, z2)):
                    for s in range(2):
                        dve.wait_ge(*p_r.at(c, step, s))
                        V.tensor_tensor(pair(dst, s), pair(y_m, s), bank(s, b), ALU.subtract).then_inc(*d_r.inc(name, s))
                for s in range(2):
                    dve.wait_ge(*p_r.at(c, "c5", s))
                    V.tensor_tensor(pair(u_m, s), bank(s, 0, 1), pair(y_m, s), ALU.subtract).then_inc(*d_r.inc("u", s))
                for s in range(2):
                    dve.wait_ge(*p_r.at(c, "y", s))
                    V.tensor_tensor(pair(s_m, s), bank(s, 1, 1), pair(s_m, s), ALU.add).then_inc(*d_r.inc("sadd", s))
                for s in range(2):
                    dve.wait_ge(*d_r.at(c, "sadd", s))
                    V.tensor_tensor(pair(s_m, s), pair(s_m, s),
                                    g_end[:, 2 * s:2 * s + 2, bass.ds(c, 1)].broadcast_to([P, 2, P]), ALU.mult)\
                        .then_inc(*d_r.inc("s", s))

            for k in range(NP):
                dve.wait_ge(*a_ya.at(k, "hi"))
                lo_of(m1_lo[k][:], ya[:, k, :], m1_hi[:, k, :]).then_inc(*d_ya.inc("lo"))

            def centre(i):
                dve.wait_ge(*p_gn.at(i, "mean"))
                V.tensor_tensor(gn_set[i % 2][0][:], kap[:, i, :], ps[0][:], ALU.subtract).then_inc(*d_gs.inc("cen"))

            centre(0)
            for i in range(NP):
                def do(ins, name):
                    ins.then_inc(*d_gn.inc(name))
                    dve.wait_ge(*d_gn.at(i, name))

                if i + 1 < NP:
                    centre(i + 1)
                y, _, factor_ = gn_set[i % 2]
                dve.wait_ge(*a_gs.at(i, "rstd"))
                do(V.tensor_tensor(y[:], y[:], factor_[:], ALU.mult), "nrm")
                do(V.tensor_scalar(y[:], y[:], pcol("lnx_w", i), pcol("lnx_b", i), ALU.mult, ALU.add), "aff")
                do(V.tensor_tensor(y[:], y[:], bon[:, i, :], ALU.add), "bon")
                dve.wait_ge(*p_gn.at(i, "gate"))
                do(V.tensor_tensor(y[:], y[:], ps[2][:], ALU.mult), "gate")
                dve.wait_ge(*a_gn.at(i, "hi"))
                do(lo_of(m1_lo[NP + i][:], y[:], m1_hi[:, NP + i, :]), "lo")

            for m in range(KT):
                add_square(1, m)
            factor(1)

            def residual(q, o, gain, gain_next, st, st_lo, a_st, hi, lo, before=None):
                for m in range(KT + 1):
                    if m < KT:
                        V.scalar_tensor_tensor(out=o[:, m, :], in0=o[:, m, :], scalar=pcol(gain, m), in1=rs[:],
                                               op0=ALU.mult, op1=ALU.mult).then_inc(*st.inc("scale"))
                        if before:
                            dve.wait_ge(*before(m))
                        dve.wait_ge(*st.at(m, "scale"))
                        V.tensor_tensor(h[:, m, :], h[:, m, :], o[:, m, :], ALU.add).then_inc(*st.inc("res"))
                    if m:
                        dve.wait_ge(*a_st.at(m - 1, "hi"))
                        lo_of(lo[:, m - 1, :], h[:, m - 1, :], hi[:, m - 1, :], pcol(gain_next, m - 1)).then_inc(*st_lo.inc("lo"))

            dve.wait_ge(w_used, U_FFN1)
            residual(2, o1, "post_mix_g", "pre_ffn_g", d_h1, d_h1l, a_h1, u2_hi, u2_lo, lambda m: (x_ld[m], 32))
            factor(2)

            for t in (fpg, fpu):
                ins = V.memset(t[:, 0:2], 0.0)
            ins.then_inc(setup_done, 1)
            dve.wait_ge(setup_done, 1)

            def round1(p, n, t, first=False):
                def conv(dst, src, j, names):
                    fc = PAR["ffn_conv_w"]
                    tile_ = p + NF1 * j
                    V.tensor_scalar(dst[:], src[:, 2:], par[:, bass.ds(tile_ + fc + 4 * NF1, 1)],
                                    par[:, bass.ds(tile_ + PAR["ffn_conv_b"], 1)], ALU.mult, ALU.add).then_inc(*d_f.inc(names[0]))
                    for q in (1, 0):
                        dve.wait_ge(*d_f.at(p, names[1 - q]))
                        V.scalar_tensor_tensor(out=dst[:], in0=src[:, q:T + q], scalar=par[:, bass.ds(tile_ + fc + 2 * NF1 * q, 1)],
                                               in1=dst[:], op0=ALU.mult, op1=ALU.add).then_inc(*d_f.inc(names[2 - q]))

                dve.wait_ge(w_used, n + 1)
                if not first:
                    dve.wait_ge(*d_f.at(p - 1, "lo"))
                V.tensor_tensor(fpg[:, 2:], ps[0][:], rs[:], ALU.mult).then_inc(*d_f.inc("evg"))
                dve.wait_ge(*d_f.at(p, "evg"))
                conv(cg, fpg, 0, ("cg1", "cg2", "cg3"))
                dve.wait_ge(w_used, n + 2)
                V.tensor_tensor(fpu[:, 2:], ps[1][:], rs[:], ALU.mult).then_inc(*d_f.inc("evu"))
                for m in range(KT):
                    if first:
                        V.memset(o1[:, m, :], 0.0).then_inc(*d_f.inc(f"add{m}"))
                        continue
                    if m < KT - 1:
                        dve.wait_ge(dn1, 7 * (p - 1) + m + 1)
                    else:
                        dve.wait_ge(w_used, n + 3)
                    V.tensor_tensor(o1[:, m, :], o1[:, m, :], ps[2 + m % 2][:], ALU.add).then_inc(*d_f.inc(f"add{m}"))
                dve.wait_ge(*d_f.at(p, "evu"))
                conv(cu, fpu, 1, ("cu1", "cu2", "cu3"))
                dve.wait_ge(*d_f.at(p, "cu3"))
                dve.wait_ge(*a_f.at(p, "gelu"))
                V.tensor_tensor(cu[:], cu[:], cg[:], ALU.mult).then_inc(*d_f.inc("prod"))
                dve.wait_ge(*a_f.at(p, "hi"))
                lo_of(f_lo[:, t, :], cu[:], f_hi[:, t, :]).then_inc(*d_f.inc("lo"))

            round1(0, U_FFN1, 0, first=True)
            with dve.Fori(0, (NF1 - 2) // 2) as i:
                for t in range(2):
                    round1(2 * i + t + 1, U_FFN1 + 2 + 6 * i + 3 * t, (t + 1) % 2)
            round1(NF1 - 1, U_FFN1 + 2 + 3 * (NF1 - 2), 1)
            dve.wait_ge(*d_f.at(NF1 - 1, "lo"))
            for m in range(KT):
                dve.wait_ge(*((dn1, 7 * (NF1 - 1) + m + 1) if m < KT - 1 else (w_used, U_IN2)))
                V.tensor_tensor(o1[:, m, :], o1[:, m, :], ps[2 + m % 2][:], ALU.add).then_inc(*d_f_last.inc("add"))
                if m:
                    add_square(3, m - 1)
            add_square(3, KT - 1)
            factor(3)
            residual(4, o1, "post_ffn_g", "g_mix", d_h2, d_h2l, a_h2, u3_hi, u3_lo)
            factor(4)

            def ev2(j, dst, part=slice(0, P), src=None):
                dve.wait_ge(w_used, U_IN2 + j + 1)
                return V.tensor_tensor(dst, ps[j % 2][part, :], rs[part, :], ALU.mult)

            ev2(0, fr[0][:], slice(0, 8)).then_inc(in2_freed, 1)
            for vt in range(5):
                ev2(1 + vt, v_cm[:, vt, :]).then_inc(in2_freed, 1)
            def do(ins, name):
                ins.then_inc(*d_fg.inc(name))
                dve.wait_ge(*d_fg.at(0, name))

            dve.wait_ge(in2_freed, 1)
            do(V.tensor_scalar(fr[0][:], fr[0][:], par[0:8, PAR["b_forget"]:PAR["b_forget"] + 1], None, ALU.add), "bias")
            do(V.scalar_tensor_tensor(out=fr[1][:], in0=fr[0][:], scalar=-1.0, in1=fr[0][:], op0=ALU.mult, op1=ALU.max), "abs")
            do(V.tensor_scalar(fr[0][:], fr[0][:], 0.0, None, ALU.min), "min")
            dve.wait_ge(*a_fg.at(0, "ln"))
            do(V.tensor_tensor(fr[0][:], fr[0][:], fr[1][:], ALU.subtract), "log")
            dve.wait_ge(spilled, 16 * KT)
            do(V.tensor_tensor_scan(negc[:], ptile("ones")[0:8, 0:1].broadcast_to([8, T]), fr[0][:], 0.0, ALU.mult, ALU.add),
               "scan")
            do(V.tensor_scalar(negc[:], negc[:], -1.0, None, ALU.mult), "neg")
            ev2(6, ka[:, P:]).then_inc(in2_freed, 1)
            for j in range(4):
                ev2(7 + j, k65[0:64, 2 * j, :], slice(0, 64))
                ev2(7 + j, k65[0:64, 2 * j + 1, :], slice(64, 128)).then_inc(in2_freed, 1)
            dve.wait_ge(*a_v.at(4, "t"))
            for j in range(4):
                ev2(11 + j, qa[:, j, :]).then_inc(in2_freed, 1)
            for j in range(4):
                ev2(15 + j, qb[:, j, :]).then_inc(in2_freed, 1)

            dve.wait_ge(negc_in, 16)
            V.memset(ka[:, 0:P], 0.0)
            V.tensor_scalar(nsink[:], par[:, PAR["sinks"]:PAR["sinks"] + 8], -1.0, None, ALU.mult)
            V.memset(va[:, 0, :], 0.0).then_inc(*d_so.begin())
            for g in range(2):
                ins = V.memset(qs[g][64 * (1 - g):64 * (1 - g) + 64, :, :], 0.0)
            ins.then_inc(*d_si.inc("z"))
            dve.wait_ge(*d_si.at(0, "z"))
            dve.wait_ge(in2_freed, UNITS_IN2)

            def swa_queries(n):
                for half, name in ((0, "qe"), (1, "qo")):
                    for g in range(SW):
                        V.tensor_scalar(qs[g][64 * g:64 * g + 64, half::2, :],
                                        qa[64 * half:64 * half + 64, 2 * g:2 * g + 2, bass.ds(n * P, P)],
                                        HD ** -0.5, None, ALU.mult).then_inc(*d_ss.inc(name, g))

            def swa_biased(n, variant, before=None):
                for j in range(4):
                    for g in range(SW):
                        if j == 0:
                            dve.wait_ge(*p_ss.at(n, "s", g))
                            if before is not None:
                                dve.wait_ge(*p_so.at(before, "t", g))
                        V.scalar_tensor_tensor(out=sc[g][:, j, :], in0=dist[:, variant, :], scalar=-(2.0 ** -(4 * g + j + 1)),
                                               in1=ps[g][:, j * 256:(j + 1) * 256], op0=ALU.mult, op1=ALU.add)\
                            .then_inc(*d_ss.inc(f"b{j}", g))
                for g in range(SW):
                    dve.wait_ge(*d_ss.at(n, "b3", g))
                    V.tensor_reduce(mx[:, 4 * g:4 * g + 4], sc[g][:], AX.X, ALU.max).then_inc(*d_ss.inc("max", g))
                for g in range(SW):
                    c = slice(4 * g, 4 * g + 4)
                    dve.wait_ge(*d_ss.at(n, "max", g))
                    V.scalar_tensor_tensor(out=nm[:, c], in0=mx[:, c], scalar=-1.0, in1=nsink[:, c], op0=ALU.mult, op1=ALU.min)\
                        .then_inc(*d_ss.inc("neg", g))
                for g in range(SW):
                    c = slice(4 * g, 4 * g + 4)
                    dve.wait_ge(*d_ss.at(n, "neg", g))
                    V.tensor_tensor(es[:, c], nm[:, c], nsink[:, c], ALU.subtract).then_inc(*d_ss.inc("sd", g))

            def swa(n, following):
                dve.wait_ge(*d_so.at(n - 1, "y", 1))
                if following is not None:
                    swa_queries(following)
                for g in range(SW):
                    c = slice(4 * g, 4 * g + 4)
                    dve.wait_ge(*a_ss.at(n, "e3", g))
                    V.tensor_tensor(ls[:, c], ls[:, c], es[:, c], ALU.add).then_inc(*d_so.inc("sum", g))
                for g in range(SW):
                    c = slice(4 * g, 4 * g + 4)
                    dve.wait_ge(*d_so.at(n, "sum", g))
                    V.reciprocal(ri[:, c], ls[:, c]).then_inc(*d_so.inc("inv", g))
                if following is not None:
                    swa_biased(following, 0, n)
                for g in range(SW):
                    dve.wait_ge(*p_so.at(n, "pv", g))
                    dve.wait_ge(*d_so.at(n, "inv", g))
                    V.tensor_tensor(ysw[g][:], ps[3][:, g * HT:(g + 1) * HT].rearrange("p (j c) -> p j c", j=4)[:, :, 64 * g:64 * g + 64],
                                    ri[:, 4 * g:4 * g + 4].unsqueeze(2).broadcast_to([P, 4, HD]), ALU.mult)\
                        .then_inc(*d_so.inc("y", g))

            swa_queries(0)
            swa_biased(0, 1)
            with dve.Fori(0, QT - 1) as n:
                swa(n, n + 1)
            swa(QT - 1, None)

            dve.wait_ge(*p_so.at(QT - 1, "yt", 1))
            V.memset(qf[0][64:65, :], 1.0).then_inc(*d_fo.begin())
            V.memset(qf[1][64:65, :], 1.0).then_inc(*d_si.inc("z"))
            dve.wait_ge(*d_si.at(1, "z"))

            def queries(n, p):
                for s in range(2):
                    V.tensor_scalar(qf[s][0:64, :], qb[64 * s:64 * s + 64, bass.ds(p, 1), n * P:(n + 1) * P].rearrange("p a c -> p (a c)"),
                                    HD ** -0.5, None, ALU.mult).then_inc(*d_fs.inc("q", s))

            def maxima(n, p):
                r, cols = p + n * (NH // 2), (n + 1) * P
                for s in range(2):
                    dve.wait_ge(*p_fs.at(r, "s", s))
                    V.tensor_tensor(ps[s][:, n * P:cols], ps[s][:, n * P:cols], ptile("causal"), ALU.add).then_inc(*d_fs.inc("mask", s))
                for s in range(2):
                    dve.wait_ge(*d_fs.at(r, "mask", s))
                    V.tensor_reduce(mx[:, s:s + 1], ps[s][:, 0:cols], AX.X, ALU.max).then_inc(*d_fs.inc("max", s))
                for s in range(2):
                    dve.wait_ge(*d_fs.at(r, "max", s))
                    V.tensor_scalar(nm[:, s:s + 1], mx[:, s:s + 1], -1.0, None, ALU.mult).then_inc(*d_fs.inc("neg", s))

            def fox(n, p, following):
                r = p + n * (NH // 2)
                dve.wait_ge(*d_fo.at(r - 1, "y", 1))
                if following:
                    queries(*following)
                for s in range(2):
                    dve.wait_ge(*a_fs.at(r, "exp", s))
                    V.reciprocal(ri[:, s:s + 1], ls[:, s:s + 1]).then_inc(*d_fo.inc("inv", s))
                if following:
                    maxima(*following)
                for s in range(2):
                    dve.wait_ge(*p_fo.at(r, "pv", s))
                    dve.wait_ge(*d_fo.at(r, "inv", s))
                    V.tensor_scalar(yf[:, 64 * s:64 * s + 64], ps[3][:, s * (HT + 64):s * (HT + 64) + 64], ri[:, s:s + 1],
                                    None, ALU.mult).then_inc(*d_fo.inc("y", s))

            queries(0, 0)
            maxima(0, 0)
            for n in range(QT):
                with dve.Fori(0, NH // 2 - 1) as p:
                    fox(n, p, (n, p + 1))
                fox(n, NH // 2 - 1, (n + 1, 0) if n < QT - 1 else None)

            for k in range(KT):
                dve.wait_ge(*a_y.at(k, "hi"))
                src = qa[:, k, :] if k < 4 else qb[:, k - 4, :]
                lo_of(y_lo[:, k, :], src, y_hi[:, k, :]).then_inc(*d_y.inc("lo"))
            dve.wait_ge(*a_y.at(KT - 1, "hi"))

            def mix(m, first=False):
                n = 3 * m + U_MIX
                if not first:
                    dve.wait_ge(*d_mx.at(m - 1, "mix"))
                dve.wait_ge(w_used, n + 1)
                V.tensor_tensor(ga[:], ps[0][:], rs[:], ALU.mult).then_inc(*d_mx.inc("ga"))
                dve.wait_ge(w_used, n + 2)
                V.tensor_tensor(gb[:], ps[1][:], rs[:], ALU.mult).then_inc(*d_mx.inc("gb"))
                dve.wait_ge(w_used, n + 3)
                dve.wait_ge(*a_mx.at(m, "siga"))
                V.tensor_tensor(ga[:], ga[:], ps[2][:], ALU.mult).then_inc(*d_mx.inc("a"))
                dve.wait_ge(*a_mx.at(m, "sigb"))
                V.tensor_tensor(gb[:], gb[:], ps[3][:], ALU.mult).then_inc(*d_mx.inc("b"))
                dve.wait_ge(*d_mx.at(m, "b"))
                V.tensor_tensor(mixed[:, bass.ds(m, 1), :].rearrange("p a c -> p (a c)"), ga[:], gb[:], ALU.add)\
                    .then_inc(*d_mx.inc("mix"))

            mix(0, first=True)
            with dve.Fori(1, KT) as m:
                mix(m)
            dve.wait_ge(w_used, U_MIXOUT)
            for k in range(KT):
                dve.wait_ge(*a_m2.at(k, "hi"))
                lo_of(m2_lo[:, k, :], mixed[:, k, :], m2_hi[:, k, :]).then_inc(*d_m2.inc("lo"))

            for m in range(KT + 1):
                if m < KT:
                    dve.wait_ge(w_used, U_MIXOUT + m + 1)
                    dve.wait_ge(x_ld[m], 48)
                    V.tensor_tensor(h[:, m, :], ps[m % 2][:], h[:, m, :], ALU.add).then_inc(*d_h3.inc("res"))
                if m:
                    add_square(5, m - 1)
                    dve.wait_ge(*a_h3.at(m - 1, "hi"))
                    lo_of(u4_lo[:, m - 1, :], h[:, m - 1, :], u4_hi[:, m - 1, :], pcol("g_mlp", m - 1)).then_inc(*d_h3l.inc("lo"))
            factor(5)

            def hidden(p, n, t):
                for j in range(2):
                    dve.wait_ge(w_used, n + j + 1)
                    V.scalar_tensor_tensor(out=fa[j][:], in0=ps[j][:], scalar=0.0, in1=rs[:], op0=ALU.max, op1=ALU.mult)\
                        .then_inc(*d_e.inc(f"ev{j}"))
                    dve.wait_ge(*a_e.at(p, f"hi{j}"))
                    lo_of(e_lo[t][:, j, :], fs[j][:], e_hi[t][:, j, :]).then_inc(*d_e.inc(f"lo{j}"))

            def adds(p, n, tail=None):
                for m in range(KT):
                    dve.wait_ge(*((w_used, n + m // 4 + 1) if m % 4 == 3 else (dn2, 6 * p + 3 * (m // 4) + m % 4 + 1)))
                    V.tensor_tensor(h[:, m, :], h[:, m, :], ps[2 + m % 2][:], ALU.add).then_inc(*d_ea.inc("add"))
                    if tail:
                        tail(m)

            n0 = U_FFN2 + 2
            hidden(0, U_FFN2, 0)
            hidden(1, n0, 1)
            adds(0, n0 + 2)
            with dve.Fori(0, (NF2 // 2 - 2) // 2) as i:
                for t in range(2):
                    p = 2 * i + t + 2
                    hidden(p, n0 + 4 + 8 * i + 4 * t, t)
                    adds(p - 1, n0 + 6 + 8 * i + 4 * t)
            R2 = NF2 // 2

            def split4(m):
                add_square(6, m)
                dve.wait_ge(*a_h4.at(m, "hi"))
                lo_of(u5_lo[:, m, :], h[:, m, :], u5_hi[:, m, :], pcol("g_ple", m)).then_inc(*d_h4.inc("lo"))

            for k in range(2):
                dve.wait_ge(*a_p.at(k, "hi"))
                lo_of(pe_lo[:, k, :], pe_raw[:, k, :], pe_hi[:, k, :]).then_inc(*d_p.inc("lo"))
            adds(R2 - 1, n0 + 4 * (R2 - 1), tail=lambda m: split4(m - 1) if m else None)
            split4(KT - 1)
            factor(6)

            def embed(i, first=False):
                for s in range(2):
                    m = 2 * i + s
                    hm = h[:, bass.ds(m, 1), :].rearrange("p a c -> p (a c)")
                    dve.wait_ge(w_used, U_PLE + 3 + m)
                    if not first:
                        dve.wait_ge(*d_g.at(m - 2, "res"))
                    V.tensor_tensor(gt[s][:], ps[s][:], rs[:], ALU.mult).then_inc(*d_g.inc("ev"))
                    dve.wait_ge(*a_g.at(m, "sig"))
                    dve.wait_ge(*a_pj.at(KT - 1, "ev"))
                    V.tensor_tensor(gt[s][:], gt[s][:], proj[:, bass.ds(m, 1), :].rearrange("p a c -> p (a c)"), ALU.mult)\
                        .then_inc(*d_g.inc("prod"))
                    dve.wait_ge(*d_g.at(m, "prod"))
                    V.tensor_tensor(hm, hm, gt[s][:], ALU.add).then_inc(*d_g.inc("res"))
                    if not (first and s == 0):
                        add_square(7, m - 1)

            embed(0, first=True)
            with dve.Fori(1, KT // 2) as i:
                embed(i)
            add_square(7, KT - 1)
            factor(7)
            for m in range(KT):
                V.scalar_tensor_tensor(out=h[:, m, :], in0=h[:, m, :], scalar=pcol("g_final", m), in1=rs[:],
                                       op0=ALU.mult, op1=ALU.mult).then_inc(*d_o.inc("out"))

        @block.scalar
        def _(act):
            A = nc.scalar.activation

            def square(q, m, src):
                if q in DIRECT:
                    act.wait_ge(sq_added, KT * q + max(m - 1, 0))
                elif q or m:
                    act.wait_ge(sq_added, KT * q + m)
                dst = sums if q in DIRECT and m % 2 else sq
                A(dst[:], src, ACT.Square).then_inc(sq_done, 1)

            def root(q):
                if q in DIRECT:
                    act.wait_ge(sq_added, KT * (q + 1))
                else:
                    act.wait_ge(ss_done, sum(j not in DIRECT for j in range(q + 1)))
                A(rs[:], ps[3][:], ACT.Ln, bias=pcol("rms_eps"), scale=1.0 / D).then_inc(var_done, 1)
                act.wait_ge(var_done, q + 1)
                A(rs[:], rs[:], ACT.Exp, scale=-0.5).then_inc(rs_done, 1)

            act.wait_ge(par_in, 16)
            for m in range(KT):
                act.wait_ge(x_ld[m], 16)
                square(0, m, x0[:, m, :])
                A(u1_hi[:, m, :], x0[:, m, :], ACT.Copy, scale=pcol("pre_mix_g", m)).then_inc(*a_x.inc("hi"))
            root(0)
            act.wait_ge(*d_sh.at(0, "mix"))
            A(ta[0:64, :], ta[0:64, :], ACT.Tanh).then_inc(*a_mis.inc("tanh"))
            for j in range(2):
                act.wait_ge(*d_sh.at(1 + j, "mix"))
                A(sg[:, j, :], sg[:, j, :], ACT.Sigmoid).then_inc(*a_mis.inc(f"sig{j}"))

            act.wait_ge(consts_in, 16)

            def key_squares(i):
                act.wait_ge(*d_kk.at(i, "kkr"))
                A(t3[:], t2[:], ACT.Square).then_inc(*a_kk.inc("ksq"))

            key_squares(0)
            for i in range(NP):
                if i:
                    act.wait_ge(*d_pre.at(i - 1, "eta"))
                act.wait_ge(*p_za.at(i, "done"))
                A(q2[:], ps[0][:], ACT.Sigmoid, bias=pcol("w0", i)).then_inc(*a_pre.inc("sigz"))
                A(q1[:], ps[1][:], ACT.Sigmoid, bias=pcol("a0", i)).then_inc(*a_pre.inc("siga"))
                act.wait_ge(*d_pre.at(i, "cprev"))
                A(q4[:], q4[:], ACT.Exp).then_inc(*a_pre.inc("eprev"))
                act.wait_ge(*d_pre.at(i, "clamp"))
                A(t3[:], t3[:], ACT.Ln).then_inc(*a_pre.inc("kln"))
                act.wait_ge(*a_pre.at(i, "kln"))
                A(t3[:], t3[:], ACT.Exp, scale=-0.5).then_inc(*a_pre.inc("kinv"))
                act.wait_ge(*d_pre.at(i, "k4"))
                A(q1[:], q3[:], ACT.Exp).then_inc(*a_pre.inc("eg"))
                A(q2[:], q3[:], ACT.Exp, scale=-1.0).then_inc(*a_pre.inc("einv"))
                if i + 1 < NP:
                    key_squares(i + 1)

            def bank(s, b, half=0):
                o = 512 * (b % 2) + 256 * half
                return ps[2 * s + b // 2][:, o:o + 256].rearrange("p (j c) -> p j c", j=2)

            act.wait_ge(*d_pre.at(NP - 1, "bon"))
            A(s_m[:], ident.unsqueeze(1).broadcast_to([P, NP, P]), ACT.Copy, scale=0.0).then_inc(*a_r.begin())
            with act.Fori(0, NCH) as c:
                for name, step, b, half, dst in (("bt", "tr", 0, 0, bet_t), ("et", "tr", 0, 1, eta_t), ("w2", "sq2", 2, 0, w2m),
                                                 ("n2", "sq2", 2, 1, n2m), ("vt", "tr", 1, 0, v_t), ("w4", "sq4", 0, 0, w4m),
                                                 ("n4", "sq4", 0, 1, n4m), ("n8", "sq8", 2, 0, n8m), ("g", "g", 2, 1, g_m)):
                    for s in range(2):
                        act.wait_ge(*p_r.at(c, step, s))
                        A(dst[:, 2 * s:2 * s + 2, :], bank(s, b, half), ACT.Copy).then_inc(*a_r.inc(name, s))
                for hh in range(2):
                    rows = slice(64 * hh, 64 * hh + 64)
                    for s in range(2):
                        act.wait_ge(*p_r.at(c, "y", s))
                        A(kap[rows, 2 * s:2 * s + 2, bass.ds(c * CH, CH)], bank(s, 2, 1)[rows, :, 64 * hh:64 * hh + 64], ACT.Copy)\
                            .then_inc(*a_r.inc(f"y{hh}", s))

            for k in range(NP):
                A(m1_hi[:, k, :], ya[:, k, :], ACT.Copy).then_inc(*a_ya.inc("hi"))

            def stats(i):
                y, y2, factor = gn_set[i % 2]
                act.wait_ge(*d_gs.at(i, "cen"))
                A(y2[:], y[:], ACT.Square).then_inc(*a_gs.inc("sq"))
                act.wait_ge(*p_gn.at(i, "var"))
                A(factor[:], ps[1][:], ACT.Ln, bias=pcol("gn_eps")).then_inc(*a_gs.inc("ln"))
                act.wait_ge(*a_gs.at(i, "ln"))
                A(factor[:], factor[:], ACT.Exp, scale=-0.5).then_inc(*a_gs.inc("rstd"))

            stats(0)
            for i in range(NP):
                if i + 1 < NP:
                    stats(i + 1)
                act.wait_ge(*d_gn.at(i, "gate"))
                A(m1_hi[:, NP + i, :], gn_set[i % 2][0][:], ACT.Copy).then_inc(*a_gn.inc("hi"))
            act.wait_ge(*d_gn.at(NP - 1, "lo"))
            for m in range(KT):
                act.dma_start(h[:, m, :], x_in[m]).then_inc(x_ld[m], 16)
            for m in range(KT):
                act.wait_ge(w_used, U_OUT1 + m + 1)
                square(1, m, ps[m % 2][:])
                A(o1[:, m, :], ps[m % 2][:], ACT.Copy).then_inc(*a_o1.inc("ev"))
            root(1)
            for m in range(KT):
                act.wait_ge(*d_h1.at(m, "res"))
                square(2, m, h[:, m, :])
                A(u2_hi[:, m, :], h[:, m, :], ACT.Copy, scale=pcol("pre_ffn_g", m)).then_inc(*a_h1.inc("hi"))
            root(2)

            def round1(p, t):
                act.wait_ge(*d_f.at(p, "cg3"))
                A(cg[:], cg[:], ACT.Gelu_apprx_tanh).then_inc(*a_f.inc("gelu"))
                act.wait_ge(*d_f.at(p, "prod"))
                A(f_hi[:, t, :], cu[:], ACT.Copy).then_inc(*a_f.inc("hi"))

            with act.Fori(0, NF1 // 2) as i:
                for t in range(2):
                    round1(2 * i + t, t)
            for m in range(KT):
                act.wait_ge(*d_f_last.at(m, "add"))
                square(3, m, o1[:, m, :])
            root(3)
            for m in range(KT):
                act.wait_ge(*d_h2.at(m, "res"))
                square(4, m, h[:, m, :])
                A(u3_hi[:, m, :], h[:, m, :], ACT.Copy, scale=pcol("g_mix", m)).then_inc(*a_h2.inc("hi"))
                act.dma_start(h_spill[m], h[:, m, :]).then_inc(spilled, 16)
            root(4)

            act.wait_ge(*d_fg.at(0, "abs"))
            A(fr[1][:], fr[1][:], ACT.Exp, scale=-1.0).then_inc(*a_fg.inc("exp"))
            act.wait_ge(*a_fg.at(0, "exp"))
            A(fr[1][:], fr[1][:], ACT.Ln, bias=1.0).then_inc(*a_fg.inc("ln"))
            act.wait_ge(spilled, 16 * KT)
            for vt in range(5):
                act.wait_ge(*p_v.at(vt, "t"))
                src = ps[2 + vt % 2][:].rearrange("p (k c) -> p k c", c=P)
                dst = va[:, 1:, :] if vt == 0 else vb[:, :, (vt - 1) * P:vt * P]
                A(dst, src, ACT.Copy).then_inc(*a_v.inc("t"))
            act.wait_ge(*d_fg.at(0, "neg"))
            act.dma_start(k65[64:65, :, :], negc[:]).then_inc(negc_in, 16)

            def swa_exponentials(n):
                for g in range(SW):
                    act.wait_ge(*d_ss.at(n, "sd", g))
                    A(es[:, 4 * g:4 * g + 4], es[:, 4 * g:4 * g + 4], ACT.Exp).then_inc(*a_ss.inc("es", g))
                for j in range(4):
                    for g in range(SW):
                        c = slice(4 * g + j, 4 * g + j + 1)
                        A(sc[g][:, j, :], sc[g][:, j, :], ACT.Exp, bias=nm[:, c], accum_out=ls[:, c]).then_inc(*a_ss.inc(f"e{j}", g))

            def swa(n, following):
                for g in range(SW):
                    act.wait_ge(*p_so.at(n, "t", g))
                    if g:
                        act.wait_ge(*p_so.at(n, "pv", 0))
                    A(pt_a[:].rearrange("p k c -> p (k c)"), ps[2][:], ACT.Copy).then_inc(*a_so.inc("pt", g))
                if following is not None:
                    swa_exponentials(following)
                for g in range(SW):
                    act.wait_ge(*p_so.at(n, "yt", g))
                    A(qa[:, 2 * g:2 * g + 2, bass.ds(n * P, P)], ps[3][:, g * HT:g * HT + 2 * P].rearrange("p (j c) -> p j c", j=2),
                      ACT.Copy).then_inc(*a_so.inc("yt", g))

            swa_exponentials(0)
            with act.Fori(0, QT - 1) as n:
                swa(n, n + 1)
            swa(QT - 1, None)

            def exponentials(n, p):
                r, cols = p + n * (NH // 2), (n + 1) * P
                for s in range(2):
                    act.wait_ge(*d_fs.at(r, "neg", s))
                    A(pr[s][:, 0:cols], ps[s][:, 0:cols], ACT.Exp, bias=nm[:, s:s + 1], accum_out=ls[:, s:s + 1])\
                        .then_inc(*a_fs.inc("exp", s))

            def fox(n, p, following):
                r, cols = p + n * (NH // 2), (n + 1) * P
                for s in range(2):
                    act.wait_ge(*p_fo.at(r, "t", s))
                    A(pt[s][:, 0:n + 1, :].rearrange("p k c -> p (k c)"), ps[2][:, 0:cols], ACT.Copy).then_inc(*a_fo.inc("pt", s))
                if following:
                    exponentials(*following)
                act.wait_ge(*p_fy.at(r, "y"))
                A(qb[:, bass.ds(p, 1), n * P:cols].rearrange("p a c -> p (a c)"), ps[3][:, HT + P:HT + 2 * P], ACT.Copy)\
                    .then_inc(*a_fy.inc("y"))

            exponentials(0, 0)
            for n in range(QT):
                with act.Fori(0, NH // 2 - 1) as p:
                    fox(n, p, (n, p + 1))
                fox(n, NH // 2 - 1, (n + 1, 0) if n < QT - 1 else None)

            act.wait_ge(*a_fy.at(QT * NH // 2 - 1, "y"))
            for k in range(KT):
                src = qa[:, k, :] if k < 4 else qb[:, k - 4, :]
                A(y_hi[:, k, :], src, ACT.Copy).then_inc(*a_y.inc("hi"))
            with act.Fori(0, KT) as m:
                act.wait_ge(*d_mx.at(m, "ga"))
                A(ga[:], ga[:], ACT.Sigmoid).then_inc(*a_mx.inc("siga"))
                act.wait_ge(*d_mx.at(m, "gb"))
                A(gb[:], gb[:], ACT.Sigmoid).then_inc(*a_mx.inc("sigb"))
            act.wait_ge(w_used, U_MIXOUT)
            for m in range(KT):
                act.dma_start(h[:, m, :], h_spill[m]).then_inc(x_ld[m], 16)
            for k in range(KT):
                act.wait_ge(*d_mx.at(k, "mix"))
                A(m2_hi[:, k, :], mixed[:, k, :], ACT.Copy).then_inc(*a_m2.inc("hi"))
            for m in range(KT):
                act.wait_ge(*d_h3.at(m, "res"))
                square(5, m, h[:, m, :])
                A(u4_hi[:, m, :], h[:, m, :], ACT.Copy, scale=pcol("g_mlp", m)).then_inc(*a_h3.inc("hi"))
            root(5)

            act.wait_ge(w_used, U_FFN2)
            for k in range(2):
                act.dma_start(pe_raw[:, k, :], p_in[k]).then_inc(p_ld, 16)
            act.wait_ge(p_ld, 32)
            for k in range(2):
                A(pe_hi[:, k, :], pe_raw[:, k, :], ACT.Copy).then_inc(*a_p.inc("hi"))
            with act.Fori(0, NF2 // 4) as i:
                for t in range(2):
                    p = 2 * i + t
                    for j in range(2):
                        act.wait_ge(*d_e.at(p, f"ev{j}"))
                        A(fs[j][:], fa[j][:], ACT.Square).then_inc(*a_e.inc(f"sq{j}"))
                        act.wait_ge(*a_e.at(p, f"sq{j}"))
                        A(e_hi[t][:, j, :], fs[j][:], ACT.Copy).then_inc(*a_e.inc(f"hi{j}"))
            for m in range(KT):
                act.wait_ge(*d_ea.at((NF2 // 2 - 1) * KT + m, "add"))
                square(6, m, h[:, m, :])
                A(u5_hi[:, m, :], h[:, m, :], ACT.Copy, scale=pcol("g_ple", m)).then_inc(*a_h4.inc("hi"))
            for m in range(KT):
                act.wait_ge(*((w_used, U_PLE + m // 4 + 1) if m % 4 == 3 else (dn3, 3 * (m // 4) + m % 4 + 1)))
                A(proj[:, m, :], ps[2 + m % 2][:], ACT.Copy).then_inc(*a_pj.inc("ev"))
            root(6)
            def embed(i, first=False):
                for s in range(2):
                    m = 2 * i + s
                    act.wait_ge(*d_g.at(m, "ev"))
                    A(gt[s][:], gt[s][:], ACT.Sigmoid).then_inc(*a_g.inc("sig"))
                    if not (first and s == 0):
                        act.wait_ge(*d_g.at(m - 1, "res"))
                        square(7, m - 1, h[:, bass.ds(m - 1, 1), :].rearrange("p a c -> p (a c)"))

            embed(0, first=True)
            with act.Fori(1, KT // 2) as i:
                embed(i)
            act.wait_ge(*d_g.at(KT - 1, "res"))
            square(7, KT - 1, h[:, KT - 1, :])
            root(7)
            for m in range(KT):
                act.wait_ge(*d_o.at(m, "out"))
                act.dma_start(out[m], h[:, m, :]).then_inc(stored, 16)
            act.wait_ge(stored, 16 * KT)


def pack_columns(w, cols):
    k = w.shape[0] // P
    out = np.zeros((P, k, P), np.float32)
    out[:, :, :len(cols)] = w[:, cols].reshape(k, P, len(cols)).transpose(1, 0, 2)
    return out


def weight_units(a):
    units = []

    def tile(w, start, n=P):
        units.append(pack_columns(w, np.arange(start, start + n)))

    w_in, w_out, w_up, w_down = a["w_in"][0], a["w_out"][0], a["w_up"][0], a["w_down"][0]
    q0 = 3 * CONV
    low = q0 + 3 * RWKV
    tile(w_in, low)
    tile(w_in, low + P)
    tile(w_in, low + 2 * P, GATE_R - P)
    for j in range(3 * RWKV // P):
        tile(w_in, q0 + j * P)
    for j in range(CONV // P):
        for part in (0, 2, 1):
            tile(w_in, part * CONV + j * P)
    for m in range(KT):
        tile(w_out, m * P)

    def rows(blocks):
        units.append(np.stack(blocks, 1))

    def block(w, k, m):
        return w[k * P:(k + 1) * P, m * P:(m + 1) * P]

    for p in range(NF1):
        tile(w_up, p * P)
        tile(w_up, FF1 + p * P)
        if p:
            rows([block(w_down, p - 1, m) for m in range(KT)])
    rows([block(w_down, NF1 - 1, m) for m in range(KT)])
    w2 = a["w_in_2"][0]
    off = dict(qa=0, ka=512, va=640, qb=768, kb=1280, vb=1792, f=2304, g=2312)
    tile(w2, off["f"], NH)
    tile(w2, off["va"])
    for j in range(4):
        tile(w2, off["vb"] + j * P)
    tile(w2, off["ka"])
    for name in ("kb", "qa", "qb"):
        for j in range(4):
            tile(w2, off[name] + j * P)
    for m in range(KT):
        tile(w2, off["g"] + m * P)
        tile(w2, off["g"] + D + m * P)
        rows([block(a["w_br_swa_2"][0], k, m) for k in range(4)] + [block(a["w_br_fox_2"][0], k, m) for k in range(4)])
    for m in range(KT):
        tile(a["w_mix_out_2"][0], m * P)
    ff1, ff2 = a["w_ff1_2"][0], a["w_ff2_2"][0]

    def down(p):
        for j in range(2):
            rows([block(ff2, 2 * p + k, m) for m in range(4 * j, 4 * j + 4) for k in range(2)])

    for p in range(NF2 // 2):
        tile(ff1, 2 * p * P)
        tile(ff1, (2 * p + 1) * P)
        if p:
            down(p - 1)
    down(NF2 // 2 - 1)
    for j in range(2):
        rows([block(a["w_ple_proj_2"][0], k, m) for m in range(4 * j, 4 * j + 4) for k in range(2)])
    for m in range(KT):
        tile(a["w_ple_gate_2"][0], m * P)
    assert len(units) == UNITS
    return np.ascontiguousarray(np.stack(units).reshape(UNITS, P, KT * P))


def parameters(a):
    par = np.zeros((P, N_PAR), np.float32)

    def put(name, v):
        n = -(-v.size // P)
        flat = np.zeros(n * P, np.float32)
        flat[:v.size] = v.reshape(-1)
        par[:, PAR[name]:PAR[name] + n] = flat.reshape(n, P).T

    for name in ("pre_mix_g", "w0", "a0", "k_k", "k_a", "r_k", "lnx_w", "lnx_b", "post_mix_g", "pre_ffn_g", "post_ffn_g",
                 "ffn_conv_b"):
        put(name, a[name][0])
    for name in ("g_mix", "g_mlp", "g_ple"):
        put(name, a[name + "_2"][0])
    put("g_final", a["g_final_2"])
    put("mu", a["shift_mu"][0])
    put("conv_a", a["conv_a_w"][0])
    put("ffn_conv_w", a["ffn_conv_w"][0])
    par[:NH, PAR["b_forget"]] = a["b_forget_2"][0]
    par[:, PAR["rms_eps"]] = RMS_EPS
    par[:, PAR["gn_eps"]] = GN_EPS
    par[:, PAR["sinks"]:PAR["sinks"] + NH] = a["swa_sinks_2"][0][None, :]
    return par


def constant_tables():
    i = np.arange(P)
    row, col = i[:, None], i[None, :]
    head, blk = row // CH == col // CH, row // 16 == col // 16
    m = {
        "ident": row == col,
        "ones": row >= 0 * col,
        "head_sum": head,
        "head_mean": head / HD,
        "up16": (row < col) & blk,
        "low16": (row > col) & blk,
        "low_off": (row > col) & head & ~blk,
        "up": (row < col) & head,
        "up_diag": (row <= col) & head,
        "causal": np.where(col <= row, 0.0, NEG),
    }
    consts = np.concatenate([np.broadcast_to(m[n], (P, P)).astype(np.float32) for n in CONSTS], 1)
    qi, si = row + P, np.arange(2 * P)[None, :]
    chunks = qi // CH - si // CH
    ok = (chunks >= 0) & (chunks <= 2)
    d = np.abs(qi - si).astype(np.float32)
    dists = np.stack([np.where(ok, d, -NEG), np.where(ok & (si >= P), d, -NEG)], 1).astype(np.float32)
    return np.ascontiguousarray(consts), np.ascontiguousarray(dists)


def kernel(**inputs):
    import concourse.bacc as _bacc
    from concourse import mybir as _mybir
    from concourse.bass_utils import run_bass_kernel_spmd as _run

    a = {k: np.asarray(v) for k, v in inputs.items()}
    consts, dists = constant_tables()
    w2 = np.zeros((P, RWKV), np.float32)
    w2[:DECAY_R] = a["w2"][0]
    a2 = np.zeros((P, RWKV), np.float32)
    a2[DECAY_R:] = a["a2"][0]
    g2 = np.zeros((P, 2, RWKV), np.float32)
    g2[:, 0] = a["g2"][0][:P]
    g2[:GATE_R - P, 1] = a["g2"][0][P:]
    arrays = {
        "xT": np.ascontiguousarray(a["x"][0].T).reshape(KT, P, T),
        "pT": np.ascontiguousarray(a["p_2"][0, 0].T).reshape(2, P, T),
        "weights": weight_units(a),
        "params": parameters(a),
        "consts": consts,
        "dists": dists,
        "w2p": w2,
        "a2p": a2,
        "g2p": g2,
    }
    nc = _bacc.Bacc("TRN2", target_bir_lowering=False, num_devices=1)
    args = [nc.dram_tensor(n, v.shape, _mybir.dt.float32, kind="ExternalInput").ap() for n, v in arrays.items()]
    out = nc.dram_tensor("outT", (KT, P, T), _mybir.dt.float32, kind="ExternalOutput").ap()
    build_program(nc, *args, out)
    r = _run(nc, [arrays], core_ids=[0])
    y = np.asarray(r.results[0]["outT"]).reshape(D, T)
    return np.ascontiguousarray(y.T)[None]
```
